# Optimizing a Trainium2 kernel written in Bass

```python
import math
import jax, jax.numpy as jnp
from jax import lax
import numpy as np

D_MODEL = 1024
BATCH = 1
SEQ = 256
DEPTH = 2

MIX_WIDTH = D_MODEL
M_HEADS = 4
M_HEAD_DIM = (MIX_WIDTH // 2) // M_HEADS
M_WIDTH = M_HEADS * M_HEAD_DIM
A_HEADS = 8
A_HEAD_DIM = (MIX_WIDTH - M_WIDTH) // A_HEADS
A_WIDTH = A_HEADS * A_HEAD_DIM
D_FF = 4 * D_MODEL
CONV_WIDTH = 5
M_CHUNK = 64
DILATED_PATTERNS = ((128, 1), (512, 4), (2048, 16))
BAND_BLOCK = 64
ROPE_THETA = 10000.0
NORM_EPS = 1e-6
NEG_INF = -1e30
IN_SPLITS = (M_WIDTH, M_WIDTH, M_WIDTH, M_WIDTH, 2 * M_HEADS, 2 * M_HEADS, A_WIDTH, A_WIDTH, A_WIDTH)
IN_WIDTH = 4 * M_WIDTH + 4 * M_HEADS + 3 * A_WIDTH


def rms_norm(x, g):
    xf = x.astype(jnp.float32)
    y = xf * lax.rsqrt(jnp.mean(xf * xf, axis=-1, keepdims=True) + NORM_EPS)
    return (y * g.astype(jnp.float32)).astype(x.dtype)

def rope(t):
    S, D = t.shape[1], t.shape[-1]
    half = D // 2
    inv_freq = ROPE_THETA ** (-jnp.arange(half, dtype=jnp.float32) / half)
    ang = jnp.arange(S, dtype=jnp.float32)[:, None] * inv_freq[None, :]
    cos = jnp.cos(ang)[None, :, None, :]
    sin = jnp.sin(ang)[None, :, None, :]
    tf = t.astype(jnp.float32)
    t1, t2 = tf[..., :half], tf[..., half:]
    return jnp.concatenate([t1 * cos - t2 * sin, t1 * sin + t2 * cos], axis=-1)

def centred_depthwise_conv(x, w):
    K, C = w.shape
    return lax.conv_general_dilated(
        x, w[:, None, :], window_strides=(1,), padding=[(K // 2, K // 2)],
        dimension_numbers=("NWC", "WIO", "NWC"), feature_group_count=C)

def mlstm_chunkwise(q, k, v, li, lf):
    B, H, S, D = q.shape
    L = M_CHUNK
    NC = S // L
    q = q.reshape(B, H, NC, L, D)
    k = k.reshape(B, H, NC, L, D)
    v = v.reshape(B, H, NC, L, D)
    li = li.reshape(B, H, NC, L)
    lf = lf.reshape(B, H, NC, L)
    b = jnp.cumsum(lf, axis=-1)
    b_last = b[..., -1]
    g = b_last[..., None] - b + li
    g_max = jnp.max(g, axis=-1)

    def step(carry, inp):
        C, n, m = carry
        k_c, v_c, g_c, gmax_c, bl_c = inp
        m_new = jnp.maximum(bl_c + m, gmax_c)
        decay = jnp.exp(bl_c + m - m_new)
        w = jnp.exp(g_c - m_new[..., None])
        C_new = decay[..., None, None] * C + jnp.einsum("bhs,bhsk,bhsv->bhkv", w, k_c, v_c)
        n_new = decay[..., None] * n + jnp.einsum("bhs,bhsk->bhk", w, k_c)
        return (C_new, n_new, m_new), (C, n, m)

    init = (jnp.zeros((B, H, D, D), jnp.float32), jnp.zeros((B, H, D), jnp.float32),
            jnp.full((B, H), NEG_INF, jnp.float32))
    xs = (jnp.moveaxis(k, 2, 0), jnp.moveaxis(v, 2, 0), jnp.moveaxis(g, 2, 0),
          jnp.moveaxis(g_max, 2, 0), jnp.moveaxis(b_last, 2, 0))
    _, (C_prev, n_prev, m_prev) = lax.scan(step, init, xs)
    C_prev = jnp.moveaxis(C_prev, 0, 2)
    n_prev = jnp.moveaxis(n_prev, 0, 2)
    m_prev = jnp.moveaxis(m_prev, 0, 2)

    a = b + m_prev[..., None]
    lower = jnp.tril(jnp.ones((L, L), dtype=bool))
    dmat = jnp.where(lower, b[..., :, None] - b[..., None, :] + li[..., None, :], NEG_INF)
    m_t = jnp.maximum(a, jnp.max(dmat, axis=-1))
    s = jnp.einsum("bhnqd,bhnkd->bhnqk", q, k) * jnp.exp(dmat - m_t[..., None])
    inter = jnp.exp(a - m_t)
    num = (jnp.einsum("bhnqk,bhnkd->bhnqd", s, v)
           + inter[..., None] * jnp.einsum("bhnqk,bhnkv->bhnqv", q, C_prev))
    den = jnp.sum(s, axis=-1) + inter * jnp.einsum("bhnqk,bhnk->bhnq", q, n_prev)
    h = num / jnp.maximum(jnp.abs(den), jnp.exp(-m_t))[..., None]
    return h.reshape(B, H, S, D)

def strided_band_attention(q, k, v, dilation, half):
    B, H, S, D = q.shape
    L = S // dilation
    qb_len = math.gcd(L, BAND_BLOCK)
    nb = L // qb_len
    span = qb_len + 2 * half

    def to_strided(t):
        return t.reshape(B, H, L, dilation, D).transpose(0, 1, 3, 2, 4)

    qs = to_strided(q).reshape(B, H, dilation, nb, qb_len, D)
    pad = ((0, 0), (0, 0), (0, 0), (half, half), (0, 0))
    kp = jnp.pad(to_strided(k), pad)
    vp = jnp.pad(to_strided(v), pad)
    idx = (jnp.arange(nb) * qb_len)[:, None] + jnp.arange(span)[None, :]
    kb = kp[:, :, :, idx, :]
    vb = vp[:, :, :, idx, :]
    qpos = (jnp.arange(nb) * qb_len)[:, None, None] + jnp.arange(qb_len)[None, :, None]
    kpos = idx[:, None, :] - half
    valid = (jnp.abs(kpos - qpos) <= half) & (kpos >= 0) & (kpos < L)
    s = jnp.einsum("bhrnqd,bhrnkd->bhrnqk", qs, kb) * (1.0 / math.sqrt(D))
    s = jnp.where(valid, s, NEG_INF)
    m = jnp.max(s, axis=-1)
    p = jnp.exp(s - m[..., None])
    l = jnp.sum(p, axis=-1)
    o = jnp.einsum("bhrnqk,bhrnkd->bhrnqd", p, vb) / l[..., None]

    def from_strided(t):
        tail = t.shape[5:]
        t = jnp.moveaxis(t.reshape((B, H, dilation, L) + tail), 2, 3)
        return t.reshape((B, H, S) + tail)

    return from_strided(o), from_strided(m), from_strided(l)

def dilated_attention(q, k, v):
    outs = [strided_band_attention(q, k, v, d, w // (2 * d)) for (w, d) in DILATED_PATTERNS]
    m_all = jnp.max(jnp.stack([m for (_, m, _) in outs]), axis=0)
    weights = [l * jnp.exp(m - m_all) for (_, m, l) in outs]
    num = sum(w[..., None] * o for w, (o, _, _) in zip(weights, outs))
    return num / sum(weights)[..., None]

def hybrid_layer(x, norm1_g, w_in, conv_w, gate_i_b, gate_f_b, head_norm_g, w_out,
                 norm2_g, w_up, w_down):
    B, S, _ = x.shape
    h = rms_norm(x, norm1_g)
    proj = h @ w_in
    mq, mk, mv, mo, mi, mf, aq, ak, av = jnp.split(
        proj, list(np.cumsum(IN_SPLITS)[:-1]), axis=-1)

    qk = jax.nn.silu(centred_depthwise_conv(jnp.concatenate([mq, mk], axis=-1), conv_w))
    mq, mk = qk[..., :M_WIDTH], qk[..., M_WIDTH:]

    def m_heads(t):
        return t.reshape(B, S, M_HEADS, M_HEAD_DIM).transpose(0, 2, 1, 3).astype(jnp.float32)

    q_m = m_heads(mq)
    k_m = m_heads(mk) * (1.0 / math.sqrt(M_HEAD_DIM))
    v_m = m_heads(mv)
    gi = (mi + gate_i_b).astype(jnp.float32).reshape(B, S, 2, M_HEADS).transpose(2, 0, 3, 1)
    gf = jax.nn.log_sigmoid((mf + gate_f_b).astype(jnp.float32)).reshape(
        B, S, 2, M_HEADS).transpose(2, 0, 3, 1)
    h_fwd = mlstm_chunkwise(q_m, k_m, v_m, gi[0], gf[0])
    flip = lambda t: jnp.flip(t, axis=2)
    h_bwd = flip(mlstm_chunkwise(flip(q_m), flip(k_m), flip(v_m), flip(gi[1]), flip(gf[1])))
    hm = h_fwd + h_bwd
    hm = hm * lax.rsqrt(jnp.mean(hm * hm, axis=-1, keepdims=True) + NORM_EPS)
    hm = hm.transpose(0, 2, 1, 3).reshape(B, S, M_WIDTH) * head_norm_g.astype(jnp.float32)
    y_m = (hm * jax.nn.sigmoid(mo.astype(jnp.float32))).astype(x.dtype)

    def a_heads(t, rotate):
        t = t.reshape(B, S, A_HEADS, A_HEAD_DIM)
        t = rope(t) if rotate else t.astype(jnp.float32)
        return t.transpose(0, 2, 1, 3)

    o_a = dilated_attention(a_heads(aq, True), a_heads(ak, True), a_heads(av, False))
    y_a = o_a.transpose(0, 2, 1, 3).reshape(B, S, A_WIDTH).astype(x.dtype)

    x = x + jnp.concatenate([y_m, y_a], axis=-1) @ w_out

    u = jax.nn.relu(rms_norm(x, norm2_g) @ w_up)
    return x + (u * u) @ w_down

def first_inputs(seed: int = 0) -> dict:
    key = jax.random.key(seed)
    ks = jax.random.split(key, 13)
    f32 = jnp.float32
    nrm = lambda k, shape: jax.random.normal(k, shape, f32)
    x = nrm(ks[0], (BATCH, SEQ, D_MODEL))
    norm1_g = 1.0 + 0.02 * nrm(ks[1], (DEPTH, D_MODEL))
    w_in = nrm(ks[2], (DEPTH, D_MODEL, IN_WIDTH)) * D_MODEL ** -0.5
    conv_w = nrm(ks[3], (DEPTH, CONV_WIDTH, 2 * M_WIDTH)) * CONV_WIDTH ** -0.5
    gate_i_b = 0.1 * nrm(ks[4], (DEPTH, 2 * M_HEADS))
    gate_f_b = (jnp.tile(jnp.linspace(3.0, 6.0, M_HEADS, dtype=f32), 2)[None, :]
                + 0.1 * nrm(ks[5], (DEPTH, 2 * M_HEADS)))
    head_norm_g = 1.0 + 0.02 * nrm(ks[6], (DEPTH, M_WIDTH))
    w_out = nrm(ks[7], (DEPTH, MIX_WIDTH, D_MODEL)) * MIX_WIDTH ** -0.5
    norm2_g = 1.0 + 0.02 * nrm(ks[8], (DEPTH, D_MODEL))
    w_up = nrm(ks[9], (DEPTH, D_MODEL, D_FF)) * D_MODEL ** -0.5
    w_down = nrm(ks[10], (DEPTH, D_FF, D_MODEL)) * D_FF ** -0.5
    final_g = 1.0 + 0.02 * nrm(ks[11], (D_MODEL,))
    return {"x": x, "norm1_g": norm1_g, "w_in": w_in, "conv_w": conv_w,
            "gate_i_b": gate_i_b, "gate_f_b": gate_f_b, "head_norm_g": head_norm_g,
            "w_out": w_out, "norm2_g": norm2_g, "w_up": w_up, "w_down": w_down,
            "final_g": final_g}

def first_block(x, norm1_g, w_in, conv_w, gate_i_b, gate_f_b, head_norm_g, w_out,
              norm2_g, w_up, w_down, final_g):
    for layer in range(DEPTH):
        x = hybrid_layer(x, norm1_g[layer], w_in[layer], conv_w[layer], gate_i_b[layer],
                         gate_f_b[layer], head_norm_g[layer], w_out[layer], norm2_g[layer],
                         w_up[layer], w_down[layer])
    return rms_norm(x, final_g)


N_MIXERS = 2
POOL_WINDOWS = (2, 4, 8, 16)
POOL_GROUPS = len(POOL_WINDOWS)
POOL_GROUP_DIM = D_MODEL // POOL_GROUPS
N_HEADS = 16
N_KV_GROUPS = 4
HEADS_PER_GROUP = N_HEADS // N_KV_GROUPS
HEAD_DIM = D_MODEL // N_HEADS
Q_DIM = N_HEADS * HEAD_DIM
KV_DIM = N_KV_GROUPS * HEAD_DIM
N_BRANCHES = 3
IN_PROJ_DIM = Q_DIM + 2 * N_BRANCHES * KV_DIM + N_BRANCHES * N_HEADS
CMP_STRIDE = 16
CMP_BLOCK = 2 * CMP_STRIDE
CMP_HIDDEN = 2 * HEAD_DIM
SEL_BLOCK = 64
SEL_TOP_N = 16
WINDOW = 512
Q_BLOCK = 64
FORCE_BONUS = 1.0e3
NEG_INF_2 = -1.0e30
ATTN_SCALE = HEAD_DIM ** -0.5
D_FF_2 = 2816
N_EXPERTS = 8
TOP_K = 2
D_FF_EXPERT = 3584
LN_EPS = 1e-5
ALPHA = (2 * DEPTH) ** 0.25
BETA = (8 * DEPTH) ** -0.25


def layer_norm(x, g, b):
    xf = x.astype(jnp.float32)
    mu = jnp.mean(xf, axis=-1, keepdims=True)
    var = jnp.mean(jnp.square(xf - mu), axis=-1, keepdims=True)
    return ((xf - mu) * lax.rsqrt(var + LN_EPS) * g.astype(jnp.float32) + b.astype(jnp.float32)).astype(x.dtype)

def rope_2(x, pos):
    half = x.shape[-1] // 2
    freqs = jnp.power(ROPE_THETA, -jnp.arange(half, dtype=jnp.float32) / half)
    ang = pos.astype(jnp.float32)[:, None] * freqs[None, :]
    cos = jnp.cos(ang)[None, :, None, :]
    sin = jnp.sin(ang)[None, :, None, :]
    xf = x.astype(jnp.float32)
    x1, x2 = xf[..., :half], xf[..., half:]
    return jnp.concatenate([x1 * cos - x2 * sin, x1 * sin + x2 * cos], axis=-1).astype(x.dtype)

def pool_mixer(x, w_grp, scale):
    B, S, _ = x.shape
    xg = x.reshape(B, S, POOL_GROUPS, POOL_GROUP_DIM)
    c = jnp.concatenate([jnp.zeros((B, 1, POOL_GROUPS, POOL_GROUP_DIM), jnp.float32),
                         jnp.cumsum(xg.astype(jnp.float32), axis=1)], axis=1)
    t1 = jnp.arange(1, S + 1)
    pooled = []
    for gi, w in enumerate(POOL_WINDOWS):
        cg = c[:, :, gi]
        lo = cg[:, jnp.maximum(t1 - w, 0)]
        cnt = jnp.minimum(t1, w).astype(jnp.float32)
        pooled.append((cg[:, 1:] - lo) / cnt[None, :, None])
    pooled = jnp.stack(pooled, axis=2).astype(x.dtype)
    y = jnp.einsum('bsgc,gcd->bsgd', pooled - xg, w_grp).reshape(B, S, D_MODEL)
    return y * scale

def compress(k, pe, w1, w2):
    B, S, G, D = k.shape
    ch = k.reshape(B, S // CMP_STRIDE, CMP_STRIDE, G, D)
    blk = jnp.concatenate([ch[:, :-1], ch[:, 1:]], axis=2)
    blk = blk + pe[None, None, :, None, :]
    nc = blk.shape[1]
    blk = blk.transpose(0, 1, 3, 2, 4).reshape(B, nc, G, CMP_BLOCK * D)
    return jax.nn.silu(blk @ w1) @ w2

def nsa_mixer(x, w_in, pe_k, w1_k, w2_k, pe_v, w1_v, w2_v, w_out):
    B, S, _ = x.shape
    G, HG, D = N_KV_GROUPS, HEADS_PER_GROUP, HEAD_DIM
    proj = x @ w_in
    splits = [Q_DIM + i * KV_DIM for i in range(2 * N_BRANCHES + 1)]
    q, kc_raw, vc_raw, ks, vs, kw, vw, g_logits = jnp.split(proj, splits, axis=-1)
    pos = jnp.arange(S)
    q = rope_2(q.reshape(B, S, N_HEADS, D), pos)
    q = q.reshape(B, S, G, HG, D).transpose(0, 2, 3, 1, 4)
    kv = lambda a: a.reshape(B, S, G, D)
    ks = rope_2(kv(ks), pos)
    kw = rope_2(kv(kw), pos)
    vs, vw = kv(vs), kv(vw)
    kc = compress(kv(kc_raw), pe_k, w1_k, w2_k)
    vc = compress(kv(vc_raw), pe_v, w1_v, w2_v)
    nc = kc.shape[1]
    cend = CMP_STRIDE * jnp.arange(nc) + CMP_BLOCK - 1
    kc = rope_2(kc, cend)
    gates = jax.nn.sigmoid(g_logits.astype(jnp.float32)).astype(x.dtype).reshape(B, S, N_HEADS, N_BRANCHES)

    nsel = S // SEL_BLOCK
    n_top = min(SEL_TOP_N, nsel)
    ks_blk = ks.reshape(B, nsel, SEL_BLOCK, G, D).transpose(0, 3, 1, 2, 4)
    vs_blk = vs.reshape(B, nsel, SEL_BLOCK, G, D).transpose(0, 3, 1, 2, 4)
    kw_pad = jnp.pad(kw, ((0, 0), (WINDOW, 0), (0, 0), (0, 0)))
    vw_pad = jnp.pad(vw, ((0, 0), (WINDOW, 0), (0, 0), (0, 0)))
    cstart = CMP_STRIDE * jnp.arange(nc)
    sstart = SEL_BLOCK * jnp.arange(nsel)
    overlap = ((cstart[:, None] <= sstart[None, :] + SEL_BLOCK - 1) &
               (cstart[:, None] + CMP_BLOCK - 1 >= sstart[None, :])).astype(jnp.float32)
    bi = jnp.arange(B)[:, None, None, None]
    gi = jnp.arange(G)[None, :, None, None]
    jsel = jnp.arange(nsel)

    def query_block(i):
        t0 = i * Q_BLOCK
        t = t0 + jnp.arange(Q_BLOCK)
        qb = lax.dynamic_slice_in_dim(q, t0, Q_BLOCK, axis=3)
        sc = jnp.einsum('bghtd,bngd->bghtn', qb, kc).astype(jnp.float32) * ATTN_SCALE
        cvalid = cend[None, :] <= t[:, None]
        pc = jax.nn.softmax(jnp.where(cvalid, sc, NEG_INF_2), axis=-1)
        pc = pc * jnp.any(cvalid, axis=-1).astype(jnp.float32)[:, None]
        o_c = jnp.einsum('bghtn,bngd->btghd', pc.astype(vc.dtype), vc)
        imp = jnp.einsum('bghtn,nj->bgtj', pc, overlap)
        blk_t = t // SEL_BLOCK
        bvalid = jsel[None, :] <= blk_t[:, None]
        forced = (jsel[None, :] == 0) | (jsel[None, :] == blk_t[:, None]) | (jsel[None, :] == blk_t[:, None] - 1)
        score = jnp.where(bvalid, imp + FORCE_BONUS * forced.astype(jnp.float32), -1.0)
        _, idx = lax.top_k(score, n_top)
        sel_valid = idx <= blk_t[None, None, :, None]
        kg = ks_blk[bi, gi, idx]
        vg = vs_blk[bi, gi, idx]
        ss = jnp.einsum('bghtd,bgtnld->bghtnl', qb, kg).astype(jnp.float32) * ATTN_SCALE
        kpos = idx[..., None] * SEL_BLOCK + jnp.arange(SEL_BLOCK)
        ms = (kpos <= t[None, None, :, None, None]) & sel_valid[..., None]
        ss = jnp.where(ms[:, :, None], ss, NEG_INF_2)
        ps = jax.nn.softmax(ss.reshape(ss.shape[:4] + (n_top * SEL_BLOCK,)), axis=-1).reshape(ss.shape)
        o_s = jnp.einsum('bghtnl,bgtnld->btghd', ps.astype(vg.dtype), vg)
        kwb = lax.dynamic_slice_in_dim(kw_pad, t0, Q_BLOCK + WINDOW, axis=1)
        vwb = lax.dynamic_slice_in_dim(vw_pad, t0, Q_BLOCK + WINDOW, axis=1)
        kpos_w = t0 - WINDOW + jnp.arange(Q_BLOCK + WINDOW)
        mw = (kpos_w[None, :] <= t[:, None]) & (kpos_w[None, :] > t[:, None] - WINDOW) & (kpos_w[None, :] >= 0)
        sw = jnp.einsum('bghtd,bkgd->bghtk', qb, kwb).astype(jnp.float32) * ATTN_SCALE
        pw = jax.nn.softmax(jnp.where(mw, sw, NEG_INF_2), axis=-1)
        o_w = jnp.einsum('bghtk,bkgd->btghd', pw.astype(vwb.dtype), vwb)
        gb = lax.dynamic_slice_in_dim(gates, t0, Q_BLOCK, axis=1).reshape(B, Q_BLOCK, G, HG, N_BRANCHES)
        return gb[..., 0:1] * o_c + gb[..., 1:2] * o_s + gb[..., 2:3] * o_w

    out = lax.map(query_block, jnp.arange(S // Q_BLOCK))
    out = out.transpose(1, 0, 2, 3, 4, 5).reshape(B, S, Q_DIM)
    return out @ w_out

def swiglu(x, w_gu, w_down):
    g, u = jnp.split(x @ w_gu, 2, axis=-1)
    return (jax.nn.silu(g) * u) @ w_down

def moe_ffn(x, router, w_gu, w_down):
    B, S, D = x.shape
    xt = x.reshape(B * S, D)
    logits = (xt @ router).astype(jnp.float32)
    top_v, top_i = lax.top_k(logits, TOP_K)
    w = jax.nn.softmax(top_v, axis=-1)
    combine = jnp.einsum('tk,tke->te', w, jax.nn.one_hot(top_i, N_EXPERTS, dtype=jnp.float32)).astype(x.dtype)
    y = jnp.zeros_like(xt)
    for e in range(N_EXPERTS):
        y = y + combine[:, e:e + 1] * swiglu(xt, w_gu[e], w_down[e])
    return y.reshape(B, S, D)

def second_inputs(seed: int = 0) -> dict:
    key = jax.random.key(seed)
    keys = iter(jax.random.split(key, 32))
    nrm = lambda shape, s: jax.random.normal(next(keys), shape, jnp.float32) * s
    na = (DEPTH + 1) // 2
    nb = DEPTH // 2
    return {
        "x": nrm((BATCH, SEQ, D_MODEL), 1.0),
        "ln_g": 1.0 + nrm((DEPTH, 2, D_MODEL), 0.05),
        "ln_b": nrm((DEPTH, 2, D_MODEL), 0.02),
        "pool_w": nrm((na, POOL_GROUPS, POOL_GROUP_DIM, POOL_GROUP_DIM), BETA * POOL_GROUP_DIM ** -0.5),
        "pool_scale": 1.0 + nrm((na, D_MODEL), 0.1),
        "nsa_w_in": nrm((nb, D_MODEL, IN_PROJ_DIM), D_MODEL ** -0.5),
        "nsa_pe_k": nrm((nb, CMP_BLOCK, HEAD_DIM), 0.1),
        "nsa_w1_k": nrm((nb, CMP_BLOCK * HEAD_DIM, CMP_HIDDEN), (CMP_BLOCK * HEAD_DIM) ** -0.5),
        "nsa_w2_k": nrm((nb, CMP_HIDDEN, HEAD_DIM), CMP_HIDDEN ** -0.5),
        "nsa_pe_v": nrm((nb, CMP_BLOCK, HEAD_DIM), 0.1),
        "nsa_w1_v": nrm((nb, CMP_BLOCK * HEAD_DIM, CMP_HIDDEN), (CMP_BLOCK * HEAD_DIM) ** -0.5),
        "nsa_w2_v": nrm((nb, CMP_HIDDEN, HEAD_DIM), CMP_HIDDEN ** -0.5),
        "nsa_w_out": nrm((nb, Q_DIM, D_MODEL), BETA * Q_DIM ** -0.5),
        "ffn_w_gu": nrm((na, D_MODEL, 2 * D_FF_2), D_MODEL ** -0.5),
        "ffn_w_down": nrm((na, D_FF_2, D_MODEL), BETA * D_FF_2 ** -0.5),
        "moe_router": nrm((nb, D_MODEL, N_EXPERTS), D_MODEL ** -0.5),
        "moe_w_gu": nrm((nb, N_EXPERTS, D_MODEL, 2 * D_FF_EXPERT), D_MODEL ** -0.5),
        "moe_w_down": nrm((nb, N_EXPERTS, D_FF_EXPERT, D_MODEL), BETA * D_FF_EXPERT ** -0.5),
    }

def second_block(x, ln_g, ln_b, pool_w, pool_scale, nsa_w_in, nsa_pe_k, nsa_w1_k, nsa_w2_k,
              nsa_pe_v, nsa_w1_v, nsa_w2_v, nsa_w_out, ffn_w_gu, ffn_w_down,
              moe_router, moe_w_gu, moe_w_down):
    for i in range(DEPTH):
        j = i // N_MIXERS
        if i % N_MIXERS == 0:
            h = pool_mixer(x, pool_w[j], pool_scale[j])
        else:
            h = nsa_mixer(x, nsa_w_in[j], nsa_pe_k[j], nsa_w1_k[j], nsa_w2_k[j],
                          nsa_pe_v[j], nsa_w1_v[j], nsa_w2_v[j], nsa_w_out[j])
        x = layer_norm(ALPHA * x + h, ln_g[i, 0], ln_b[i, 0])
        if i % 2 == 0:
            f = swiglu(x, ffn_w_gu[j], ffn_w_down[j])
        else:
            f = moe_ffn(x, moe_router[j], moe_w_gu[j], moe_w_down[j])
        x = layer_norm(ALPHA * x + f, ln_g[i, 1], ln_b[i, 1])
    return x


def setup_inputs(seed=0):
    out = dict(first_inputs(seed))
    for name, value in second_inputs(seed + 1).items():
        if name != "x":
            out[name + "_2"] = value
    return out


def reference(
    x, norm1_g, w_in, conv_w, gate_i_b, gate_f_b, head_norm_g, w_out, norm2_g, w_up, w_down,
    final_g, ln_g_2, ln_b_2, pool_w_2, pool_scale_2, nsa_w_in_2, nsa_pe_k_2, nsa_w1_k_2,
    nsa_w2_k_2, nsa_pe_v_2, nsa_w1_v_2, nsa_w2_v_2, nsa_w_out_2, ffn_w_gu_2, ffn_w_down_2,
    moe_router_2, moe_w_gu_2, moe_w_down_2,
):
    x = first_block(
        x, norm1_g, w_in, conv_w, gate_i_b, gate_f_b, head_norm_g, w_out, norm2_g, w_up, w_down,
        final_g,
    )
    return second_block(
        x, ln_g_2, ln_b_2, pool_w_2, pool_scale_2, nsa_w_in_2, nsa_pe_k_2, nsa_w1_k_2,
        nsa_w2_k_2, nsa_pe_v_2, nsa_w1_v_2, nsa_w2_v_2, nsa_w_out_2, ffn_w_gu_2, ffn_w_down_2,
        moe_router_2, moe_w_gu_2, moe_w_down_2,
    )


_drawn_inputs = setup_inputs


def setup_inputs(seed=0):
    import zlib

    import numpy as np

    out = dict(_drawn_inputs(seed))
    spreads = {}
    factors = {'gate_i_b': 8.0,
     'head_norm_g': 3.848,
     'nsa_pe_k_2': 8.0,
     'nsa_w1_k_2': 3.085,
     'nsa_w2_k_2': 3.171,
     'nsa_pe_v_2': 3.909}
    for name, (base, spread) in spreads.items():
        noise = np.random.default_rng([zlib.crc32(name.encode()), seed]).standard_normal(out[name].shape)
        drawn = base * np.exp(spread * noise) if base else spread * noise
        out[name] = __import__('jax').numpy.asarray(drawn.astype(out[name].dtype))
    for name, factor in factors.items():
        out[name] = (out[name] * factor).astype(out[name].dtype)
    return out
```

```python
import math
from contextlib import ExitStack

import numpy as np
import concourse.bass as bass
from concourse import mybir

F32 = mybir.dt.float32
I32 = mybir.dt.int32
ALU = mybir.AluOpType
ACT = mybir.ActivationFunctionType
AX = mybir.AxisListType

P = 128
S = 256
D = 1024
KB = D // P
SLOT = 4480
NSLOT = 5
NEG = -1.0e30
ALPHA = (2 * 2) ** 0.25
N_EXP = 8
FE = 3584
FF2 = 2816


def constants():
    parts, at = [], {}
    n = 0

    def add(name, a):
        nonlocal n
        a = np.asarray(a, np.float32).reshape(P, -1)
        at[name] = (n, a.shape[1])
        parts.append(a)
        n += a.shape[1]

    i = np.arange(P)
    add("ident", np.eye(P))
    add("ones", np.ones((P, P)))
    add("upper", (i[:, None] <= i[None, :]))
    add("lower", (i[:, None] >= i[None, :]))
    add("strict", (i[:, None] < i[None, :]))
    add("iota", np.tile(np.arange(S), (P, 1)))
    t = np.arange(S)
    d = np.abs(t[:, None] - t[None, :])
    cnt = (d <= 64).astype(np.float32) + (d % 4 == 0) + (d % 16 == 0)
    tok = lambda a: np.asarray(a, np.float32).reshape(2, P, -1).transpose(1, 0, 2)
    add("cnt", tok(cnt))
    add("mask_a", tok(np.where(cnt > 0, 0.0, NEG)))
    add("mask_f", tok(np.where(t[None, :] <= t[:, None], 0.0, NEG)))
    add("mask_b", tok(np.where(t[None, :] >= t[:, None], 0.0, NEG)))
    nn = np.arange(32)
    cend = 16 * nn + 31
    ok = (cend[None, :] <= t[:, None]) & (nn[None, :] < 15)
    add("mask_c", tok(np.where(ok, 0.0, NEG)))
    add("any_c", tok(ok.any(axis=1)))
    inv = (np.float32(10000.0) ** (-np.arange(32, dtype=np.float32) / np.float32(32))).astype(np.float32)
    ang = (t.astype(np.float32)[:, None] * inv[None, :]).astype(np.float32)
    add("cos", tok(np.cos(ang)))
    add("sin", tok(np.sin(ang)))
    angc = (np.tile(cend, 4).astype(np.float32)[:, None] * inv[None, :]).astype(np.float32)
    add("cos_c", np.cos(angc))
    add("sin_c", np.sin(angc))
    pool = np.zeros((P, 2, 4, S), np.float32)
    for g, w in enumerate((2, 4, 8, 16)):
        m = np.zeros((S, S), np.float32)
        for q in range(S):
            lo = max(q + 1 - w, 0)
            m[lo:q + 1, q] = np.float32(1.0) / np.float32(min(q + 1, w))
            m[q, q] -= 1.0
        pool[:, :, g, :] = m.reshape(2, P, S).transpose(1, 0, 2)
    return at, np.concatenate(parts, axis=1), pool.reshape(P, -1)


class Op:

    def __init__(self, eng, fn, waits, part):
        self.eng, self.fn, self.waits, self.part = eng, fn, waits, part
        self.used = False
        self.sem = self.value = None


class Mark:

    def __init__(self, sem, value):
        self.sem, self.value = sem, value


class Queues:

    ENGINES = ("tensor", "vector", "scalar", "gpsimd", "sync")

    def __init__(self, nc, ctx):
        self.nc, self.ctx = nc, ctx
        self.q = {}
        self.part = "main"
        self.last = {}
        self.dcount = {}

    def add(self, eng, fn, waits, chain):
        ws = [w for w in waits if w is not None]
        prev = self.last.get((self.part, eng))
        if chain and prev is not None:
            ws.append(prev)
        for w in ws:
            if isinstance(w, Op):
                w.used = True
        op = Op(eng, fn, ws, self.part)
        self.q.setdefault((self.part, eng), []).append(op)
        self.last[(self.part, eng)] = op
        return op

    def pe(self, fn, *w):
        return self.add("tensor", fn, w, False)

    def v(self, fn, *w):
        return self.add("vector", fn, w, True)

    def a(self, fn, *w):
        return self.add("scalar", fn, w, True)

    def g(self, fn, *w):
        return self.add("gpsimd", fn, w, True)

    def dma(self, eng, sem, out, in_, *w):
        n = self.dcount[sem] = self.dcount.get(sem, 0) + 16
        self.add(eng, lambda e: e.dma_start(out, in_).then_inc(sem, 16), w, False).dma = True
        self.last.pop((self.part, eng), None)
        return Mark(sem, n)

    def number(self):
        self.total = {}
        for (part, eng), ops in self.q.items():
            sem = None
            n = 0
            for op in ops:
                if op.used:
                    if sem is None:
                        sem = self.ctx.enter_context(self.nc.semaphore(f"s_{part}_{eng}"))
                    n += 1
                    op.sem, op.value = sem, n
            if sem is not None:
                self.total[(part, eng)] = Mark(sem, n)

    def emit(self, e, eng, part, seen):
        for op in self.q.get((part, eng), []):
            need = {}
            for w in op.waits:
                if seen.get(w.sem, 0) < w.value:
                    need[w.sem] = max(need.get(w.sem, 0), w.value)
            for sem, value in need.items():
                e.wait_ge(sem, value)
                seen[sem] = value
            ins = op.fn(e)
            if op.used:
                ins.then_inc(op.sem, 1)


class Banks:

    def __init__(self, psum, numbers):
        self.psum, self.numbers, self.n = psum, numbers, 0
        self.free = {}

    def take(self):
        b = self.numbers[self.n % len(self.numbers)]
        self.n += 1
        return b, self.psum[:, b, :], self.free.get(b)

    def give(self, b, *ops):
        self.free[b] = ops[-1]


def build(nc, d, out, tables):
    at, cons_cols, pool_cols = tables
    with ExitStack() as ctx:
        q = Queues(nc, ctx)

        def sb(name, cols, dt=F32, rows=P):
            return ctx.enter_context(nc.sbuf_tensor(name, [rows, cols], dt))

        psum = ctx.enter_context(nc.psum_tensor("psum", [P, 8, 512], F32))
        ring = sb("ring", NSLOT * SLOT)
        cons = sb("cons", cons_cols)
        par = sb("par", 512)
        bcs = sb("bcs", 3 * D)
        X = sb("X", 2 * D)[:].rearrange("p (t n) -> p t n", t=2)
        XT = sb("XT", KB * S)[:].rearrange("p (k s) -> p k s", k=KB)
        SML = sb("SML", 1024)
        AR = sb("AR", 18464)
        flag = sb("flag", 1, I32)

        def sem(name):
            return ctx.enter_context(nc.semaphore(name))

        s_ring = [sem(f"s_ring{i}") for i in range(NSLOT)]
        s_bc = [sem(f"s_bc{i}") for i in range(3)]
        s_x, s_c, s_p, s_out = sem("s_x"), sem("s_c"), sem("s_p"), sem("s_out")
        s_ov = [sem(f"s_ov{i}") for i in range(NSLOT)]

        def C(name, rows=P):
            a, n = at[name]
            return cons[0:rows, a:a + n]

        def C2(name):
            return C(name).rearrange("p (t n) -> p t n", t=2)

        ident = C("ident")

        small = [0]

        def sm(n):
            a = small[0]
            if a + n > 1024:
                a = 0
            small[0] = a + n
            return SML[:, a:a + n]

        slot_n = [0]
        slot_free = [None] * NSLOT
        over = [False]

        def load(*pieces):
            i = slot_n[0] % NSLOT
            slot_n[0] += 1
            views, mark = [], None
            for off, cols, src, view in pieces:
                dst = view(ring[:, i * SLOT + off:i * SLOT + off + cols])
                mark = q.dma("sync", (s_ov if over[0] else s_ring)[i], dst, src, slot_free[i])
                views.append(dst)
            return i, views, mark

        def done(i, op):
            slot_free[i] = op

        def cols_tile(w, a, b):
            n = b - a
            return (0, KB * n, w[:, a:b].rearrange("(k p) n -> p k n", p=P),
                    lambda r: r.rearrange("p (k n) -> p k n", k=KB))

        def rows_tile(w, a, kb):
            return (0, kb * D, w[a:a + kb * P, :].rearrange("(k p) n -> p k n", p=P),
                    lambda r: r.rearrange("p (k n) -> p k n", k=kb))

        bc_n = [0]
        bc_free = [None] * 3

        def bcast(src, n):
            i = bc_n[0] % 3
            bc_n[0] += 1
            dst = bcs[:, i * D:i * D + n]
            mark = q.dma("gpsimd", s_bc[i], dst, src.partition_broadcast(P), bc_free[i])
            return i, dst, mark

        def bdone(i, op):
            bc_free[i] = op

        m_x = q.dma("sync", s_x, X, d["x"][0].rearrange("(t p) n -> p t n", p=P))
        m_c = q.dma("gpsimd", s_c, cons[:], d["cons"])
        m_p = None
        pat = {}
        n = 0
        for name in ("n1g", "n2g", "cw", "pek", "pev"):
            w = d[name].shape[1]
            m_p = q.dma("gpsimd", s_p, par[:, n:n + w], d[name])
            pat[name] = (n, w)
            n += w
        for name in ("gib", "gfb"):
            m_p = q.dma("gpsimd", s_p, par[:, n:n + 16], d[name].partition_broadcast(P))
            pat[name] = (n, 16)
            n += 16

        def PR(name):
            a, w = pat[name]
            return par[:, a:a + w]

        B4 = Banks(psum, [0, 1, 2, 3])
        BA = [4, 5, 6, 7]
        acc_free = [None] * 8

        def mms(b, out_ap, pairs, *waits, start=True, stop=True):
            def go(e):
                for n, (l, r) in enumerate(pairs):
                    ins = e.matmul(out_ap, lhsT=l, rhs=r, start=start and n == 0,
                                   stop=stop and n == len(pairs) - 1)
                return ins
            return q.pe(go, *waits)

        def bc3(ap, n, axis=2):
            a = ap.unsqueeze(axis)
            sh = list(a.shape)
            sh[axis] = n
            return a.to_broadcast(sh)

        def to_cols(src, dst, nblk, ready, gain=None, first=None):
            op = None
            for tt in range(2):
                for k0 in range(0, nblk, 4):
                    nb = min(4, nblk - k0)
                    b, bank, fr = B4.take()

                    def go(e, bank=bank, tt=tt, k0=k0, nb=nb):
                        for j in range(nb):
                            ins = e.transpose(bank[:, j * P:(j + 1) * P], src(tt, k0 + j), ident)
                        return ins
                    t = q.pe(go, ready, fr, m_c)
                    pv = bank[:, 0:nb * P].rearrange("p (k s) -> p k s", k=nb)
                    if gain is not None:
                        op = q.v(lambda e, pv=pv, k0=k0, nb=nb, tt=tt: e.tensor_tensor(
                            dst(k0, nb, tt), pv, bc3(gain[:, k0:k0 + nb], P), ALU.mult), t, m_p)
                    else:
                        op = q.v(lambda e, pv=pv, k0=k0, nb=nb, tt=tt: e.tensor_copy(
                            dst(k0, nb, tt), pv), t, first)
                    B4.give(b, op)
            return op

        def xt_dst(k0, nb, tt):
            return XT[:, k0:k0 + nb, tt * P:(tt + 1) * P]

        TMP = AR[:, 0:1024]

        def rstd_of(src, n, eps, tmp, r, *ready):
            ss = sm(1)
            o = q.a(lambda e: e.activation(tmp, src, ACT.Square, accum_out=ss), *ready)
            v = sm(1)
            o = q.v(lambda e: e.tensor_scalar(v, ss, 1.0 / n, eps, ALU.mult, ALU.add), o)
            o = q.a(lambda e: e.activation(r, v, ACT.Sqrt), o)
            return q.v(lambda e: e.reciprocal(r, r), o)

        def rms_cols(gain, ready):
            op = ready
            rows = AR[:, 0:2048].rearrange("p (t n) -> p t n", t=2)
            for tt in range(2):
                r = sm(1)
                o = rstd_of(X[:, tt, :], D, 1e-6, rows[:, tt, :], r, ready)
                op = q.v(lambda e, tt=tt, r=r: e.tensor_scalar(
                    rows[:, tt, :], X[:, tt, :], r, None, ALU.mult), o)
            return to_cols(lambda tt, k: rows[:, tt, k * P:(k + 1) * P], xt_dst, KB, op, gain, None)

        def layer_norm(i, j, ready):
            gi, g, mg = bcast(d["ln_g_2"][i, j], D)
            bi, b, mb = bcast(d["ln_b_2"][i, j], D)
            op = ready
            for tt in range(2):
                x = X[:, tt, :]
                s1, mu, r = sm(1), sm(1), sm(1)
                q.v(lambda e, x=x, s1=s1: e.tensor_reduce(s1, x, AX.X, ALU.add), ready)
                q.v(lambda e, s1=s1, mu=mu: e.tensor_scalar(mu, s1, 1.0 / D, None, ALU.mult))
                o = q.v(lambda e, x=x, mu=mu: e.tensor_scalar(x, x, mu, None, ALU.subtract))
                o = rstd_of(x, D, 1e-5, TMP, r, o)
                q.v(lambda e, x=x, r=r: e.scalar_tensor_tensor(x, x, r, g, ALU.mult, ALU.mult), mg)
                op = q.v(lambda e, x=x: e.tensor_tensor(x, x, b, ALU.add), mb)
            bdone(gi, op)
            bdone(bi, op)
            return op

        def x_cols(ready):
            return to_cols(lambda tt, k: X[:, tt, k * P:(k + 1) * P], xt_dst, KB, ready)

        def by_tokens(w, a, b, tt, ready, mark):
            k, bank, fr = B4.take()
            o = mms(k, bank[:, 0:b - a], [(XT[:, j, tt * P:(tt + 1) * P], w[:, j, a:b])
                                          for j in range(KB)], ready, mark, fr)
            return k, bank[:, 0:b - a], o

        def by_cols(lhs, bank_ap, ready, mark, fr):
            return mms(0, bank_ap, [(lhs(j), XT[:, j, :]) for j in range(KB)], ready, mark, fr)

        def rope(src, dst, nh, cos, sin, tmp, *ready):
            s1, s2 = src[:, :, 0:32], src[:, :, 32:64]
            o1, o2 = dst[:, :, 0:32], dst[:, :, 32:64]
            t = tmp[:, 0:nh * 64].rearrange("p (h c) -> p h c", h=nh)
            cb, nb = bc3(cos, nh, 1), bc3(sin, nh, 1)
            q.v(lambda e: e.tensor_tensor(o1, s1, cb, ALU.mult), *ready)
            q.v(lambda e: e.tensor_tensor(o2, s2, cb, ALU.mult))
            q.v(lambda e: e.tensor_tensor(t[:, :, 0:32], s2, nb, ALU.mult))
            last = q.v(lambda e: e.tensor_tensor(t[:, :, 32:64], s1, nb, ALU.mult))
            q.v(lambda e: e.tensor_tensor(o1, o1, t[:, :, 0:32], ALU.subtract))
            op = q.v(lambda e: e.tensor_tensor(o2, o2, t[:, :, 32:64], ALU.add))
            return last, op

        def project_out(w, yt_ready, alpha):
            op = None
            for nh in range(2):
                i, (wv,), mk = load(cols_tile(w, nh * 512, nh * 512 + 512))
                for tt in range(2):
                    k, bank, o = by_tokens(wv, 0, 512, tt, yt_ready, mk)
                    xs = X[:, tt, nh * 512:nh * 512 + 512]
                    op = q.v(lambda e, xs=xs, bank=bank: e.scalar_tensor_tensor(
                        xs, xs, alpha, bank, ALU.mult, ALU.add), o)
                    B4.give(k, op)
                done(i, o)
            return op

        HC = AR[:, 2048:2048 + 4096].rearrange("p (b j s) -> p b j s", b=2, j=8)

        def ffn(nchunk, chunk_kb, load_up, act, load_down, ready, alpha):
            state = {}
            hfree = [None, None]

            def up(c):
                hb = c % 2
                i, views, mk = load_up(c)
                op = None
                for j in range(chunk_kb):
                    op, o = act(views, j, HC[:, hb, j, :], mk, hfree[hb])
                done(i, o)
                state[c] = op

            def down(c):
                hb = c % 2
                i, (wv,), mk = load_down(c)
                for tt in range(2):
                    for nh in range(2):
                        b = BA[tt * 2 + nh]
                        o = mms(b, psum[:, b, :], [
                            (HC[:, hb, j, tt * P:(tt + 1) * P], wv[:, j, nh * 512:nh * 512 + 512])
                            for j in range(chunk_kb)], state[c], mk, acc_free[b],
                            start=c == 0, stop=c == nchunk - 1)
                hfree[hb] = o
                done(i, o)
                return o

            for c in range(nchunk + 1):
                if c < nchunk:
                    up(c)
                if c:
                    last = down(c - 1)
            op = None
            for tt in range(2):
                for nh in range(2):
                    b = BA[tt * 2 + nh]
                    xs = X[:, tt, nh * 512:nh * 512 + 512]
                    op = q.v(lambda e, xs=xs, b=b: e.scalar_tensor_tensor(
                        xs, xs, alpha, psum[:, b, :], ALU.mult, ALU.add), last)
                    acc_free[b] = op
            return op

        tmp_n = [0]

        def softmax_block(bank, nk, nh, mask, cnt, scale, W, fr_b, o):
            pv = bank.rearrange("p (h k) -> p h k", h=nh)
            w3 = W.rearrange("p (h k) -> p h k", h=nh)
            mx, l = sm(nh), sm(nh)
            rd = q.v(lambda e: e.scalar_tensor_tensor(w3, pv, scale, bc3(mask, nh, 1),
                                                      ALU.mult, ALU.add), o, fr_b)
            q.v(lambda e: e.tensor_reduce(mx, w3, AX.X, ALU.max))
            o = q.v(lambda e: e.tensor_tensor(w3, w3, bc3(mx, nk), ALU.subtract))
            o = q.a(lambda e: e.activation(W, W, ACT.Exp), o)
            if cnt is not None:
                o = q.v(lambda e: e.tensor_tensor(w3, w3, bc3(cnt, nh, 1), ALU.mult), o)
            o = q.v(lambda e: e.tensor_reduce(l, w3, AX.X, ALU.add), o)
            return rd, o, l

        def transposed_block(blocks, PT, o, fr_pt):
            b, bank, fr = B4.take()
            nb = len(blocks)

            def go(e):
                for i, src in enumerate(blocks):
                    ins = e.transpose(bank[:, i * P:(i + 1) * P], src, ident)
                return ins
            t = q.pe(go, o, fr)
            c = q.a(lambda e: e.activation(PT[:, 0:nb * P], bank[:, 0:nb * P], ACT.Copy), t, fr_pt)
            B4.give(b, c)
            return t, c

        def attention(nblk, qT, kz, v, mask, cnt, causal, W2, PT2, obanks, ready):
            res = []
            wfree, ptfree = [None, None], [None, None]
            n = 0
            pend = None
            for qt in range(2):
                nk = P if (causal and qt == 0) else S
                L = sm(2 * nblk)
                for b in range(nblk):
                    k, bank, fr = B4.take()
                    o = mms(k, bank[:, 0:2 * nk], [(qT[:, b, qt * P:(qt + 1) * P],
                                                    kz(b)[:, :, 0:nk])], ready, fr)
                    W = W2[:, n % 2, 0:2 * nk]
                    rd, o, l = softmax_block(bank[:, 0:2 * nk], nk, 2, mask[:, qt, 0:nk],
                                             None if cnt is None else cnt[:, qt, :],
                                             0.125, W, wfree[n % 2], o)
                    B4.give(k, rd)
                    o = q.v(lambda e, L=L, b=b, l=l: e.tensor_copy(L[:, 2 * b:2 * b + 2], l))
                    cur = (qt, b, nk, n, W, o)
                    if pend is not None:
                        last = finish(pend, v, PT2, obanks, wfree, ptfree)
                        if pend[0] != qt:
                            res[-1][1] = last
                    pend = cur
                    n += 1
                res.append([L, None])
            res[-1][1] = finish(pend, v, PT2, obanks, wfree, ptfree)
            return res

        def finish(cur, v, PT2, obanks, wfree, ptfree):
            qt, b, nk, n, W, o = cur
            kt = nk // P
            PT = PT2[:, n % 2, :]
            t, c = transposed_block([W[:, i * P:(i + 1) * P] for i in range(2 * kt)], PT, o,
                                    ptfree[n % 2])
            wfree[n % 2] = t
            for h in range(2):
                head = 2 * b + h
                ob = obanks[qt][head // 8]
                col = (head % 8) * 64
                last = mms(ob, psum[:, ob, col:col + 64],
                           [(PT[:, (h * kt + i) * P:(h * kt + i + 1) * P], v(i, head))
                            for i in range(kt)], c, acc_free[ob])
            ptfree[n % 2] = last
            return last

        def hybrid(l, ready):
            w_in = d["w_in"][l]
            xr = rms_cols(PR("n1g")[:, l * KB:(l + 1) * KB], ready)
            A = lambda a, n: AR[:, a:a + n]
            PADW = S + 4
            pad = A(0, 8 * PADW).rearrange("p (b s) -> p b s", b=8)
            kz = A(0, 2048).rearrange("p (b h s) -> p b h s", b=4, h=2)
            qk = A(2080, 2048).rearrange("p (b s) -> p b s", b=8)
            mv = A(4128, 1024).rearrange("p (t n) -> p t n", t=2)
            mo = A(5152, 1024).rearrange("p (t n) -> p t n", t=2)
            aq = A(6176, 1024).rearrange("p (t n) -> p t n", t=2)
            ak = A(7200, 1024).rearrange("p (t n) -> p t n", t=2)
            qks = A(6176, 2048).rearrange("p (t n) -> p t n", t=2)
            av = A(8224, 1024).rearrange("p (t n) -> p t n", t=2)
            qT = A(9248, 1024).rearrange("p (b s) -> p b s", b=4)
            Y = A(10272, 2048).rearrange("p (t n) -> p t n", t=2)
            W2 = A(12320, 2048).rearrange("p (t n) -> p t n", t=2)
            PT2 = A(14368, 2048).rearrange("p (t n) -> p t n", t=2)
            HM = A(16416, 1024).rearrange("p (t n) -> p t n", t=2)
            TM = A(17440, 1024)

            z1 = q.v(lambda e: e.memset(pad[:, :, 0:2], 0.0), xr)
            z1 = q.v(lambda e: e.memset(pad[:, :, PADW - 2:PADW], 0.0))
            cw = PR("cw").rearrange("p (l b k) -> p l b k", l=2, b=8)
            for part in range(2):
                i, (wv,), mk = load(cols_tile(w_in, part * 512, part * 512 + 512))
                for jj in range(2):
                    b, bank, fr = B4.take()
                    for h in range(2):
                        j = jj * 2 + h
                        o = by_cols(lambda k, j=j, wv=wv: wv[:, k, j * P:(j + 1) * P],
                                    bank[:, h * S:(h + 1) * S], xr, mk, fr)
                    blk = part * 4 + jj * 2
                    c = q.a(lambda e, blk=blk, bank=bank: e.activation(
                        pad[:, blk:blk + 2, 2:2 + S], bank.rearrange("p (b s) -> p b s", b=2),
                        ACT.Copy), o, xr)
                    B4.give(b, c)
                    for j in range(blk, blk + 2):
                        q.v(lambda e, j=j: e.tensor_scalar(
                            qk[:, j, :], pad[:, j, 0:S], cw[:, l, j, 0:1], None, ALU.mult), c, m_p)
                        for k in range(1, 5):
                            o2 = q.v(lambda e, j=j, k=k: e.scalar_tensor_tensor(
                                qk[:, j, :], pad[:, j, k:k + S], cw[:, l, j, k:k + 1], qk[:, j, :],
                                ALU.mult, ALU.add))
                    qk_op = q.a(lambda e, blk=blk: e.activation(
                        qk[:, blk:blk + 2, :], qk[:, blk:blk + 2, :], ACT.Silu), o2)
                done(i, o)
            conv_done = o2
            i, (wv,), mk = load(cols_tile(w_in, 1024, 1536))
            for tt in range(2):
                k, bank, o = by_tokens(wv, 0, 512, tt, xr, mk)
                mv_op = q.a(lambda e, tt=tt, bank=bank: e.activation(mv[:, tt, :], bank, ACT.Copy), o)
                B4.give(k, mv_op)
            done(i, o)
            i, (wv,), mk = load(cols_tile(w_in, 1536, 2064))
            for tt in range(2):
                k, bank, o = by_tokens(wv, 0, 512, tt, xr, mk)
                mo_op = q.a(lambda e, tt=tt, bank=bank: e.activation(
                    mo[:, tt, :], bank, ACT.Sigmoid), o)
                B4.give(k, mo_op)
            G = sm(32).rearrange("p (t g) -> p t g", t=2)
            for tt in range(2):
                k, bank, o = by_tokens(wv, 512, 528, tt, xr, mk)
                q.v(lambda e, tt=tt, bank=bank: e.tensor_tensor(
                    G[:, tt, 0:8], bank[:, 0:8], PR("gib")[:, l * 8:l * 8 + 8], ALU.add), o, m_p)
                g_op = q.v(lambda e, tt=tt, bank=bank: e.tensor_tensor(
                    G[:, tt, 8:16], bank[:, 8:16], PR("gfb")[:, l * 8:l * 8 + 8], ALU.add))
                B4.give(k, g_op)
            done(i, o)
            aop = None
            for dst, c0 in ((aq, 2064), (ak, 2576)):
                i, (wv,), mk = load(cols_tile(w_in, c0, c0 + 512))
                for tt in range(2):
                    k, bank, o = by_tokens(wv, 0, 512, tt, xr, mk)
                    rd, aop = rope(bank.rearrange("p (h c) -> p h c", h=8),
                                   dst[:, tt, :].rearrange("p (h c) -> p h c", h=8), 8,
                                   C2("cos")[:, tt, :], C2("sin")[:, tt, :], TM[:, 0:512], o, m_c)
                    B4.give(k, rd)
                done(i, o)
            i, (wv,), mk = load(cols_tile(w_in, 3088, 3600))
            for tt in range(2):
                k, bank, o = by_tokens(wv, 0, 512, tt, xr, mk)
                av_op = q.a(lambda e, tt=tt, bank=bank: e.activation(av[:, tt, :], bank, ACT.Copy), o)
                B4.give(k, av_op)
            done(i, o)
            qt_op = to_cols(lambda tt, k: aq[:, tt, k * P:(k + 1) * P],
                            lambda k0, nb, tt: qT[:, k0:k0 + nb, tt * P:(tt + 1) * P], 4, aop)
            q.v(lambda e: e.memset(kz, 0.0), conv_done)
            for tt in range(2):
                b, bank, fr = B4.take()

                def go(e, tt=tt, bank=bank):
                    for j in range(4):
                        ins = e.transpose(bank[:, j * P:(j + 1) * P], ak[:, tt, j * P:(j + 1) * P],
                                          ident)
                    return ins
                t = q.pe(go, aop, fr)
                pv = bank.rearrange("p (k s) -> p k s", k=4)
                q.v(lambda e, tt=tt, pv=pv: e.tensor_copy(
                    kz[0:64, :, 0, tt * P:(tt + 1) * P], pv[0:64]), t)
                kz_op = q.v(lambda e, tt=tt, pv=pv: e.tensor_copy(
                    kz[64:128, :, 1, tt * P:(tt + 1) * P], pv[64:128]))
                B4.give(b, kz_op)

            f = G[:, :, 8:16]
            ab, ex, ln, LF, CC, BB = (sm(16).rearrange("p (t g) -> p t g", t=2) for _ in range(6))
            o = q.v(lambda e: e.scalar_tensor_tensor(ab, f, -1.0, f, ALU.mult, ALU.max), g_op)
            o = q.a(lambda e: e.activation(ex, ab, ACT.Exp, scale=-1.0), o)
            o = q.v(lambda e: e.tensor_scalar(ex, ex, 1.0, None, ALU.add), o)
            o = q.a(lambda e: e.activation(ln, ex, ACT.Ln), o)
            o = q.v(lambda e: e.scalar_tensor_tensor(LF, f, 0.0, ln, ALU.min, ALU.subtract), o)
            b, bank, fr = B4.take()
            ct = bank[:, 0:16].rearrange("p (t g) -> p t g", t=2)
            up, lo, on = C("upper"), C("lower"), C("ones")

            def cums(e):
                for tt, dr, pairs in ((0, 0, [(up, 0)]), (1, 0, [(on, 0), (up, 1)]),
                                      (1, 1, [(lo, 1)]), (0, 1, [(lo, 0), (on, 1)])):
                    for n, (m, s) in enumerate(pairs):
                        ins = e.matmul(ct[:, tt, dr * 4:dr * 4 + 4], lhsT=m,
                                       rhs=LF[:, s, dr * 4:dr * 4 + 4], start=n == 0,
                                       stop=n == len(pairs) - 1)
                return ins
            o = q.pe(cums, o, fr)
            o = q.v(lambda e: e.tensor_copy(BB, ct), o)
            B4.give(b, o)
            o = q.v(lambda e: e.tensor_tensor(CC, G[:, :, 0:8], BB, ALU.subtract))
            b, bank, fr = B4.take()

            def tr(e, bank=bank):
                for tt in range(2):
                    ins = e.transpose(bank[0:8, tt * P:(tt + 1) * P], CC[:, tt, :], ident)
                return ins
            o = q.pe(tr, o, fr)
            CT = TM[0:8, 512:768]
            ct_op = q.v(lambda e, bank=bank: e.tensor_copy(CT, bank[0:8, 0:256]), o)
            B4.give(b, ct_op)

            for qt in range(2):
                for hp in range(2):
                    b, bank, fr = B4.take()

                    def sc(e, qt=qt, hp=hp, bank=bank):
                        for h in range(2):
                            hd = hp * 2 + h
                            ins = e.matmul(bank[:, h * S:(h + 1) * S],
                                           lhsT=qk[:, hd, qt * P:(qt + 1) * P],
                                           rhs=qk[:, 4 + hd, :], start=True, stop=True)
                        return ins
                    o = q.pe(sc, qk_op, fr)
                    qs_op = q.a(lambda e, qt=qt, hp=hp, bank=bank: e.activation(
                        qks[:, qt, hp * 512:(hp + 1) * 512], bank, ACT.Copy,
                        scale=1.0 / math.sqrt(128.0)), o, kz_op, qt_op)
                    B4.give(b, qs_op)
            wf = [None, None]
            ptf = [None, None]
            n = 0
            for dr in range(2):
                cbb = BA[0:2]

                def cb(e, dr=dr, cbb=cbb):
                    for h in range(4):
                        ins = e.matmul(psum[:, cbb[h // 2], (h % 2) * S:(h % 2) * S + S],
                                       lhsT=ident[0:8, dr * 4 + h:dr * 4 + h + 1].to_broadcast([8, P]),
                                       rhs=CT, start=True, stop=True)
                    return ins
                cb_op = q.pe(cb, ct_op, acc_free[cbb[0]], acc_free[cbb[1]])
                mask = C2("mask_b" if dr else "mask_f")
                for qt in range(2):
                    k0, k1 = ((0, P), (0, S), (0, S), (P, S))[dr * 2 + qt]
                    nk = k1 - k0
                    W = W2[:, n % 2, 0:4 * nk]
                    w3 = W.rearrange("p (h k) -> p h k", h=4)
                    mx, den, en = sm(4), sm(4), sm(4)
                    for hp in range(2):
                        pv = psum[:, cbb[hp], :].rearrange("p (h k) -> p h k", h=2)
                        rd = q.v(lambda e, hp=hp, pv=pv, w3=w3, k0=k0, k1=k1, qt=qt, mask=mask:
                                 e.tensor_tensor(w3[:, hp * 2:hp * 2 + 2, :], pv[:, :, k0:k1],
                                                 bc3(mask[:, qt, k0:k1], 2, 1), ALU.add),
                                 cb_op, wf[n % 2])
                        acc_free[cbb[hp]] = rd
                    q.v(lambda e, w3=w3, mx=mx: e.tensor_reduce(mx, w3, AX.X, ALU.max))
                    o = q.v(lambda e, w3=w3, mx=mx, nk=nk: e.tensor_tensor(
                        w3, w3, bc3(mx, nk), ALU.subtract))
                    o = q.a(lambda e, W=W: e.activation(W, W, ACT.Exp), o)
                    qv = qks[:, qt, :].rearrange("p (h k) -> p h k", h=4)
                    q.v(lambda e, w3=w3, qv=qv, k0=k0, k1=k1: e.tensor_tensor(
                        w3, w3, qv[:, :, k0:k1], ALU.mult), o, qs_op)
                    w_op = q.v(lambda e, w3=w3, den=den: e.tensor_reduce(den, w3, AX.X, ALU.add))
                    o = q.v(lambda e, mx=mx, qt=qt, dr=dr: e.tensor_tensor(
                        mx, mx, BB[:, qt, dr * 4:dr * 4 + 4], ALU.add))
                    o = q.a(lambda e, mx=mx, en=en: e.activation(en, mx, ACT.Exp, scale=-1.0), o)
                    q.v(lambda e, den=den, mx=mx: e.scalar_tensor_tensor(
                        mx, den, -1.0, den, ALU.mult, ALU.max), o)
                    q.v(lambda e, en=en, mx=mx: e.tensor_tensor(en, en, mx, ALU.max))
                    q.v(lambda e, en=en: e.reciprocal(en, en))
                    ob = BA[2 + n % 2]
                    kt = nk // P
                    pvs = []
                    for hp in range(0, 4, 2):
                        PT = PT2[:, hp // 2, :]
                        t, c = transposed_block(
                            [W[:, (h * kt + i) * P:(h * kt + i + 1) * P]
                             for h in (hp, hp + 1) for i in range(kt)], PT, w_op, ptf[hp // 2])
                        for h in (hp, hp + 1):
                            o = mms(ob, psum[:, ob, h * P:(h + 1) * P],
                                    [(PT[:, ((h - hp) * kt + i) * P:((h - hp) * kt + i + 1) * P],
                                      mv[:, k0 // P + i, h * P:(h + 1) * P]) for i in range(kt)],
                                    c, mv_op, acc_free[ob])
                        ptf[hp // 2] = o
                    wf[n % 2] = t
                    ov = psum[:, ob, :].rearrange("p (h k) -> p h k", h=4)
                    hm = HM[:, qt, :].rearrange("p (h k) -> p h k", h=4)
                    if dr == 0:
                        h_op = q.v(lambda e, hm=hm, ov=ov, en=en: e.tensor_tensor(
                            hm, ov, bc3(en, P), ALU.mult), o)
                        acc_free[ob] = h_op
                    else:
                        tm = TM[:, 0:512].rearrange("p (h k) -> p h k", h=4)
                        r = q.v(lambda e, tm=tm, ov=ov, en=en: e.tensor_tensor(
                            tm, ov, bc3(en, P), ALU.mult), o)
                        acc_free[ob] = r
                        h_op = q.v(lambda e, hm=hm, tm=tm: e.tensor_tensor(hm, hm, tm, ALU.add))
                    n += 1
            gi, hg, mg = bcast(d["head_norm_g"][l], 512)
            for qt in range(2):
                hm = HM[:, qt, :].rearrange("p (h k) -> p h k", h=4)
                tm = TM[:, 0:512].rearrange("p (h k) -> p h k", h=4)
                ss = sm(4)
                q.v(lambda e, hm=hm, tm=tm: e.tensor_tensor(tm, hm, hm, ALU.mult))
                q.v(lambda e, tm=tm, ss=ss: e.tensor_reduce(ss, tm, AX.X, ALU.add))
                o = q.v(lambda e, ss=ss: e.tensor_scalar(ss, ss, 1.0 / P, 1e-6, ALU.mult, ALU.add))
                o = q.a(lambda e, ss=ss: e.activation(ss, ss, ACT.Sqrt), o)
                q.v(lambda e, ss=ss: e.reciprocal(ss, ss), o)
                q.v(lambda e, hm=hm, ss=ss: e.tensor_tensor(hm, hm, bc3(ss, P), ALU.mult))
                o = q.v(lambda e, qt=qt: e.tensor_tensor(HM[:, qt, :], HM[:, qt, :], hg, ALU.mult),
                        mg, mo_op)
                ym = q.v(lambda e, qt=qt: e.tensor_tensor(
                    Y[:, qt, 0:512], HM[:, qt, :], mo[:, qt, :], ALU.mult))
            bdone(gi, o)

            res = attention(4, qT, lambda b: kz[:, b, :, :], lambda i, h: av[:, i, h * 64:h * 64 + 64],
                            C2("mask_a"), C2("cnt"), False, W2, PT2, [[BA[0]], [BA[2]]], kz_op)
            for qt in range(2):
                L, last = res[qt]
                ob = (BA[0], BA[2])[qt]
                q.v(lambda e, L=L: e.reciprocal(L, L))
                y_op = q.v(lambda e, L=L, ob=ob, qt=qt: e.tensor_tensor(
                    Y[:, qt, 512:1024].rearrange("p (h c) -> p h c", h=8),
                    psum[:, ob, :].rearrange("p (h c) -> p h c", h=8), bc3(L, 64), ALU.mult), last)
                acc_free[ob] = y_op
            yt = to_cols(lambda tt, k: Y[:, tt, k * P:(k + 1) * P], xt_dst, KB, y_op)
            xo = project_out(d["w_out"][l], yt, 1.0)

            xr = rms_cols(PR("n2g")[:, l * KB:(l + 1) * KB], xo)
            RL = AR[:, 8192:8192 + 1024].rearrange("p (b n) -> p b n", b=2)
            rn = [0]

            def act(views, j, dst, mk, fr_h):
                b, bank, fr = B4.take()
                o = by_cols(lambda k: views[0][:, k, j * P:(j + 1) * P], bank[:, 0:S], xr, mk, fr)
                r = RL[:, rn[0] % 2, 0:S]
                rn[0] += 1
                c = q.a(lambda e: e.activation(r, bank[:, 0:S], ACT.Relu), o)
                B4.give(b, c)
                op = q.a(lambda e: e.activation(dst, r, ACT.Square), fr_h)
                return op, o

            return ffn(8, 4, lambda c: load(cols_tile(d["w_up"][l], c * 512, c * 512 + 512)), act,
                       lambda c: load(rows_tile(d["w_down"][l], c * 512, 4)), xr, 1.0)

        def final_rms(ready):
            gi, g, mg = bcast(d["final_g"], D)
            for tt in range(2):
                r = sm(1)
                rstd_of(X[:, tt, :], D, 1e-6, TMP, r, ready)
                op = q.v(lambda e, tt=tt, r=r: e.scalar_tensor_tensor(
                    X[:, tt, :], X[:, tt, :], r, g, ALU.mult, ALU.mult), mg)
            bdone(gi, op)
            return op

        def pool_layer(ready):
            si, sc, ms = bcast(d["pool_scale_2"][0], D)
            i, (pm,), mk = load((0, 2048, d["poolm"], lambda r: r))
            pm = pm.rearrange("p (t g s) -> p t g s", t=2, g=4)
            PX = AR[:, 2048:4096].rearrange("p (k s) -> p k s", k=8)
            for kp in range(4):
                b, bank, fr = B4.take()

                def go(e, kp=kp, bank=bank):
                    for h in range(2):
                        k = kp * 2 + h
                        for jt in range(2):
                            ins = e.matmul(bank[:, h * S:(h + 1) * S],
                                           lhsT=X[:, jt, k * P:(k + 1) * P], rhs=pm[:, jt, k // 2, :],
                                           start=jt == 0, stop=jt == 1)
                    return ins
                o = q.pe(go, ready, mk, fr)
                c = q.v(lambda e, kp=kp, bank=bank: e.tensor_copy(
                    PX[:, kp * 2:kp * 2 + 2, :], bank.rearrange("p (k s) -> p k s", k=2)), o)
                B4.give(b, c)
            done(i, o)
            i, (pw,), mk = load((0, 2048, d["pool_w_2"][0].rearrange("g (c p) n -> p (g c) n", p=P),
                                 lambda r: r.rearrange("p (g n) -> p g n", g=8)))
            for tt in range(2):
                for nh in range(2):
                    b, bank, fr = B4.take()

                    def go(e, tt=tt, nh=nh, bank=bank):
                        for gg in range(2):
                            g = nh * 2 + gg
                            for c in range(2):
                                ins = e.matmul(bank[:, gg * 256:gg * 256 + 256],
                                               lhsT=PX[:, g * 2 + c, tt * P:(tt + 1) * P],
                                               rhs=pw[:, g * 2 + c, :], start=c == 0, stop=c == 1)
                        return ins
                    o = q.pe(go, c, mk, fr)
                    t = AR[:, 4096:4608]
                    xs = X[:, tt, nh * 512:nh * 512 + 512]
                    r = q.v(lambda e, bank=bank, t=t, nh=nh: e.tensor_tensor(
                        t, bank, sc[:, nh * 512:nh * 512 + 512], ALU.mult), o, ms)
                    B4.give(b, r)
                    op = q.v(lambda e, xs=xs, t=t: e.scalar_tensor_tensor(
                        xs, xs, ALPHA, t, ALU.mult, ALU.add))
            done(i, o)
            bdone(si, r)
            x1 = layer_norm(0, 0, op)
            xc = x_cols(x1)
            wgu, wd = d["ffn_w_gu_2"][0], d["ffn_w_down_2"][0]
            SG = AR[:, 8192:8192 + 512].rearrange("p (b n) -> p b n", b=2)
            rn = [0]

            def load_up(c):
                v3 = lambda r: r.rearrange("p (k n) -> p k n", k=KB)
                src = lambda a: wgu[:, a:a + 256].rearrange("(k p) n -> p k n", p=P)
                return load((0, 2048, src(c * 256), v3), (2048, 2048, src(FF2 + c * 256), v3))

            def act(views, j, dst, mk, fr_h):
                b, bank, fr = B4.take()
                by_cols(lambda k: views[0][:, k, j * P:(j + 1) * P], bank[:, 0:S], xc, mk, fr)
                o = by_cols(lambda k: views[1][:, k, j * P:(j + 1) * P], bank[:, S:2 * S], xc, mk, fr)
                r = SG[:, rn[0] % 2, :]
                rn[0] += 1
                c = q.a(lambda e: e.activation(r, bank[:, 0:S], ACT.Silu), o, rfree[rn[0] % 2])
                op = q.v(lambda e: e.tensor_tensor(dst, r, bank[:, S:2 * S], ALU.mult), c, fr_h)
                rfree[rn[0] % 2] = op
                B4.give(b, op)
                return op, o

            rfree = [None, None]
            op = ffn(FF2 // 256, 2, load_up, act, lambda c: load(rows_tile(wd, c * 256, 2)), xc, ALPHA)
            return layer_norm(0, 1, op)

        def nsa(ready):
            xc = x_cols(ready)
            w_in = d["nsa_w_in_2"][0]
            A = lambda a, n: AR[:, a:a + n]
            two = lambda r: r.rearrange("p (t n) -> p t n", t=2)
            Q = two(A(0, 2048))
            KZ = [A(0, 2048).rearrange("p (g h s) -> p g h s", g=4, h=2),
                  A(2048, 2048).rearrange("p (g h s) -> p g h s", g=4, h=2)]
            KR = [two(A(4096, 512)), two(A(4608, 512))]
            qT = A(5120, 2048).rearrange("p (b s) -> p b s", b=8)
            V = [two(A(7168, 512)), two(A(7680, 512))]
            Y = two(A(8192, 2048))
            W2 = two(A(10240, 1024))
            PT2 = two(A(11264, 1024))
            CB = [A(12288, 1024).rearrange("p (g s) -> p g s", g=4),
                  A(13312, 1024).rearrange("p (g s) -> p g s", g=4)]
            TM = A(14336, 1024)
            HID = A(15360, 128)
            KZC = A(15488, 256).rearrange("p (g h s) -> p g h s", g=4, h=2)
            VBD = A(15744, 256).rearrange("p (g c) -> p g c", g=4)
            GT = two(A(16000, 96))
            KC = A(16096, 64)
            KC2 = A(16160, 512)

            for nh in range(2):
                i, (wv,), mk = load(cols_tile(w_in, nh * 512, nh * 512 + 512))
                for tt in range(2):
                    k, bank, o = by_tokens(wv, 0, 512, tt, xc, mk)
                    rd, q_op = rope(bank.rearrange("p (h c) -> p h c", h=8),
                                    Q[:, tt, nh * 512:nh * 512 + 512].rearrange("p (h c) -> p h c", h=8),
                                    8, C2("cos")[:, tt, :], C2("sin")[:, tt, :], TM[:, 0:512], o)
                    B4.give(k, rd)
                done(i, o)
            qt_op = to_cols(lambda tt, k: Q[:, tt, k * P:(k + 1) * P],
                            lambda k0, nb, tt: qT[:, k0:k0 + nb, tt * P:(tt + 1) * P], 8, q_op)
            i, (wv,), mk = load(cols_tile(w_in, 1024, 1536))
            for kind in range(2):
                for gp in range(2):
                    b, bank, fr = B4.take()

                    def go(e, kind=kind, gp=gp, wv=wv, bank=bank):
                        for h in range(2):
                            c0 = kind * 256 + (gp * 2 + h) * 64
                            for half in range(2):
                                for k in range(KB):
                                    ins = e.matmul(
                                        bank[64 * half:64 * half + 64, h * S:(h + 1) * S],
                                        lhsT=wv[:, k, c0:c0 + 64], rhs=XT[:, k, :],
                                        start=k == 0, stop=k == KB - 1)
                        return ins
                    o = q.pe(go, xc, mk, fr)
                    pv = bank.rearrange("p (g s) -> p g s", g=2)
                    cbv = CB[kind][:, gp * 2:gp * 2 + 2, :]
                    q.v(lambda e, cbv=cbv, pv=pv: e.tensor_copy(cbv[0:64], pv[0:64]), o)
                    cb_op = q.v(lambda e, cbv=cbv, pv=pv: e.tensor_copy(
                        cbv[64:128, :, 0:S - 1], pv[64:128, :, 1:S]))
                    B4.give(b, cb_op)
            done(i, o)
            for kind, (a, b_) in enumerate(((1536, 2048), (2048, 2608))):
                i, (wv,), mk = load(cols_tile(w_in, a, b_))
                for tt in range(2):
                    k, bank, o = by_tokens(wv, 0, 512, tt, xc, mk)
                    rd, k_op = rope(bank[:, 0:256].rearrange("p (h c) -> p h c", h=4),
                                    KR[kind][:, tt, :].rearrange("p (h c) -> p h c", h=4), 4,
                                    C2("cos")[:, tt, :], C2("sin")[:, tt, :], TM[:, 0:512], o)
                    v_op = q.v(lambda e, kind=kind, tt=tt, bank=bank: e.tensor_copy(
                        V[kind][:, tt, :], bank[:, 256:512]))
                    B4.give(k, v_op)
                if kind == 1:
                    for tt in range(2):
                        k, bank, o = by_tokens(wv, 512, 560, tt, xc, mk)
                        gt_op = q.a(lambda e, tt=tt, bank=bank: e.activation(
                            GT[:, tt, :], bank, ACT.Sigmoid), o)
                        B4.give(k, gt_op)
                done(i, o)
            for kind in range(2):
                q.v(lambda e, kind=kind: e.memset(KZ[kind], 0.0), qt_op)
                for tt in range(2):
                    b, bank, fr = B4.take()

                    def go(e, kind=kind, tt=tt, bank=bank):
                        for g in range(4):
                            src = KR[kind][:, tt, g * 64:g * 64 + 64]
                            ins = e.transpose(bank[0:64, g * P:(g + 1) * P], src, ident)
                        return ins
                    t = q.pe(go, k_op, fr)
                    pv = bank.rearrange("p (k s) -> p k s", k=4)
                    kz_op = q.v(lambda e, kind=kind, tt=tt, pv=pv: e.tensor_copy(
                        KZ[kind][0:64, :, 0, tt * P:(tt + 1) * P], pv[0:64]), t)
                    B4.give(b, kz_op)
            for kind in range(2):
                for tt in range(2):
                    b, bank, fr = B4.take()

                    def go(e, kind=kind, tt=tt, bank=bank):
                        for g in range(4):
                            ins = e.matmul(bank[64:128, g * P:(g + 1) * P],
                                           lhsT=KR[kind][:, tt, g * 64:g * 64 + 64], rhs=ident,
                                           start=True, stop=True)
                        return ins
                    t = q.pe(go, fr)
                    pv = bank.rearrange("p (k s) -> p k s", k=4)
                    kz_op = q.v(lambda e, kind=kind, tt=tt, pv=pv: e.tensor_copy(
                        KZ[kind][64:128, :, 1, tt * P:(tt + 1) * P], pv[64:128]), t)
                    B4.give(b, kz_op)
            q.v(lambda e: e.memset(HID, 0.0))
            q.v(lambda e: e.memset(KZC, 0.0))
            z_op = q.v(lambda e: e.memset(VBD, 0.0))
            for kind, (w1n, w2n, pen) in enumerate((("nsa_w1_k_2", "nsa_w2_k_2", "pek"),
                                                    ("nsa_w1_v_2", "nsa_w2_v_2", "pev"))):
                i, (w1, w2), mk = load(
                    (0, 2048, d[w1n][0].rearrange("(r p) n -> p r n", p=P),
                     lambda r: r.rearrange("p (r n) -> p r n", r=16)),
                    (2048, 64, d[w2n][0], lambda r: r))
                b, bank, fr = B4.take()
                pe_ = PR(pen)

                def go(e, kind=kind, w1=w1, bank=bank, pe_=pe_):
                    for r in range(16):
                        e.matmul(bank[:, 64:65], lhsT=w1[:, r, :], rhs=pe_[:, r:r + 1],
                                 start=r == 0, stop=r == 15)
                    for r in range(16):
                        ins = e.matmul(bank[:, 0:60].rearrange("p (g n) -> p g n", g=4),
                                       lhsT=w1[:, r, :], rhs=CB[kind][:, :, 2 * r:2 * r + 225:16],
                                       start=r == 0, stop=r == 15)
                    return ins
                o = q.pe(go, cb_op, mk, fr, m_p)
                pc = sm(1)
                q.v(lambda e, pc=pc, bank=bank: e.tensor_copy(pc, bank[:, 64:65]), o)
                hv = HID.rearrange("p (g n) -> p g n", g=4)[:, :, 0:15]
                o = q.v(lambda e, pc=pc, bank=bank, hv=hv: e.tensor_scalar(
                    hv, bank[:, 0:60].rearrange("p (g n) -> p g n", g=4), pc, None, ALU.add))
                B4.give(b, o)
                o = q.a(lambda e, hv=hv: e.activation(hv, hv, ACT.Silu), o)
                b, bank, fr = B4.take()
                o = mms(b, bank[:, 0:64], [(HID, w2)], o, fr, mk)
                done(i, o)
                if kind == 0:
                    rd, o = rope(bank[:, 0:64].rearrange("p (h c) -> p h c", h=1),
                                 KC.rearrange("p (h c) -> p h c", h=1), 1,
                                 C("cos_c"), C("sin_c"), TM[:, 0:512], o)
                    B4.give(b, rd)
                    q.v(lambda e: e.memset(KC2, 0.0))
                    q.v(lambda e: e.tensor_copy(KC2[:, 0:64], KC))
                    o = q.v(lambda e: e.tensor_copy(KC2[:, 128 + 64:256], KC))
                    b, bank, fr = B4.take()

                    def tr(e, bank=bank):
                        for h in range(2):
                            ins = e.transpose(bank[:, h * P:(h + 1) * P], KC2[:, h * P:(h + 1) * P],
                                              ident)
                        return ins
                    t = q.pe(tr, o, fr)
                    kc_op = q.v(lambda e, bank=bank: e.tensor_copy(
                        KZC, bank[:, 0:256].rearrange("p (h g n) -> p g h n", h=2, g=4)), t)
                    B4.give(b, kc_op)
                else:
                    for g in range(4):
                        vc_op = q.v(lambda e, g=g, bank=bank: e.tensor_copy(
                            VBD[32 * g:32 * g + 32, g, :], bank[32 * g:32 * g + 32, 0:64]), o)
                    B4.give(b, vc_op)
            wp_free = None
            for qt in range(2):
                b, bank, fr = B4.take()

                def sc(e, qt=qt, bank=bank):
                    for blk in range(8):
                        ins = e.matmul(bank[:, blk * 64:blk * 64 + 64],
                                       lhsT=qT[:, blk, qt * P:(qt + 1) * P],
                                       rhs=KZC[:, blk // 2, :, :], start=True, stop=True)
                    return ins
                o = q.pe(sc, kc_op, fr)
                W = W2[:, qt, :]
                rd, o, l = softmax_block(bank, 32, 16, C2("mask_c")[:, qt, :], None, 0.125, W, None, o)
                B4.give(b, rd)
                gl = sm(16)
                q.v(lambda e, l=l: e.reciprocal(l, l))
                gl_op = q.v(lambda e, l=l, gl=gl, qt=qt: e.scalar_tensor_tensor(
                    gl, l, C2("any_c")[:, qt, :],
                    GT[:, qt, :].rearrange("p (h b) -> p h b", b=3)[:, :, 0],
                    ALU.mult, ALU.mult), gt_op)
                wp = TM[:, 512:1024]
                o = q.v(lambda e, W=W, wp=wp: e.tensor_copy(
                    wp.rearrange("p (x g n) -> p g x n", x=4, g=4),
                    W.rearrange("p (g x n) -> p g x n", g=4, x=4)), wp_free)
                t, c = transposed_block([wp[:, x * P:(x + 1) * P] for x in range(4)],
                                        PT2[:, qt, :], o, None)
                wp_free = t
                for xp in range(2):
                    b, bank, fr = B4.take()

                    def pv_(e, xp=xp, bank=bank, qt=qt):
                        for x in range(2):
                            ins = e.matmul(bank[:, x * 256:x * 256 + 256],
                                           lhsT=PT2[:, qt, (xp * 2 + x) * P:(xp * 2 + x + 1) * P],
                                           rhs=VBD, start=True, stop=True)
                        return ins
                    o = q.pe(pv_, c, vc_op, fr)
                    for x in range(2):
                        yv = Y[:, qt, :].rearrange("p (g x c) -> p g x c", g=4, x=4)[:, :, xp * 2 + x, :]
                        glv = gl.rearrange("p (g x) -> p g x", g=4)[:, :, xp * 2 + x]
                        y_op = q.v(lambda e, yv=yv, glv=glv, bank=bank, x=x: e.tensor_tensor(
                            yv, bank[:, x * 256:x * 256 + 256].rearrange("p (g c) -> p g c", g=4),
                            bc3(glv, 64), ALU.mult), o)
                    B4.give(b, y_op)
            for kind in range(2):
                res = attention(8, qT, lambda b, kind=kind: KZ[kind][:, b // 2, :, :],
                                lambda i, h, kind=kind: V[kind][:, i, (h // 4) * 64:(h // 4) * 64 + 64],
                                C2("mask_f"), None, True, W2, PT2, [BA[0:2], BA[2:4]],
                                kz_op if kind == 0 else y_op)
                for qt in range(2):
                    L, last = res[qt]
                    q.v(lambda e, L=L: e.reciprocal(L, L))
                    q.v(lambda e, L=L, qt=qt, kind=kind: e.tensor_tensor(
                        L, L, GT[:, qt, :].rearrange("p (h b) -> p h b", b=3)[:, :, 1 + kind],
                        ALU.mult))
                    for hb in range(2):
                        ob = BA[qt * 2 + hb]
                        tm = TM[:, 0:512].rearrange("p (h c) -> p h c", h=8)
                        r = q.v(lambda e, L=L, ob=ob, hb=hb, tm=tm: e.tensor_tensor(
                            tm, psum[:, ob, :].rearrange("p (h c) -> p h c", h=8),
                            bc3(L[:, hb * 8:hb * 8 + 8], 64), ALU.mult), last)
                        acc_free[ob] = r
                        y_op = q.v(lambda e, qt=qt, hb=hb: e.tensor_tensor(
                            Y[:, qt, hb * 512:hb * 512 + 512], Y[:, qt, hb * 512:hb * 512 + 512],
                            TM[:, 0:512], ALU.add))
            yt = to_cols(lambda tt, k: Y[:, tt, k * P:(k + 1) * P], xt_dst, KB, y_op)
            xo = project_out(d["nsa_w_out_2"][0], yt, ALPHA)
            return layer_norm(1, 0, xo)

        A_ = lambda a, n: AR[:, a:a + n]
        YA = A_(0, 2048).rearrange("p (t n) -> p t n", t=2)
        RT = A_(2048, 2 * 8 * 8).rearrange("p (t n) -> p t n", t=2)
        RW = A_(2304, 512)
        SEL = A_(2816, 16).rearrange("p (t n) -> p t n", t=2)
        CMB = A_(2832, 16).rearrange("p (t n) -> p t n", t=2)
        POS = A_(2848, 16).rearrange("p (t n) -> p t n", t=2)
        LG = A_(2864, 16).rearrange("p (t n) -> p t n", t=2)
        EQ = A_(2880, 128)
        EQ2 = A_(3008, 128)
        RK = A_(3136, 16).rearrange("p (t n) -> p t n", t=2)
        SM_ = A_(3200, 2 * 512).rearrange("p (b t n) -> p b t n", b=2, t=2)[:, :, :, 0:P]
        SW_ = A_(4224, 2 * 256).rearrange("p (b t n) -> p b t n", b=2, t=2)
        ST_ = A_(4736, 2 * 256).rearrange("p (b n) -> p b n", b=2)
        XG = A_(5248, 2 * 1024).rearrange("p (b k n) -> p b k n", b=2, k=8)
        GS = A_(7296, 2 * 512).rearrange("p (b n) -> p b n", b=2)
        HH = A_(8320, 2 * 512).rearrange("p (b n) -> p b n", b=2)
        HT = A_(9344, 2 * 512).rearrange("p (b n) -> p b n", b=2)
        YE = A_(10368, 1024)

        def route(ready):
            xc = x_cols(ready)
            i, (rw,), mk = load((0, 64, d["moe_router_2"][0].rearrange("(k p) n -> p k n", p=P),
                                 lambda r: r.rearrange("p (k n) -> p k n", k=KB)))
            for tt in range(2):
                k, bank, o = by_tokens(rw, 0, 8, tt, xc, mk)
                r = q.v(lambda e, tt=tt, bank=bank: e.tensor_copy(LG[:, tt, :], bank), o)
                B4.give(k, r)
            done(i, o)
            idx = C("iota")[:, 0:8]
            for tt in range(2):
                lg = LG[:, tt, :]
                a = bc3(lg, 8, 1)
                b = bc3(lg, 8, 2)
                m = EQ[:, 0:64].rearrange("p (a b) -> p a b", a=8)
                m2 = EQ2[:, 0:64].rearrange("p (a b) -> p a b", a=8)
                m3 = EQ2[:, 64:128].rearrange("p (a b) -> p a b", a=8)
                q.v(lambda e, a=a, b=b, m=m: e.tensor_tensor(m, a, b, ALU.is_gt))
                q.v(lambda e, a=a, b=b, m2=m2: e.tensor_tensor(m2, a, b, ALU.is_equal))
                q.v(lambda e, m3=m3: e.tensor_tensor(m3, bc3(idx, 8, 1), bc3(idx, 8, 2), ALU.is_lt))
                q.v(lambda e, m2=m2, m3=m3: e.tensor_tensor(m2, m2, m3, ALU.mult))
                q.v(lambda e, m=m, m2=m2: e.tensor_tensor(m, m, m2, ALU.add))
                q.v(lambda e, m=m, tt=tt: e.tensor_reduce(RK[:, tt, :], m, AX.X, ALU.add))
                q.v(lambda e, tt=tt: e.tensor_scalar(SEL[:, tt, :], RK[:, tt, :], 1.5, None, ALU.is_lt))
                mx, s = sm(1), sm(1)
                q.v(lambda e, lg=lg, mx=mx: e.tensor_reduce(mx, lg, AX.X, ALU.max))
                o = q.v(lambda e, lg=lg, mx=mx, tt=tt: e.tensor_scalar(
                    CMB[:, tt, :], lg, mx, None, ALU.subtract))
                o = q.a(lambda e, tt=tt: e.activation(CMB[:, tt, :], CMB[:, tt, :], ACT.Exp), o)
                q.v(lambda e, tt=tt: e.tensor_tensor(CMB[:, tt, :], CMB[:, tt, :], SEL[:, tt, :],
                                                     ALU.mult), o)
                q.v(lambda e, tt=tt, s=s: e.tensor_reduce(s, CMB[:, tt, :], AX.X, ALU.add))
                q.v(lambda e, s=s: e.reciprocal(s, s))
                o = q.v(lambda e, tt=tt, s=s: e.tensor_scalar(CMB[:, tt, :], CMB[:, tt, :], s, None,
                                                              ALU.mult))
            k, bank, fr = B4.take()

            def cum(e, bank=bank):
                e.matmul(bank[:, 0:8], lhsT=C("strict"), rhs=SEL[:, 0, :], start=True, stop=True)
                e.matmul(bank[:, 8:16], lhsT=C("ones"), rhs=SEL[:, 0, :], start=True, stop=False)
                e.matmul(bank[:, 8:16], lhsT=C("strict"), rhs=SEL[:, 1, :], start=False, stop=True)
                e.matmul(bank[:, 16:24], lhsT=C("ones"), rhs=SEL[:, 0, :], start=True, stop=False)
                return e.matmul(bank[:, 16:24], lhsT=C("ones"), rhs=SEL[:, 1, :], start=False,
                                stop=True)
            o = q.pe(cum, o, fr)
            q.v(lambda e, bank=bank: e.tensor_copy(
                POS, bank[:, 0:16].rearrange("p (t n) -> p t n", t=2)), o)
            mx = sm(1)
            r = q.v(lambda e, bank=bank, mx=mx: e.tensor_reduce(mx, bank[:, 16:24], AX.X, ALU.max))
            B4.give(k, r)
            f_op = q.v(lambda e, mx=mx: e.tensor_scalar(
                flag[0:1, :], mx[0:1, :], P + 0.5, None, ALU.is_gt))
            q.v(lambda e: e.memset(YA, 0.0))
            return xc, f_op

        def experts(chunk, ready):
            wgu, wd = d["moe_w_gu_2"][0], d["moe_w_down_2"][0]
            iota = C("iota")[:, chunk * P:chunk * P + P]
            gather = {}
            gsf, htf, stf = [None, None], [None, None], [None, None]
            xgf = [None, None]

            def prepare(e_):
                eb = e_ % 2
                for tt in range(2):
                    q.v(lambda e, tt=tt: e.tensor_scalar(
                        SM_[:, eb, tt, :], iota, POS[:, tt, e_:e_ + 1], SEL[:, tt, e_:e_ + 1],
                        ALU.is_equal, ALU.mult), ready, xgf[eb])
                    s_op = q.v(lambda e, tt=tt: e.tensor_scalar(
                        SW_[:, eb, tt, :], SM_[:, eb, tt, :], CMB[:, tt, e_:e_ + 1], None, ALU.mult))
                b, bank, fr = B4.take()

                def tr(e, bank=bank):
                    for tt in range(2):
                        ins = e.transpose(bank[:, tt * P:(tt + 1) * P], SW_[:, eb, tt, :], ident)
                    return ins
                t = q.pe(tr, s_op, fr)
                st_op = q.v(lambda e, bank=bank: e.tensor_copy(ST_[:, eb, :], bank[:, 0:256]), t, stf[eb])
                B4.give(b, st_op)
                for k0 in range(0, 8, 4):
                    b, bank, fr = B4.take()

                    def go(e, k0=k0, bank=bank):
                        for j in range(4):
                            for tt in range(2):
                                ins = e.matmul(bank[:, j * P:(j + 1) * P],
                                               lhsT=X[:, tt, (k0 + j) * P:(k0 + j + 1) * P],
                                               rhs=SM_[:, eb, tt, :], start=tt == 0, stop=tt == 1)
                        return ins
                    o = q.pe(go, s_op, fr)
                    xgf_old = xgf[eb]
                    g_op = q.v(lambda e, k0=k0, bank=bank: e.tensor_copy(
                        XG[:, eb, k0:k0 + 4, :], bank.rearrange("p (k s) -> p k s", k=4)), o, xgf_old)
                    B4.give(b, g_op)
                gather[e_] = (st_op, g_op)

            n = [0]

            def up(e_, c):
                eb = e_ % 2
                cb = n[0] % 2
                n[0] += 1
                g_op = gather[e_][1]
                banks = []
                for part in range(2):
                    a = part * FE + c * 512
                    i, (wv,), mk = load(cols_tile(wgu[e_], a, a + 512))
                    b, bank, fr = B4.take()
                    o = mms(b, bank, [(XG[:, eb, j, :], wv[:, j, :]) for j in range(KB)],
                            g_op, mk, fr)
                    done(i, o)
                    banks.append((b, bank, o))
                (b0, g, o0), (b1, u, o1) = banks
                s = q.a(lambda e: e.activation(GS[:, cb, :], g, ACT.Silu), o0, gsf[cb])
                B4.give(b0, s)
                h = q.v(lambda e: e.tensor_tensor(HH[:, cb, :], GS[:, cb, :], u, ALU.mult), s, o1)
                gsf[cb] = h
                B4.give(b1, h)
                xgf[eb] = o1
                return e_, c, cb, h

            def down(e_, c, cb, h):
                b, bank, fr = B4.take()

                def tr(e):
                    for j in range(4):
                        ins = e.transpose(bank[:, j * P:(j + 1) * P], HH[:, cb, j * P:(j + 1) * P],
                                          ident)
                    return ins
                t = q.pe(tr, h, fr)
                cp = q.a(lambda e: e.activation(HT[:, cb, :], bank, ACT.Copy), t, htf[cb])
                B4.give(b, cp)
                return lambda: down2(e_, c, cb, cp)

            def down2(e_, c, cb, cp):
                i, (wv,), mk = load(rows_tile(wd[e_], c * 512, 4))
                for nh in range(2):
                    ab = BA[(e_ % 2) * 2 + nh]
                    o = mms(ab, psum[:, ab, :], [(HT[:, cb, j * P:(j + 1) * P],
                                                  wv[:, j, nh * 512:nh * 512 + 512])
                                                 for j in range(4)], cp, mk, acc_free[ab],
                            start=c == 0, stop=c == FE // 512 - 1)
                htf[cb] = o
                done(i, o)
                return o

            def combine(e_, last):
                eb = e_ % 2
                for nh in range(2):
                    ab = BA[eb * 2 + nh]
                    ye = q.a(lambda e, nh=nh, ab=ab: e.activation(
                        YE[:, nh * 512:nh * 512 + 512], psum[:, ab, :], ACT.Copy), last, yef[0])
                    acc_free[ab] = ye
                def later():
                    for tt in range(2):
                        for nh in range(2):
                            b, bank, fr = B4.take()
                            o = mms(b, bank, [(ST_[:, eb, tt * P:(tt + 1) * P],
                                               YE[:, nh * 512:nh * 512 + 512])], ye, gather[e_][0], fr)
                            y = YA[:, tt, nh * 512:nh * 512 + 512]
                            r = q.v(lambda e, y=y, bank=bank: e.tensor_tensor(y, y, bank, ALU.add), o)
                            B4.give(b, r)
                    stf[eb] = o
                    yef[0] = o
                    return r
                return later

            yef = [None]
            prepare(0)
            prev = None
            tail = None
            for e_ in range(N_EXP):
                for c in range(FE // 512):
                    cur = up(e_, c)
                    if prev is not None:
                        fin = down(*prev)
                    if tail is not None:
                        tail()
                        tail = None
                    if c == 1 and e_ + 1 < N_EXP:
                        prepare(e_ + 1)
                    if prev is not None:
                        last = fin()
                        if prev[1] == FE // 512 - 1:
                            tail = combine(prev[0], last)
                    prev = cur
            last = down(*prev)()
            return combine(N_EXP - 1, last)()

        op = hybrid(0, m_x)
        op = hybrid(1, op)
        op = final_rms(op)
        op = pool_layer(op)
        op = nsa(op)
        xc, f_op = route(op)
        f_op.used = True
        op = experts(0, f_op)
        join = [Mark(None, 0)]
        q.part = "over"
        over[0] = True
        start_over = op
        op = experts(1, op)
        q.part = "post"
        over[0] = False
        for i in range(NSLOT):
            slot_free[i] = None
        for b in range(8):
            B4.free.pop(b, None)
            acc_free[b] = None
        for tt in range(2):
            op = q.v(lambda e, tt=tt: e.scalar_tensor_tensor(
                X[:, tt, :], X[:, tt, :], ALPHA, YA[:, tt, :], ALU.mult, ALU.add), start_over)
        op = layer_norm(1, 1, op)
        q.dma("sync", s_out, out.rearrange("b (t p) n -> p (b t) n", p=P), X, op)

        q.number()
        main_end = {e: q.q[("main", e)][-1] for e in q.ENGINES if ("main", e) in q.q}
        block = ctx.enter_context(nc.Block())

        def run(eng, e):
            seen = {}
            q.emit(e, eng, "main", seen)
            e.wait_ge(f_op.sem, f_op.value)
            val = e.value_load(flag[0:1, 0:1])
            with e.If(val > 0):
                inner = dict(seen)
                for (part, _), m in q.total.items():
                    if part == "main":
                        e.wait_ge(m.sem, m.value)
                        inner[m.sem] = m.value
                q.emit(e, eng, "over", inner)
                for (part, _), m in q.total.items():
                    if part == "over":
                        e.wait_ge(m.sem, m.value)
            q.emit(e, eng, "post", seen)
            if eng == "sync":
                e.wait_ge(s_out, 16)

        @block.sync
        def _(e):
            run("sync", e)

        @block.tensor
        def _(e):
            run("tensor", e)

        @block.vector
        def _(e):
            run("vector", e)

        @block.scalar
        def _(e):
            run("scalar", e)

        @block.gpsimd
        def _(e):
            run("gpsimd", e)


def arrange(inputs):
    at, cons, pool = constants()
    a = {k: np.ascontiguousarray(np.asarray(v)) for k, v in inputs.items()}

    def cols(x, n):
        return np.ascontiguousarray(x.reshape(2, KB, P).transpose(2, 0, 1).reshape(P, n))

    arrays = {k: a[k] for k in (
        "x", "w_in", "head_norm_g", "w_out", "w_up", "w_down", "final_g", "ln_g_2", "ln_b_2",
        "pool_w_2", "pool_scale_2", "nsa_w_in_2", "nsa_w1_k_2", "nsa_w2_k_2", "nsa_w1_v_2",
        "nsa_w2_v_2", "nsa_w_out_2", "ffn_w_gu_2", "ffn_w_down_2", "moe_router_2", "moe_w_gu_2",
        "moe_w_down_2")}
    arrays["n1g"] = cols(a["norm1_g"], 16)
    arrays["n2g"] = cols(a["norm2_g"], 16)
    arrays["cw"] = np.ascontiguousarray(
        a["conv_w"].reshape(2, 5, KB, P).transpose(3, 0, 2, 1).reshape(P, 80))
    for new, old in (("pek", "nsa_pe_k_2"), ("pev", "nsa_pe_v_2")):
        arrays[new] = np.ascontiguousarray(a[old].reshape(16, P).T)
    arrays["gib"] = a["gate_i_b"].reshape(16)
    arrays["gfb"] = a["gate_f_b"].reshape(16)
    arrays["cons"] = cons
    arrays["poolm"] = pool
    return arrays, (at, cons.shape[1], pool.shape[1])


def kernel(**inputs):
    import concourse.bacc as bacc
    from concourse.bass_utils import run_bass_kernel_spmd

    nc = bacc.Bacc("TRN2", target_bir_lowering=False, num_devices=1)
    arrays, tables = arrange(inputs)
    d = {n: nc.dram_tensor(f"in_{n}", v.shape, mybir.dt.from_np(v.dtype), kind="ExternalInput").ap()
         for n, v in arrays.items()}
    out = nc.dram_tensor("out_0", (1, S, D), F32, kind="ExternalOutput").ap()
    build(nc, d, out, tables)
    r = run_bass_kernel_spmd(nc, [{f"in_{n}": v for n, v in arrays.items()}], core_ids=[0])
    return r.results[0]["out_0"]
```

```python
import math
from contextlib import ExitStack

import numpy as np
import concourse.bass as bass
from concourse import mybir

F32 = mybir.dt.float32
F32R = mybir.dt.float32r
I32 = mybir.dt.int32
ALU = mybir.AluOpType
ACT = mybir.ActivationFunctionType
AX = mybir.AxisListType

P = 128
S = 256
D = 1024
KB = D // P
UNIT = 2048
NSLOT = 4
NHL = 3
NEG = -1.0e30
ALPHA = (2 * 2) ** 0.25
N_EXP = 8
FE = 3584
FF2 = 2816


def constants():
    parts, at = [], {}
    n = 0

    def add(name, a):
        nonlocal n
        a = np.asarray(a, np.float32).reshape(P, -1)
        at[name] = (n, a.shape[1])
        parts.append(a)
        n += a.shape[1]

    i = np.arange(P)
    add("ident", np.eye(P))
    add("ones", np.ones((P, P)))
    add("upper", (i[:, None] <= i[None, :]))
    add("lower", (i[:, None] >= i[None, :]))
    add("strict", (i[:, None] < i[None, :]))
    add("iota", np.tile(np.arange(S), (P, 1)))
    t = np.arange(S)
    d = np.abs(t[:, None] - t[None, :])
    cnt = (d <= 64).astype(np.float32) + (d % 4 == 0) + (d % 16 == 0)
    tok = lambda a: np.asarray(a, np.float32).reshape(2, P, -1).transpose(1, 0, 2)
    add("mask_a", tok(np.where(cnt > 0, np.log(np.maximum(cnt, 1)), NEG)))
    add("mask_f", tok(np.where(t[None, :] <= t[:, None], 0.0, NEG)))
    add("mask_b", tok(np.where(t[None, :] >= t[:, None], 0.0, NEG)))
    nn = np.arange(32)
    cend = 16 * nn + 31
    ok = (cend[None, :] <= t[:, None]) & (nn[None, :] < 15)
    add("mask_c", tok(np.where(ok, 0.0, NEG)))
    add("any_c", tok(ok.any(axis=1)))
    inv = (np.float32(10000.0) ** (-np.arange(32, dtype=np.float32) / np.float32(32))).astype(np.float32)
    ang = (t.astype(np.float32)[:, None] * inv[None, :]).astype(np.float32)
    add("cos", tok(np.cos(ang)))
    add("sin", tok(np.sin(ang)))
    angc = (np.tile(cend, 4).astype(np.float32)[:, None] * inv[None, :]).astype(np.float32)
    add("cos_c", np.cos(angc))
    add("sin_c", np.sin(angc))
    pool = np.zeros((P, 2, 4, S), np.float32)
    for g, w in enumerate((2, 4, 8, 16)):
        m = np.zeros((S, S), np.float32)
        for q in range(S):
            lo = max(q + 1 - w, 0)
            m[lo:q + 1, q] = np.float32(1.0) / np.float32(min(q + 1, w))
            m[q, q] -= 1.0
        pool[:, :, g, :] = m.reshape(2, P, S).transpose(1, 0, 2)
    return at, np.concatenate(parts, axis=1), pool.reshape(P, -1)


class Op:

    def __init__(self, eng, fn, waits, part):
        self.eng, self.fn, self.waits, self.part = eng, fn, waits, part
        self.used = self.own = False
        self.extra = 0
        self.unit = None
        self.sem = self.value = None


class Mark:

    def __init__(self, sem, value):
        self.sem, self.value = sem, value


class End:

    def __init__(self, part, eng):
        self.part, self.eng = part, eng
        self.sem = self.value = None


class Queues:

    def __init__(self, nc, sems):
        self.nc, self.sems = nc, sems
        self.parts = ["first"]
        self.part = "first"
        self.q = {}
        self.last = {}
        self.dcount = {}
        self.ends = []

    def enter(self, part):
        self.part = part
        self.parts.append(part)
        self.last = {}

    def end(self, name, eng):
        m = End(name, eng)
        self.ends.append(m)
        return m

    def add(self, eng, fn, waits, chain, own=None):
        ws = []
        for w in waits:
            ws += list(w) if isinstance(w, (list, tuple)) else [w]
        ws = [w for w in ws if w is not None]
        prev = self.last.get(eng)
        if chain and prev is not None:
            ws.append(prev)
        for w in ws:
            if isinstance(w, Op):
                w.used = True
        op = Op(eng, fn, ws, self.part)
        if own is not None:
            op.sem, op.value, op.own = own[0], own[1], True
        self.q.setdefault((self.part, eng), []).append(op)
        if chain:
            self.last[eng] = op
        return op

    def pe(self, fn, *w, own=None):
        return self.add("tensor", fn, w, False, own)

    def v(self, fn, *w):
        return self.add("vector", fn, w, True)

    def a(self, fn, *w):
        return self.add("scalar", fn, w, True)

    def dma(self, eng, sem, out, in_, *w):
        n = self.dcount[sem] = self.dcount.get(sem, 0) + 16
        self.add(eng, lambda e: e.dma_start(out, in_).then_inc(sem, 16), w, False)
        return Mark(sem, n)

    def number(self):
        count = {}
        after = {}
        for part in self.parts:
            side = part[1] if isinstance(part, tuple) else None
            if side is None or side == 0:
                base = dict(count)
            ends = {}
            for eng in ("tensor", "vector", "scalar"):
                n = base.get(eng, 0)
                ops = [o for o in self.q.get((part, eng), []) if not o.own]
                if side is not None:
                    ops[-1].used = True
                for op in ops:
                    if op.used:
                        n += 1
                        op.sem, op.value = self.sems[eng], n
                ends[eng] = n
                if side is not None:
                    after[(part, eng)] = (ops[-1], n)
            if side == 1:
                for eng in ends:
                    hi = max(ends[eng], first_ends[eng])
                    for p in ((part[0], 0), part):
                        op, n = after[(p, eng)]
                        op.extra = hi - n
                    ends[eng] = hi
            elif side == 0:
                first_ends = dict(ends)
            count = ends
            for m in self.ends:
                if m.part == (part[0] if side is not None else part):
                    m.sem, m.value = self.sems[m.eng], count.get(m.eng, 0)

    def emit(self, e, eng, part, seen):
        for op in self.q.get((part, eng), []):
            if op.unit is not None and op.unit >= self.n_units:
                continue
            need = {}
            for w in op.waits:
                if seen.get(w.sem, 0) < w.value:
                    need[w.sem] = max(need.get(w.sem, 0), w.value)
            for sem, value in need.items():
                e.wait_ge(sem, value)
                seen[sem] = value
            ins = op.fn(e)
            if ins is not None and (op.used or op.own):
                ins.then_inc(op.sem, 1 + op.extra)


class Banks:

    def __init__(self, psum, numbers):
        self.psum, self.numbers, self.n = psum, numbers, 0
        self.free = {}

    def take(self):
        b = self.numbers[self.n % len(self.numbers)]
        self.n += 1
        return b, self.psum[:, b, :], self.free.get(b)

    def give(self, b, *ops):
        self.free[b] = ops[-1]


def build(nc, d, out, tables):
    at, cons_cols, pool_cols = tables
    with ExitStack() as ctx:
        def sem(name):
            return ctx.enter_context(nc.semaphore(name))

        def sb(name, cols, dt=F32, rows=P):
            return ctx.enter_context(nc.sbuf_tensor(name, [rows, cols], dt))

        q = Queues(nc, {e: sem(f"s_{e}") for e in ("tensor", "vector", "scalar")})
        psum = ctx.enter_context(nc.psum_tensor("psum", [P, 8, 512], F32))
        ring = sb("ring", NSLOT * UNIT)
        HI = sb("HI", NHL * UNIT, F32R)
        LO = sb("LO", NHL * UNIT, F32R)
        cons = sb("cons", cons_cols)
        par = sb("par", 240)
        bcs = sb("bcs", 2 * D)
        X = sb("X", 2 * D)[:].rearrange("p (t n) -> p t n", t=2)
        XTH = sb("XTH", KB * S, F32R)[:].rearrange("p (k s) -> p k s", k=KB)
        XTL = sb("XTL", KB * S, F32R)[:].rearrange("p (k s) -> p k s", k=KB)
        HTH = sb("HTH", 8 * S, F32R)[:].rearrange("p (b j s) -> p b j s", b=2, j=4)
        HTL = sb("HTL", 8 * S, F32R)[:].rearrange("p (b j s) -> p b j s", b=2, j=4)
        SML = sb("SML", 512)
        AR = sb("AR", 16416)
        flag = sb("flag", N_EXP, I32)

        s_ring = [sem(f"s_ring{i}") for i in range(NSLOT)]
        s_bc = [sem(f"s_bc{i}") for i in range(2)]
        s_x, s_c, s_p, s_out = sem("s_x"), sem("s_c"), sem("s_p"), sem("s_out")
        s_hi, s_lo, s_use = sem("s_hi"), sem("s_lo"), sem("s_use")

        def C(name, rows=P):
            a, n = at[name]
            return cons[0:rows, a:a + n]

        def C2(name):
            return C(name).rearrange("p (t n) -> p t n", t=2)

        ident = C("ident")

        small = [0]

        def sm(n):
            a = small[0]
            if a + n > 512:
                a = 0
            small[0] = a + n
            return SML[:, a:a + n]

        units = []
        unit_n = [0]
        AHEAD = 2

        def split(u):
            def sizes():
                src, k, n = units[u]
                return k * n

            def hi(e):
                if u >= len(units):
                    return None
                n = sizes()
                r, h = (u % NSLOT) * UNIT, (u % NHL) * UNIT
                return e.activation(HI[:, h:h + n], ring[:, r:r + n], ACT.Copy)

            def lo(e):
                if u >= len(units):
                    return None
                n = sizes()
                r, h = (u % NSLOT) * UNIT, (u % NHL) * UNIT
                return e.tensor_tensor(LO[:, h:h + n], ring[:, r:r + n],
                                       HI[:, h:h + n].bitcast(F32), ALU.subtract)

            loaded = Mark(s_ring[u % NSLOT], 16 * (u // NSLOT + 1))
            used = Mark(s_use, u - NHL + 1)
            q.add("scalar", hi, (loaded, used), False, own=(s_hi, u + 1)).unit = u
            q.add("vector", lo, (Mark(s_hi, u + 1),), False, own=(s_lo, u + 1)).unit = u

        def unit(src, k, n):
            u = unit_n[0]
            unit_n[0] += 1
            if u == len(units):
                units.append((src, k, n))
            if u == 0:
                for v in range(AHEAD):
                    split(v)
            split(u + AHEAD)
            h = (u % NHL) * UNIT
            view = lambda t: t[:, h:h + k * n].rearrange("p (k n) -> p k n", k=k)
            return view(HI), view(LO), Mark(s_lo, u + 1), (s_use, u + 1)

        def group3(out_ap, trios, start, stop):
            def go(e):
                n, m = 0, 3 * len(trios)
                for lh, ll, rh, rl in trios:
                    for a, b in ((lh, rh), (lh, rl), (ll, rh)):
                        ins = e.matmul(out_ap, lhsT=a, rhs=b, start=start and n == 0,
                                       stop=stop and n == m - 1)
                        n += 1
                return ins
            return go

        def gemm_cols(w, a, b, nt, ready):
            n = b - a
            kk = 4 if n > 256 else 8
            banks = [B4.take() for _ in range(nt)]
            ops = []
            for k0 in range(0, KB, kk):
                hv, lv, mk, own = unit(
                    w[k0 * P:(k0 + kk) * P, a:b].rearrange("(k p) n -> p k n", p=P), kk, n)
                ops = []
                for t in range(nt):
                    _, bank, fr = banks[t]
                    ts = slice(t * P, t * P + P)
                    ops.append(q.pe(group3(bank[:, 0:n], [
                        (XTH[:, k0 + k, ts], XTL[:, k0 + k, ts], hv[:, k, :], lv[:, k, :])
                        for k in range(kk)], k0 == 0, k0 + kk == KB),
                        ready, mk, fr if k0 == 0 else None, own=own if t == nt - 1 else None))
            return [(bk[0], bk[1][:, 0:n], o) for bk, o in zip(banks, ops)]

        def gemm_rows(w, a, kb, hb, nt, acc, start, stop, ready):
            for k0 in range(0, kb, 2):
                hv, lv, mk, own = unit(
                    w[a + k0 * P:a + (k0 + 2) * P, :].rearrange("(k p) n -> p k n", p=P), 2, D)
                for t in range(nt):
                    ts = slice(t * P, t * P + P)
                    for nh in range(2):
                        bk = acc[t * 2 + nh]
                        ns = slice(nh * 512, nh * 512 + 512)
                        first = start and k0 == 0
                        o = q.pe(group3(psum[:, bk, :], [
                            (HTH[:, hb, k0 + k, ts], HTL[:, hb, k0 + k, ts], hv[:, k, ns],
                             lv[:, k, ns]) for k in range(2)], first, stop and k0 + 2 == kb),
                            ready, mk, acc_free[bk] if first else None,
                            own=own if (t, nh) == (nt - 1, 1) else None)
            return o

        bc_n = [0]
        bc_free = [None] * 2

        def bcast(src, n):
            i = bc_n[0] % 2
            bc_n[0] += 1
            dst = bcs[:, i * D:i * D + n]
            mark = q.dma("gpsimd", s_bc[i], dst, src.partition_broadcast(P), bc_free[i])
            return i, dst, mark

        def bdone(i, op):
            bc_free[i] = op

        m_x = q.dma("sync", s_x, X, d["x"][0].rearrange("(t p) n -> p t n", p=P))
        m_c = q.dma("gpsimd", s_c, cons[:], d["cons"])
        m_p = None
        pat = {}
        n = 0
        for name in ("n1g", "n2g", "cw", "pek", "pev"):
            w = d[name].shape[1]
            m_p = q.dma("gpsimd", s_p, par[:, n:n + w], d[name])
            pat[name] = (n, w)
            n += w
        for name in ("gib", "gfb"):
            m_p = q.dma("gpsimd", s_p, par[:, n:n + 16], d[name].partition_broadcast(P))
            pat[name] = (n, 16)
            n += 16

        def PR(name):
            a, w = pat[name]
            return par[:, a:a + w]

        B4 = Banks(psum, [0, 1, 2, 3])
        BA = [4, 5, 6, 7]
        acc_free = [None] * 8

        def mms(b, out_ap, pairs, *waits, start=True, stop=True):
            def go(e):
                for n, (l, r) in enumerate(pairs):
                    ins = e.matmul(out_ap, lhsT=l, rhs=r, start=start and n == 0,
                                   stop=stop and n == len(pairs) - 1)
                return ins
            return q.pe(go, *waits)

        def bc3(ap, n, axis=2):
            a = ap.unsqueeze(axis)
            sh = list(a.shape)
            sh[axis] = n
            return a.to_broadcast(sh)

        def to_cols(src, dst, nblk, ready):
            op = None
            for tt in range(2):
                for k0 in range(0, nblk, 4):
                    b, bank, fr = B4.take()

                    def go(e, bank=bank, tt=tt, k0=k0):
                        for j in range(4):
                            ins = e.transpose(bank[:, j * P:(j + 1) * P], src(tt, k0 + j), ident)
                        return ins
                    t = q.pe(go, ready, fr, m_c)
                    pv = bank.rearrange("p (k s) -> p k s", k=4)
                    op = q.v(lambda e, pv=pv, k0=k0, tt=tt: e.tensor_copy(dst(k0, 4, tt), pv), t)
                    B4.give(b, op)
            return op

        def split_cols(src, ready, gain=None):
            op = None
            n = 0
            tfree = [None, None]
            for tt in range(2):
                for k0 in range(0, KB, 4):
                    b, bank, fr = B4.take()

                    def go(e, bank=bank, tt=tt, k0=k0):
                        for j in range(4):
                            ins = e.transpose(bank[:, j * P:(j + 1) * P], src(tt, k0 + j), ident)
                        return ins
                    t = q.pe(go, ready[tt] if isinstance(ready, list) else ready, fr, m_c)
                    pv = bank.rearrange("p (k s) -> p k s", k=4)
                    xh = XTH[:, k0:k0 + 4, tt * P:(tt + 1) * P]
                    xl = XTL[:, k0:k0 + 4, tt * P:(tt + 1) * P]
                    if gain is not None:
                        tmp = AR[:, 2048 + (n % 2) * 512:2560 + (n % 2) * 512]
                        g3 = tmp.rearrange("p (k s) -> p k s", k=4)
                        t = q.v(lambda e, pv=pv, k0=k0, g3=g3: e.tensor_tensor(
                            g3, pv, bc3(gain[:, k0:k0 + 4], P), ALU.mult), t, m_p, tfree[n % 2])
                        B4.give(b, t)
                        pv = g3
                    h = q.a(lambda e, xh=xh, pv=pv: e.activation(xh, pv, ACT.Copy), t)
                    op = q.v(lambda e, xh=xh, xl=xl, pv=pv: e.tensor_tensor(
                        xl, pv, xh.bitcast(F32), ALU.subtract), h)
                    if gain is None:
                        B4.give(b, op)
                    tfree[n % 2] = op
                    n += 1
            return op

        TMP = AR[:, 0:1024]

        def rstd_of(src, n, eps, tmp, r, *ready):
            ss = sm(1)
            o = q.a(lambda e: e.activation(tmp, src, ACT.Square, accum_out=ss), *ready)
            v = sm(1)
            o = q.v(lambda e: e.tensor_scalar(v, ss, 1.0 / n, eps, ALU.mult, ALU.add), o)
            o = q.a(lambda e: e.activation(r, v, ACT.Sqrt), o)
            return q.v(lambda e: e.reciprocal(r, r), o)

        def rms_cols(gain, ready):
            ops = []
            rows = AR[:, 0:2048].rearrange("p (t n) -> p t n", t=2)
            for tt in range(2):
                r = sm(1)
                o = rstd_of(X[:, tt, :], D, 1e-6, rows[:, tt, :], r, ready)
                ops.append(q.v(lambda e, tt=tt, r=r: e.tensor_scalar(
                    rows[:, tt, :], X[:, tt, :], r, None, ALU.mult), o))
            return split_cols(lambda tt, k: rows[:, tt, k * P:(k + 1) * P], ops, gain)

        def layer_norm(i, j, ready):
            gi, g, mg = bcast(d["ln_g_2"][i, j], D)
            bi, b, mb = bcast(d["ln_b_2"][i, j], D)
            op = ready
            for tt in range(2):
                x = X[:, tt, :]
                s1, mu, r = sm(1), sm(1), sm(1)
                q.v(lambda e, x=x, s1=s1: e.tensor_reduce(s1, x, AX.X, ALU.add), ready)
                q.v(lambda e, s1=s1, mu=mu: e.tensor_scalar(mu, s1, 1.0 / D, None, ALU.mult))
                o = q.v(lambda e, x=x, mu=mu: e.tensor_scalar(x, x, mu, None, ALU.subtract))
                o = rstd_of(x, D, 1e-5, TMP, r, o)
                q.v(lambda e, x=x, r=r: e.scalar_tensor_tensor(x, x, r, g, ALU.mult, ALU.mult), mg)
                op = q.v(lambda e, x=x: e.tensor_tensor(x, x, b, ALU.add), mb)
            bdone(gi, op)
            bdone(bi, op)
            return op

        def x_cols(ready):
            return split_cols(lambda tt, k: X[:, tt, k * P:(k + 1) * P], ready)

        def rope(src, dst, nh, cos, sin, tmp, *ready):
            s1, s2 = src[:, :, 0:32], src[:, :, 32:64]
            o1, o2 = dst[:, :, 0:32], dst[:, :, 32:64]
            t = tmp[:, 0:nh * 64].rearrange("p (h c) -> p h c", h=nh)
            cb, nb = bc3(cos, nh, 1), bc3(sin, nh, 1)
            q.v(lambda e: e.tensor_tensor(o1, s1, cb, ALU.mult), *ready)
            q.v(lambda e: e.tensor_tensor(o2, s2, cb, ALU.mult))
            q.v(lambda e: e.tensor_tensor(t[:, :, 0:32], s2, nb, ALU.mult))
            last = q.v(lambda e: e.tensor_tensor(t[:, :, 32:64], s1, nb, ALU.mult))
            q.v(lambda e: e.tensor_tensor(o1, o1, t[:, :, 0:32], ALU.subtract))
            op = q.v(lambda e: e.tensor_tensor(o2, o2, t[:, :, 32:64], ALU.add))
            return last, op

        def project_out(w, yt_ready, alpha):
            op = None
            for nh in range(2):
                for tt, (k, bank, o) in enumerate(gemm_cols(w, nh * 512, nh * 512 + 512, 2, yt_ready)):
                    xs = X[:, tt, nh * 512:nh * 512 + 512]
                    op = q.v(lambda e, xs=xs, bank=bank: e.scalar_tensor_tensor(
                        xs, xs, alpha, bank, ALU.mult, ALU.add), o)
                    B4.give(k, op)
            return op

        GS = AR[:, 4096:6144].rearrange("p (b t n) -> p b t n", b=2, t=2)

        def network(nt, chunks, wu, second, wd, acc, ready, last_mid=None):
            nc_ = len(chunks)
            hh_free, ht_free = [None, None], [None, None]
            hh, ht = {}, {}

            def up(c):
                a, n = chunks[c]
                hb = c % 2
                parts = []
                for tt, (k, bank, o) in enumerate(gemm_cols(wu, a, a + n, nt, ready)):
                    g = GS[:, hb, tt, 0:n]
                    f = ACT.Silu if second else ACT.Relu
                    op = q.a(lambda e, g=g, bank=bank, f=f: e.activation(g, bank, f), o, hh_free[hb])
                    B4.give(k, op)
                    parts.append(op)
                    if not second:
                        op = q.v(lambda e, g=g: e.tensor_tensor(g, g, g, ALU.mult), op)
                        hh[(c, tt)] = op
                if second:
                    for tt, (k, bank, o) in enumerate(
                            gemm_cols(wu, second + a, second + a + n, nt, ready)):
                        g = GS[:, hb, tt, 0:n]
                        op = q.v(lambda e, g=g, bank=bank: e.tensor_tensor(g, g, bank, ALU.mult),
                                 o, parts[tt])
                        B4.give(k, op)
                        hh[(c, tt)] = op

            def turn(c):
                a, n = chunks[c]
                hb = c % 2
                nb = n // P
                for tt in range(nt):
                    b, bank, fr = B4.take()

                    def go(e, bank=bank, tt=tt):
                        for j in range(nb):
                            ins = e.transpose(bank[:, j * P:(j + 1) * P],
                                              GS[:, hb, tt, j * P:(j + 1) * P], ident)
                        return ins
                    t = q.pe(go, hh[(c, tt)], fr)
                    pv = bank[:, 0:n].rearrange("p (j s) -> p j s", j=nb)
                    xh = HTH[:, hb, 0:nb, tt * P:(tt + 1) * P]
                    xl = HTL[:, hb, 0:nb, tt * P:(tt + 1) * P]
                    h = q.a(lambda e, xh=xh, pv=pv: e.activation(xh, pv, ACT.Copy), t, ht_free[hb])
                    op = q.v(lambda e, xh=xh, xl=xl, pv=pv: e.tensor_tensor(
                        xl, pv, xh.bitcast(F32), ALU.subtract), h)
                    B4.give(b, op)
                hh_free[hb] = t
                ht[c] = op

            def down(c):
                a, n = chunks[c]
                o = gemm_rows(wd, a, n // P, c % 2, nt, acc, c == 0, c == nc_ - 1, ht[c])
                ht_free[c % 2] = o
                return o

            for c in range(nc_):
                up(c)
                if c >= 1:
                    turn(c - 1)
                if c >= 2:
                    down(c - 2)
                if c == 2 and last_mid is not None:
                    last_mid()
            turn(nc_ - 1)
            down(nc_ - 2)
            return down(nc_ - 1)

        def residual(alpha, last):
            op = None
            for tt in range(2):
                for nh in range(2):
                    b = BA[tt * 2 + nh]
                    xs = X[:, tt, nh * 512:nh * 512 + 512]
                    op = q.v(lambda e, xs=xs, b=b: e.scalar_tensor_tensor(
                        xs, xs, alpha, psum[:, b, :], ALU.mult, ALU.add), last)
                    acc_free[b] = op
            return op

        def softmax_block(bank, nk, nh, mask, cnt, scale, W, fr_b, o):
            pv = bank.rearrange("p (h k) -> p h k", h=nh)
            w3 = W.rearrange("p (h k) -> p h k", h=nh)
            mx, l = sm(nh), sm(nh)
            rd = q.v(lambda e: e.scalar_tensor_tensor(w3, pv, scale, bc3(mask, nh, 1),
                                                      ALU.mult, ALU.add), o, fr_b)
            q.v(lambda e: e.tensor_reduce(mx, w3, AX.X, ALU.max))
            o = q.v(lambda e: e.tensor_tensor(w3, w3, bc3(mx, nk), ALU.subtract))
            o = q.a(lambda e: e.activation(W, W, ACT.Exp), o)
            if cnt is not None:
                o = q.v(lambda e: e.tensor_tensor(w3, w3, bc3(cnt, nh, 1), ALU.mult), o)
            o = q.v(lambda e: e.tensor_reduce(l, w3, AX.X, ALU.add), o)
            return rd, o, l

        def transposed_block(blocks, PT, o, fr_pt):
            b, bank, fr = B4.take()
            nb = len(blocks)

            def go(e):
                for i, src in enumerate(blocks):
                    ins = e.transpose(bank[:, i * P:(i + 1) * P], src, ident)
                return ins
            t = q.pe(go, o, fr)
            c = q.a(lambda e: e.activation(PT[:, 0:nb * P], bank[:, 0:nb * P], ACT.Copy), t, fr_pt)
            B4.give(b, c)
            return t, c

        def attention(nblk, qT, kz, v, mask, causal, W4, PT2, obanks, ready):
            res = [[sm(2 * nblk), None] for _ in range(2)]
            todo = [(qt, b) for qt in range(2) for b in range(nblk)]
            wfree, ptfree = [None] * 4, [None] * 2
            probs, turned = {}, {}

            def weigh(n):
                qt, b = todo[n]
                nk = P if (causal and qt == 0) else S
                L = res[qt][0]
                k, bank, fr = B4.take()
                o = mms(k, bank[:, 0:2 * nk], [(qT[:, b, qt * P:(qt + 1) * P],
                                                kz(b)[:, :, 0:nk])], ready, fr)
                W = W4[:, n % 4, 0:2 * nk]
                w3 = W.rearrange("p (h k) -> p h k", h=2)
                nm = sm(2)
                rd = q.v(lambda e: e.scalar_tensor_tensor(
                    w3, bank[:, 0:2 * nk].rearrange("p (h k) -> p h k", h=2), 0.125,
                    bc3(mask[:, qt, 0:nk], 2, 1), ALU.mult, ALU.add), o, wfree[n % 4])
                B4.give(k, rd)
                o = q.v(lambda e: e.tensor_reduce(nm, w3, AX.X, ALU.max, negate=True))
                for h in range(2):
                    o2 = q.a(lambda e, h=h: e.activation(
                        w3[:, h, :], w3[:, h, :], ACT.Exp, bias=nm[:, h:h + 1],
                        accum_out=L[:, 2 * b + h:2 * b + h + 1]), o)
                probs[n] = W, nk // P, o2

            def turn(n):
                W, kt, o = probs[n]
                t, c = transposed_block([W[:, i * P:(i + 1) * P] for i in range(2 * kt)],
                                        PT2[:, n % 2, :], o, ptfree[n % 2])
                wfree[n % 4] = t
                turned[n] = c

            def gather(n):
                qt, b = todo[n]
                kt = probs[n][1]
                for h in range(2):
                    head = 2 * b + h
                    ob = obanks[qt][head // 8]
                    col = (head % 8) * 64
                    PT = PT2[:, n % 2, :]
                    last = mms(ob, psum[:, ob, col:col + 64],
                               [(PT[:, (h * kt + i) * P:(h * kt + i + 1) * P], v(i, head))
                                for i in range(kt)], turned[n], acc_free[ob])
                ptfree[n % 2] = last
                res[qt][1] = last

            for n in range(len(todo) + 3):
                if n < len(todo):
                    weigh(n)
                if n >= 3:
                    gather(n - 3)
                if 2 <= n < len(todo) + 2:
                    turn(n - 2)
            return res

        def hybrid(l, ready):
            w_in = d["w_in"][l]
            xr = rms_cols(PR("n1g")[:, l * KB:(l + 1) * KB], ready)
            A = lambda a, n: AR[:, a:a + n]
            two = lambda r: r.rearrange("p (t n) -> p t n", t=2)
            PADW = S + 4
            pad = A(0, 8 * PADW).rearrange("p (b s) -> p b s", b=8)
            kz = A(2080, 2048).rearrange("p (b h s) -> p b h s", b=4, h=2)
            qk = A(2080, 2048).rearrange("p (b s) -> p b s", b=8)
            mv, mo = two(A(4128, 1024)), two(A(5152, 1024))
            aq, ak = two(A(6176, 1024)), two(A(7200, 1024))
            qks = two(A(0, 2048))
            av = two(A(8224, 1024))
            qT = A(9248, 1024).rearrange("p (b s) -> p b s", b=4)
            Y = two(A(10272, 2048))
            W2 = two(A(12320, 2048))
            W4 = A(12320, 2048).rearrange("p (t n) -> p t n", t=4)
            PT2 = two(A(14368, 1024))
            HM = Y[:, :, 0:512]
            TM = A(15392, 1024)

            q.v(lambda e: e.memset(pad[:, :, 0:2], 0.0), xr)
            q.v(lambda e: e.memset(pad[:, :, PADW - 2:PADW], 0.0))
            cw = PR("cw").rearrange("p (l b k) -> p l b k", l=2, b=8)
            raw = [two(A(12320, 1024)), two(A(13344, 1024))]
            rop = {}

            def project(part):
                for tt, (k, bank, o) in enumerate(
                        gemm_cols(w_in, part * 512, part * 512 + 512, 2, xr)):
                    c = q.a(lambda e, tt=tt, bank=bank: e.activation(
                        raw[part][:, tt, :], bank, ACT.Copy), o)
                    B4.give(k, c)
                    rop[(part, tt)] = c

            def conv(part):
                for tt in range(2):
                    b, bank, fr = B4.take()

                    def go(e, tt=tt, bank=bank):
                        for j in range(4):
                            ins = e.transpose(bank[:, j * P:(j + 1) * P],
                                              raw[part][:, tt, j * P:(j + 1) * P], ident)
                        return ins
                    t = q.pe(go, rop[(part, tt)], fr)
                    c = q.a(lambda e, tt=tt, bank=bank: e.activation(
                        pad[:, part * 4:part * 4 + 4, 2 + tt * P:2 + tt * P + P],
                        bank.rearrange("p (b s) -> p b s", b=4), ACT.Copy), t)
                    B4.give(b, c)
                for j in range(part * 4, part * 4 + 4):
                    q.v(lambda e, j=j: e.tensor_scalar(
                        qk[:, j, :], pad[:, j, 0:S], cw[:, l, j, 0:1], None, ALU.mult), c, m_p)
                    for k in range(1, 5):
                        o2 = q.v(lambda e, j=j, k=k: e.scalar_tensor_tensor(
                            qk[:, j, :], pad[:, j, k:k + S], cw[:, l, j, k:k + 1], qk[:, j, :],
                            ALU.mult, ALU.add))
                return o2, q.a(lambda e: e.activation(
                    qk[:, part * 4:part * 4 + 4, :], qk[:, part * 4:part * 4 + 4, :], ACT.Silu), o2)

            project(0)
            project(1)
            G = sm(32).rearrange("p (t g) -> p t g", t=2)
            for tt, (k, bank, o) in enumerate(gemm_cols(w_in, 2048, 2064, 2, xr)):
                q.v(lambda e, tt=tt, bank=bank: e.tensor_tensor(
                    G[:, tt, 0:8], bank[:, 0:8], PR("gib")[:, l * 8:l * 8 + 8], ALU.add), o, m_p)
                g_op = q.v(lambda e, tt=tt, bank=bank: e.tensor_tensor(
                    G[:, tt, 8:16], bank[:, 8:16], PR("gfb")[:, l * 8:l * 8 + 8], ALU.add))
                B4.give(k, g_op)
            f = G[:, :, 8:16]
            ab, ex, ln, LF, CC, BB = (sm(16).rearrange("p (t g) -> p t g", t=2) for _ in range(6))
            o = q.v(lambda e: e.scalar_tensor_tensor(ab, f, -1.0, f, ALU.mult, ALU.max), g_op)
            o = q.a(lambda e: e.activation(ex, ab, ACT.Exp, scale=-1.0), o)
            o = q.v(lambda e: e.tensor_scalar(ex, ex, 1.0, None, ALU.add), o)
            o = q.a(lambda e: e.activation(ln, ex, ACT.Ln), o)
            o = q.v(lambda e: e.scalar_tensor_tensor(LF, f, 0.0, ln, ALU.min, ALU.subtract), o)
            lf_op = o
            conv(0)
            for tt, (k, bank, o) in enumerate(gemm_cols(w_in, 1024, 1536, 2, xr)):
                mv_op = q.a(lambda e, tt=tt, bank=bank: e.activation(mv[:, tt, :], bank, ACT.Copy), o)
                B4.give(k, mv_op)
            conv_done, qk_op = conv(1)
            b, bank, fr = B4.take()
            ct = bank[:, 0:16].rearrange("p (t g) -> p t g", t=2)
            up, lo, on = C("upper"), C("lower"), C("ones")

            def cums(e):
                for tt, dr, pairs in ((0, 0, [(up, 0)]), (1, 0, [(on, 0), (up, 1)]),
                                      (1, 1, [(lo, 1)]), (0, 1, [(lo, 0), (on, 1)])):
                    for n, (m, s) in enumerate(pairs):
                        ins = e.matmul(ct[:, tt, dr * 4:dr * 4 + 4], lhsT=m,
                                       rhs=LF[:, s, dr * 4:dr * 4 + 4], start=n == 0,
                                       stop=n == len(pairs) - 1)
                return ins
            o = q.pe(cums, lf_op, fr)
            o = q.v(lambda e: e.tensor_copy(BB, ct), o)
            B4.give(b, o)
            o = q.v(lambda e: e.tensor_tensor(CC, G[:, :, 0:8], BB, ALU.subtract))
            cc_op = o
            for tt, (k, bank, o) in enumerate(gemm_cols(w_in, 1536, 2048, 2, xr)):
                mo_op = q.a(lambda e, tt=tt, bank=bank: e.activation(
                    mo[:, tt, :], bank, ACT.Sigmoid), o)
                B4.give(k, mo_op)
            b, bank, fr = B4.take()

            def tr(e, bank=bank):
                for tt in range(2):
                    ins = e.transpose(bank[0:8, tt * P:(tt + 1) * P], CC[:, tt, :], ident)
                return ins
            o = q.pe(tr, cc_op, fr)
            CT = TM[0:8, 512:768]
            ct_op = q.v(lambda e, bank=bank: e.tensor_copy(CT, bank[0:8, 0:256]), o)
            B4.give(b, ct_op)

            for qt in range(2):
                for hp in range(2):
                    b, bank, fr = B4.take()

                    def sc(e, qt=qt, hp=hp, bank=bank):
                        for h in range(2):
                            hd = hp * 2 + h
                            ins = e.matmul(bank[:, h * S:(h + 1) * S],
                                           lhsT=qk[:, hd, qt * P:(qt + 1) * P],
                                           rhs=qk[:, 4 + hd, :], start=True, stop=True)
                        return ins
                    o = q.pe(sc, qk_op, fr)
                    qs_op = q.a(lambda e, qt=qt, hp=hp, bank=bank: e.activation(
                        qks[:, qt, hp * 512:(hp + 1) * 512], bank, ACT.Copy,
                        scale=1.0 / math.sqrt(128.0)), o, conv_done)
                    B4.give(b, qs_op)
            todo = [(dr, qt) for dr in range(2) for qt in range(2)]
            ranges = ((0, P), (0, S), (0, S), (P, S))
            wf, ptf = [None, None], [None, None]
            logw, turned = {}, {}

            def weigh(n):
                dr, qt = todo[n]
                k0, k1 = ranges[n]
                nk = k1 - k0
                cbb = BA[dr * 2:dr * 2 + 2]
                if qt == 0:
                    def cb(e):
                        for h in range(4):
                            ins = e.matmul(
                                psum[:, cbb[h // 2], (h % 2) * S:(h % 2) * S + S],
                                lhsT=ident[0:8, dr * 4 + h:dr * 4 + h + 1].to_broadcast([8, P]),
                                rhs=CT, start=True, stop=True)
                        return ins
                    cbo[dr] = q.pe(cb, ct_op, acc_free[cbb[0]], acc_free[cbb[1]])
                mask = C2("mask_b" if dr else "mask_f")
                W = W2[:, n % 2, 0:4 * nk]
                w3 = W.rearrange("p (h k) -> p h k", h=4)
                nm, en = sm(4), sm(4)
                for hp in range(2):
                    pv = psum[:, cbb[hp], :].rearrange("p (h k) -> p h k", h=2)
                    acc_free[cbb[hp]] = q.v(lambda e, hp=hp, pv=pv: e.tensor_tensor(
                        w3[:, hp * 2:hp * 2 + 2, :], pv[:, :, k0:k1],
                        bc3(mask[:, qt, k0:k1], 2, 1), ALU.add), cbo[dr], wf[n % 2])
                o = q.v(lambda e: e.tensor_reduce(nm, w3, AX.X, ALU.max, negate=True))
                o3 = q.v(lambda e: e.tensor_tensor(
                    en, nm, BB[:, qt, dr * 4:dr * 4 + 4], ALU.subtract))
                for h in range(4):
                    o2 = q.a(lambda e, h=h: e.activation(
                        w3[:, h, :], w3[:, h, :], ACT.Exp, bias=nm[:, h:h + 1]), o)
                o3 = q.a(lambda e: e.activation(en, en, ACT.Exp), o3)
                logw[n] = W, w3, en, o3

            def turn(n):
                dr, qt = todo[n]
                k0, k1 = ranges[n]
                W, w3, en, o3 = logw[n]
                kt = (k1 - k0) // P
                den, ad = sm(4), sm(4)
                qv = qks[:, qt, :].rearrange("p (h k) -> p h k", h=4)
                for h in range(4):
                    w_op = q.v(lambda e, h=h: e.scalar_tensor_tensor(
                        w3[:, h, :], w3[:, h, :], 1.0, qv[:, h, k0:k1], ALU.mult, ALU.mult,
                        accum_out=den[:, h:h + 1]), o3, qs_op)
                q.v(lambda e: e.scalar_tensor_tensor(ad, den, -1.0, den, ALU.mult, ALU.max))
                q.v(lambda e: e.tensor_tensor(en, en, ad, ALU.max))
                q.v(lambda e: e.reciprocal(en, en))
                cs = []
                for hp in range(0, 4, 2):
                    t, c = transposed_block(
                        [W[:, (h * kt + i) * P:(h * kt + i + 1) * P]
                         for h in (hp, hp + 1) for i in range(kt)], PT2[:, hp // 2, :], w_op,
                        ptf[hp // 2])
                    cs.append(c)
                wf[n % 2] = t
                turned[n] = cs

            def gather(n):
                dr, qt = todo[n]
                k0, k1 = ranges[n]
                kt = (k1 - k0) // P
                en = logw[n][2]
                ob, bank, fr = B4.take()
                for hp in range(0, 4, 2):
                    PT = PT2[:, hp // 2, :]
                    for h in (hp, hp + 1):
                        o = mms(ob, bank[:, h * P:(h + 1) * P],
                                [(PT[:, ((h - hp) * kt + i) * P:((h - hp) * kt + i + 1) * P],
                                  mv[:, k0 // P + i, h * P:(h + 1) * P]) for i in range(kt)],
                                turned[n][hp // 2], mv_op, fr)
                    ptf[hp // 2] = o
                ov = bank.rearrange("p (h k) -> p h k", h=4)
                hm = HM[:, qt, :].rearrange("p (h k) -> p h k", h=4)
                if dr == 0:
                    r = q.v(lambda e: e.tensor_tensor(hm, ov, bc3(en, P), ALU.mult), o)
                else:
                    tm = TM[:, 0:512].rearrange("p (h k) -> p h k", h=4)
                    r = q.v(lambda e: e.tensor_tensor(tm, ov, bc3(en, P), ALU.mult), o)
                    q.v(lambda e: e.tensor_tensor(hm, hm, tm, ALU.add))
                B4.give(ob, r)

            cbo = {}

            def mlstm(step):
                if step < 4:
                    weigh(step)
                if 1 <= step <= 4:
                    turn(step - 1)
                if 1 <= step <= 4:
                    gather(step - 1)

            mlstm(0)
            for dst, c0 in ((aq, 2064), (ak, 2576)):
                for tt, (k, bank, o) in enumerate(gemm_cols(w_in, c0, c0 + 512, 2, xr)):
                    rd, aop = rope(bank.rearrange("p (h c) -> p h c", h=8),
                                   dst[:, tt, :].rearrange("p (h c) -> p h c", h=8), 8,
                                   C2("cos")[:, tt, :], C2("sin")[:, tt, :], TM[:, 0:512], o, m_c)
                    B4.give(k, rd)
                mlstm(1 + (c0 > 2064))
            for tt, (k, bank, o) in enumerate(gemm_cols(w_in, 3088, 3600, 2, xr)):
                av_op = q.a(lambda e, tt=tt, bank=bank: e.activation(av[:, tt, :], bank, ACT.Copy), o)
                B4.give(k, av_op)
            mlstm(3)
            qt_op = to_cols(lambda tt, k: aq[:, tt, k * P:(k + 1) * P],
                            lambda k0, nb, tt: qT[:, k0:k0 + nb, tt * P:(tt + 1) * P], 4, aop)
            q.v(lambda e: e.memset(kz, 0.0), qs_op)
            for tt in range(2):
                b, bank, fr = B4.take()

                def go(e, tt=tt, bank=bank):
                    for j in range(4):
                        ins = e.transpose(bank[:, j * P:(j + 1) * P], ak[:, tt, j * P:(j + 1) * P],
                                          ident)
                    return ins
                t = q.pe(go, aop, fr)
                pv = bank.rearrange("p (k s) -> p k s", k=4)
                q.v(lambda e, tt=tt, pv=pv: e.tensor_copy(
                    kz[0:64, :, 0, tt * P:(tt + 1) * P], pv[0:64]), t)
                kz_op = q.v(lambda e, tt=tt, pv=pv: e.tensor_copy(
                    kz[64:128, :, 1, tt * P:(tt + 1) * P], pv[64:128]))
                B4.give(b, kz_op)

            mlstm(4)
            gi, hg, mg = bcast(d["head_norm_g"][l], 512)
            for qt in range(2):
                hm = HM[:, qt, :].rearrange("p (h k) -> p h k", h=4)
                tm = TM[:, 0:512].rearrange("p (h k) -> p h k", h=4)
                ss = sm(4)
                q.v(lambda e, hm=hm, tm=tm: e.tensor_tensor(tm, hm, hm, ALU.mult))
                q.v(lambda e, tm=tm, ss=ss: e.tensor_reduce(ss, tm, AX.X, ALU.add))
                o = q.v(lambda e, ss=ss: e.tensor_scalar(ss, ss, 1.0 / P, 1e-6, ALU.mult, ALU.add))
                o = q.a(lambda e, ss=ss: e.activation(ss, ss, ACT.Sqrt), o)
                q.v(lambda e, ss=ss: e.reciprocal(ss, ss), o)
                q.v(lambda e, hm=hm, ss=ss: e.tensor_tensor(hm, hm, bc3(ss, P), ALU.mult))
                o = q.v(lambda e, qt=qt: e.tensor_tensor(HM[:, qt, :], HM[:, qt, :], hg, ALU.mult),
                        mg, mo_op)
                ym = q.v(lambda e, qt=qt: e.tensor_tensor(
                    Y[:, qt, 0:512], HM[:, qt, :], mo[:, qt, :], ALU.mult))
            bdone(gi, o)

            res = attention(4, qT, lambda b: kz[:, b, :, :], lambda i, h: av[:, i, h * 64:h * 64 + 64],
                            C2("mask_a"), False, W4, PT2, [[BA[0]], [BA[2]]], [kz_op, av_op])
            for qt in range(2):
                L, last = res[qt]
                ob = (BA[0], BA[2])[qt]
                q.v(lambda e, L=L: e.reciprocal(L, L), last)
                y_op = q.v(lambda e, L=L, ob=ob, qt=qt: e.tensor_tensor(
                    Y[:, qt, 512:1024].rearrange("p (h c) -> p h c", h=8),
                    psum[:, ob, :].rearrange("p (h c) -> p h c", h=8), bc3(L, 64), ALU.mult), last)
                acc_free[ob] = y_op
            yt = split_cols(lambda tt, k: Y[:, tt, k * P:(k + 1) * P], y_op)
            xo = project_out(d["w_out"][l], yt, 1.0)

            xr = rms_cols(PR("n2g")[:, l * KB:(l + 1) * KB], xo)
            last = network(2, [(c * 512, 512) for c in range(8)], d["w_up"][l], 0, d["w_down"][l],
                           BA, xr)
            return residual(1.0, last)

        def final_rms(ready):
            gi, g, mg = bcast(d["final_g"], D)
            for tt in range(2):
                r = sm(1)
                rstd_of(X[:, tt, :], D, 1e-6, TMP, r, ready)
                op = q.v(lambda e, tt=tt, r=r: e.scalar_tensor_tensor(
                    X[:, tt, :], X[:, tt, :], r, g, ALU.mult, ALU.mult), mg)
            bdone(gi, op)
            return op

        def pool_layer(ready):
            si, sc, ms = bcast(d["pool_scale_2"][0], D)
            pm = AR[:, 4608:6656].rearrange("p (t g s) -> p t g s", t=2, g=4)
            mk = q.dma("gpsimd", s_p, AR[:, 4608:6656], d["poolm"], ready)
            PX = AR[:, 2048:4096].rearrange("p (k s) -> p k s", k=8)
            pw = AR[:, 6656:8704].rearrange("p (g n) -> p g n", g=8)
            mk2 = q.dma("gpsimd", s_c, pw, d["pool_w_2"][0].rearrange("g (c p) n -> p (g c) n", p=P),
                        ready)
            for kp in range(4):
                b, bank, fr = B4.take()

                def go(e, kp=kp, bank=bank):
                    for h in range(2):
                        k = kp * 2 + h
                        for jt in range(2):
                            ins = e.matmul(bank[:, h * S:(h + 1) * S],
                                           lhsT=X[:, jt, k * P:(k + 1) * P], rhs=pm[:, jt, k // 2, :],
                                           start=jt == 0, stop=jt == 1)
                    return ins
                o = q.pe(go, ready, mk, fr)
                c = q.v(lambda e, kp=kp, bank=bank: e.tensor_copy(
                    PX[:, kp * 2:kp * 2 + 2, :], bank.rearrange("p (k s) -> p k s", k=2)), o)
                B4.give(b, c)
            for tt in range(2):
                for nh in range(2):
                    b, bank, fr = B4.take()

                    def go(e, tt=tt, nh=nh, bank=bank):
                        for gg in range(2):
                            g = nh * 2 + gg
                            for c in range(2):
                                ins = e.matmul(bank[:, gg * 256:gg * 256 + 256],
                                               lhsT=PX[:, g * 2 + c, tt * P:(tt + 1) * P],
                                               rhs=pw[:, g * 2 + c, :], start=c == 0, stop=c == 1)
                        return ins
                    o = q.pe(go, c, mk2, fr)
                    t = AR[:, 4096:4608]
                    xs = X[:, tt, nh * 512:nh * 512 + 512]
                    r = q.v(lambda e, bank=bank, t=t, nh=nh: e.tensor_tensor(
                        t, bank, sc[:, nh * 512:nh * 512 + 512], ALU.mult), o, ms)
                    B4.give(b, r)
                    op = q.v(lambda e, xs=xs, t=t: e.scalar_tensor_tensor(
                        xs, xs, ALPHA, t, ALU.mult, ALU.add))
            bdone(si, r)
            x1 = layer_norm(0, 0, op)
            xc = x_cols(x1)
            chunks = [(c * 512, min(512, FF2 - c * 512)) for c in range(6)]
            last = network(2, chunks, d["ffn_w_gu_2"][0], FF2, d["ffn_w_down_2"][0], BA, xc)
            return layer_norm(0, 1, residual(ALPHA, last))

        def nsa(ready):
            xc = x_cols(ready)
            w_in = d["nsa_w_in_2"][0]
            A = lambda a, n: AR[:, a:a + n]
            two = lambda r: r.rearrange("p (t n) -> p t n", t=2)
            Q = two(A(0, 2048))
            KZ = [A(0, 2048).rearrange("p (g h s) -> p g h s", g=4, h=2),
                  A(2048, 2048).rearrange("p (g h s) -> p g h s", g=4, h=2)]
            KR = [two(A(8192, 1024)), two(A(9216, 1024))]
            KCD = [two(A(4096, 1024)), two(A(10240, 1024))]
            qT = A(5120, 2048).rearrange("p (b s) -> p b s", b=8)
            V = [two(A(7168, 512)), two(A(7680, 512))]
            Y = two(A(8192, 2048))
            W2 = two(A(10240, 1024))
            W4 = A(10240, 2048).rearrange("p (t n) -> p t n", t=4)
            PT2 = two(A(12288, 1024))
            CB = [A(12288, 1024).rearrange("p (g s) -> p g s", g=4),
                  A(13312, 1024).rearrange("p (g s) -> p g s", g=4)]
            TM = A(14336, 1024)
            HID = A(15360, 128)
            KZC = A(15488, 256).rearrange("p (g h s) -> p g h s", g=4, h=2)
            VBD = A(15744, 256).rearrange("p (g c) -> p g c", g=4)
            GT = two(A(16000, 96))
            KC = A(16096, 64)
            KC2 = A(16160, 256)
            dup = lambda r: r.rearrange("p (g h c) -> p g h c", g=4, h=2)

            for nh in range(2):
                for tt, (k, bank, o) in enumerate(gemm_cols(w_in, nh * 512, nh * 512 + 512, 2, xc)):
                    rd, q_op = rope(bank.rearrange("p (h c) -> p h c", h=8),
                                    Q[:, tt, nh * 512:nh * 512 + 512].rearrange("p (h c) -> p h c", h=8),
                                    8, C2("cos")[:, tt, :], C2("sin")[:, tt, :], TM[:, 0:512], o)
                    B4.give(k, rd)
            for tt, (k, bank, o) in enumerate(gemm_cols(w_in, 1024, 1536, 2, xc)):
                for kind in range(2):
                    for h in range(2):
                        c_op = q.a(lambda e, kind=kind, h=h, tt=tt, bank=bank: e.activation(
                            dup(KCD[kind][:, tt, :])[:, :, h, :],
                            bank[:, kind * 256:kind * 256 + 256].rearrange("p (g c) -> p g c", g=4),
                            ACT.Copy), o)
                B4.give(k, c_op)
            qt_op = to_cols(lambda tt, k: Q[:, tt, k * P:(k + 1) * P],
                            lambda k0, nb, tt: qT[:, k0:k0 + nb, tt * P:(tt + 1) * P], 8,
                            [q_op, c_op])
            for kind, a in enumerate((1536, 2048)):
                for tt, (k, bank, o) in enumerate(gemm_cols(w_in, a, a + 512, 2, xc)):
                    kd = dup(KR[kind][:, tt, :])
                    rd, o2 = rope(bank[:, 0:256].rearrange("p (h c) -> p h c", h=4),
                                  kd[:, :, 0, :], 4,
                                  C2("cos")[:, tt, :], C2("sin")[:, tt, :], TM[:, 0:512], o)
                    v_op = q.v(lambda e, kind=kind, tt=tt, bank=bank: e.tensor_copy(
                        V[kind][:, tt, :], bank[:, 256:512]))
                    B4.give(k, v_op)
                    k_op = q.v(lambda e, kd=kd: e.tensor_copy(kd[:, :, 1, :], kd[:, :, 0, :]))
            for tt, (k, bank, o) in enumerate(gemm_cols(w_in, 2560, 2608, 2, xc)):
                gt_op = q.a(lambda e, tt=tt, bank=bank: e.activation(
                    GT[:, tt, :], bank, ACT.Sigmoid), o)
                B4.give(k, gt_op)
            for kind in range(2):
                for tt in range(2):
                    b, bank, fr = B4.take()

                    def go(e, kind=kind, tt=tt, bank=bank):
                        for g in range(4):
                            ins = e.transpose(bank[:, g * P:(g + 1) * P],
                                              KCD[kind][:, tt, g * P:(g + 1) * P], ident)
                        return ins
                    t = q.pe(go, c_op, fr)
                    pv = bank.rearrange("p (g s) -> p g s", g=4)
                    q.v(lambda e, kind=kind, tt=tt, pv=pv: e.tensor_copy(
                        CB[kind][0:64, :, tt * P:(tt + 1) * P], pv[0:64]), t)
                    if tt == 0:
                        cb_op = q.v(lambda e, kind=kind, pv=pv: e.tensor_copy(
                            CB[kind][64:128, :, 0:P - 1], pv[64:128, :, 1:P]))
                    else:
                        cb_op = q.v(lambda e, kind=kind, pv=pv: e.tensor_copy(
                            CB[kind][64:128, :, P - 1:S - 1], pv[64:128]))
                    B4.give(b, cb_op)
            for kind in range(2):
                q.v(lambda e, kind=kind: e.memset(KZ[kind], 0.0), qt_op)
                for tt in range(2):
                    b, bank, fr = B4.take()

                    def go(e, kind=kind, tt=tt, bank=bank):
                        for g in range(4):
                            ins = e.transpose(bank[:, g * P:(g + 1) * P],
                                              KR[kind][:, tt, g * P:(g + 1) * P], ident)
                        return ins
                    t = q.pe(go, k_op, fr)
                    pv = bank.rearrange("p (k s) -> p k s", k=4)
                    q.v(lambda e, kind=kind, tt=tt, pv=pv: e.tensor_copy(
                        KZ[kind][0:64, :, 0, tt * P:(tt + 1) * P], pv[0:64]), t)
                    kz_op = q.v(lambda e, kind=kind, tt=tt, pv=pv: e.tensor_copy(
                        KZ[kind][64:128, :, 1, tt * P:(tt + 1) * P], pv[64:128]))
                    B4.give(b, kz_op)
            q.v(lambda e: e.memset(HID, 0.0))
            q.v(lambda e: e.memset(KZC, 0.0))
            z_op = q.v(lambda e: e.memset(VBD, 0.0))
            for kind, (w1n, w2n, pen) in enumerate((("nsa_w1_k_2", "nsa_w2_k_2", "pek"),
                                                    ("nsa_w1_v_2", "nsa_w2_v_2", "pev"))):
                w1h, w1l, mk, own1 = unit(d[w1n][0].rearrange("(r p) n -> p r n", p=P), 16, P)
                w2h, w2l, mk2, own2 = unit(d[w2n][0].unsqueeze(1), 1, 64)
                w1 = [w1h.bitcast(F32), w1l.bitcast(F32)]
                w2 = [w2h.bitcast(F32)[:, 0, :], w2l.bitcast(F32)[:, 0, :]]
                b, bank, fr = B4.take()
                pe_ = PR(pen)

                def go(e, kind=kind, w1=w1, bank=bank, pe_=pe_):
                    for r in range(16):
                        for n in range(2):
                            e.matmul(bank[:, 64:65], lhsT=w1[n][:, r, :], rhs=pe_[:, r:r + 1],
                                     start=r + n == 0, stop=r + n == 16)
                    for r in range(16):
                        for n in range(2):
                            ins = e.matmul(bank[:, 0:60].rearrange("p (g n) -> p g n", g=4),
                                           lhsT=w1[n][:, r, :],
                                           rhs=CB[kind][:, :, 2 * r:2 * r + 225:16],
                                           start=r + n == 0, stop=r + n == 16)
                    return ins
                o = q.pe(go, cb_op, mk, fr, m_p, own=own1)
                pc = sm(1)
                q.v(lambda e, pc=pc, bank=bank: e.tensor_copy(pc, bank[:, 64:65]), o)
                hv = HID.rearrange("p (g n) -> p g n", g=4)[:, :, 0:15]
                o = q.v(lambda e, pc=pc, bank=bank, hv=hv: e.tensor_scalar(
                    hv, bank[:, 0:60].rearrange("p (g n) -> p g n", g=4), pc, None, ALU.add))
                B4.give(b, o)
                o = q.a(lambda e, hv=hv: e.activation(hv, hv, ACT.Silu), o)
                b, bank, fr = B4.take()
                o = q.pe(lambda e, bank=bank, w2=w2: [e.matmul(
                    bank[:, 0:64], lhsT=HID, rhs=w2[n], start=n == 0, stop=n == 1)
                    for n in range(2)][-1], o, fr, mk2, own=own2)
                if kind == 0:
                    rd, o = rope(bank[:, 0:64].rearrange("p (h c) -> p h c", h=1),
                                 KC.rearrange("p (h c) -> p h c", h=1), 1,
                                 C("cos_c"), C("sin_c"), TM[:, 0:512], o)
                    B4.give(b, rd)
                    q.v(lambda e: e.memset(KC2, 0.0))
                    q.v(lambda e: e.tensor_copy(KC2[:, 0:64], KC))
                    o = q.v(lambda e: e.tensor_copy(KC2[:, 128 + 64:256], KC))
                    b, bank, fr = B4.take()

                    def tr(e, bank=bank):
                        for h in range(2):
                            ins = e.transpose(bank[:, h * P:(h + 1) * P], KC2[:, h * P:(h + 1) * P],
                                              ident)
                        return ins
                    t = q.pe(tr, o, fr)
                    kc_op = q.v(lambda e, bank=bank: e.tensor_copy(
                        KZC, bank[:, 0:256].rearrange("p (h g n) -> p g h n", h=2, g=4)), t)
                    B4.give(b, kc_op)
                else:
                    for g in range(4):
                        vc_op = q.v(lambda e, g=g, bank=bank: e.tensor_copy(
                            VBD[32 * g:32 * g + 32, g, :], bank[32 * g:32 * g + 32, 0:64]), o)
                    B4.give(b, vc_op)
            wp_free = None
            for qt in range(2):
                b, bank, fr = B4.take()

                def sc(e, qt=qt, bank=bank):
                    for blk in range(8):
                        ins = e.matmul(bank[:, blk * 64:blk * 64 + 64],
                                       lhsT=qT[:, blk, qt * P:(qt + 1) * P],
                                       rhs=KZC[:, blk // 2, :, :], start=True, stop=True)
                    return ins
                o = q.pe(sc, kc_op, fr)
                W = W2[:, qt, :]
                rd, o, l = softmax_block(bank, 32, 16, C2("mask_c")[:, qt, :], None, 0.125, W, None, o)
                B4.give(b, rd)
                gl = sm(16)
                q.v(lambda e, l=l: e.reciprocal(l, l))
                gl_op = q.v(lambda e, l=l, gl=gl, qt=qt: e.scalar_tensor_tensor(
                    gl, l, C2("any_c")[:, qt, :],
                    GT[:, qt, :].rearrange("p (h b) -> p h b", b=3)[:, :, 0],
                    ALU.mult, ALU.mult), gt_op)
                wp = TM[:, 512:1024]
                o = q.v(lambda e, W=W, wp=wp: e.tensor_copy(
                    wp.rearrange("p (x g n) -> p g x n", x=4, g=4),
                    W.rearrange("p (g x n) -> p g x n", g=4, x=4)), wp_free)
                t, c = transposed_block([wp[:, x * P:(x + 1) * P] for x in range(4)],
                                        PT2[:, qt, :], o, None)
                wp_free = t
                for xp in range(2):
                    b, bank, fr = B4.take()

                    def pv_(e, xp=xp, bank=bank, qt=qt):
                        for x in range(2):
                            ins = e.matmul(bank[:, x * 256:x * 256 + 256],
                                           lhsT=PT2[:, qt, (xp * 2 + x) * P:(xp * 2 + x + 1) * P],
                                           rhs=VBD, start=True, stop=True)
                        return ins
                    o = q.pe(pv_, c, vc_op, fr)
                    for x in range(2):
                        yv = Y[:, qt, :].rearrange("p (g x c) -> p g x c", g=4, x=4)[:, :, xp * 2 + x, :]
                        glv = gl.rearrange("p (g x) -> p g x", g=4)[:, :, xp * 2 + x]
                        y_op = q.v(lambda e, yv=yv, glv=glv, bank=bank, x=x: e.tensor_tensor(
                            yv, bank[:, x * 256:x * 256 + 256].rearrange("p (g c) -> p g c", g=4),
                            bc3(glv, 64), ALU.mult), o)
                    B4.give(b, y_op)
            for kind in range(2):
                res = attention(8, qT, lambda b, kind=kind: KZ[kind][:, b // 2, :, :],
                                lambda i, h, kind=kind: V[kind][:, i, (h // 4) * 64:(h // 4) * 64 + 64],
                                C2("mask_f"), True, W4, PT2, [BA[0:2], BA[2:4]],
                                [kz_op, v_op] if kind == 0 else y_op)
                for qt in range(2):
                    L, last = res[qt]
                    q.v(lambda e, L=L: e.reciprocal(L, L), last)
                    q.v(lambda e, L=L, qt=qt, kind=kind: e.tensor_tensor(
                        L, L, GT[:, qt, :].rearrange("p (h b) -> p h b", b=3)[:, :, 1 + kind],
                        ALU.mult))
                    for hb in range(2):
                        ob = BA[qt * 2 + hb]
                        tm = TM[:, 0:512].rearrange("p (h c) -> p h c", h=8)
                        r = q.v(lambda e, L=L, ob=ob, hb=hb, tm=tm: e.tensor_tensor(
                            tm, psum[:, ob, :].rearrange("p (h c) -> p h c", h=8),
                            bc3(L[:, hb * 8:hb * 8 + 8], 64), ALU.mult), last)
                        acc_free[ob] = r
                        y_op = q.v(lambda e, qt=qt, hb=hb: e.tensor_tensor(
                            Y[:, qt, hb * 512:hb * 512 + 512], Y[:, qt, hb * 512:hb * 512 + 512],
                            TM[:, 0:512], ALU.add))
            yt = split_cols(lambda tt, k: Y[:, tt, k * P:(k + 1) * P], y_op)
            xo = project_out(d["nsa_w_out_2"][0], yt, ALPHA)
            return layer_norm(1, 0, xo)

        A_ = lambda a, n: AR[:, a:a + n]
        YA = A_(0, 2048).rearrange("p (t n) -> p t n", t=2)
        SEL = A_(2816, 16).rearrange("p (t n) -> p t n", t=2)
        CMB = A_(2832, 16).rearrange("p (t n) -> p t n", t=2)
        POS = A_(2848, 16).rearrange("p (t n) -> p t n", t=2)
        LG = A_(2864, 16).rearrange("p (t n) -> p t n", t=2)
        EQ = A_(2880, 128)
        EQ2 = A_(3008, 128)
        RK = A_(3136, 16).rearrange("p (t n) -> p t n", t=2)
        PL = A_(6144, 2 * 2 * S).rearrange("p (b t n) -> p b t n", b=2, t=2)
        PW = A_(7168, 2 * S).rearrange("p (t n) -> p t n", t=2)
        PB = A_(7680, 2 * 2 * S).rearrange("p (b t n) -> p b t n", b=2, t=2)
        YE = A_(8704, 2048).rearrange("p (t n) -> p t n", t=2)

        def route(ready):
            xc = x_cols(ready)
            for tt, (k, bank, o) in enumerate(gemm_cols(d["moe_router_2"][0], 0, 8, 2, xc)):
                r = q.v(lambda e, tt=tt, bank=bank: e.tensor_copy(LG[:, tt, :], bank), o)
                B4.give(k, r)
            idx = C("iota")[:, 0:8]
            for tt in range(2):
                lg = LG[:, tt, :]
                a = bc3(lg, 8, 1)
                b = bc3(lg, 8, 2)
                m = EQ[:, 0:64].rearrange("p (a b) -> p a b", a=8)
                m2 = EQ2[:, 0:64].rearrange("p (a b) -> p a b", a=8)
                m3 = EQ2[:, 64:128].rearrange("p (a b) -> p a b", a=8)
                q.v(lambda e, a=a, b=b, m=m: e.tensor_tensor(m, a, b, ALU.is_gt))
                q.v(lambda e, a=a, b=b, m2=m2: e.tensor_tensor(m2, a, b, ALU.is_equal))
                q.v(lambda e, m3=m3: e.tensor_tensor(m3, bc3(idx, 8, 1), bc3(idx, 8, 2), ALU.is_lt))
                q.v(lambda e, m2=m2, m3=m3: e.tensor_tensor(m2, m2, m3, ALU.mult))
                q.v(lambda e, m=m, m2=m2: e.tensor_tensor(m, m, m2, ALU.add))
                q.v(lambda e, m=m, tt=tt: e.tensor_reduce(RK[:, tt, :], m, AX.X, ALU.add))
                q.v(lambda e, tt=tt: e.tensor_scalar(SEL[:, tt, :], RK[:, tt, :], 1.5, None, ALU.is_lt))
                mx, s = sm(1), sm(1)
                q.v(lambda e, lg=lg, mx=mx: e.tensor_reduce(mx, lg, AX.X, ALU.max))
                o = q.v(lambda e, lg=lg, mx=mx, tt=tt: e.tensor_scalar(
                    CMB[:, tt, :], lg, mx, None, ALU.subtract))
                o = q.a(lambda e, tt=tt: e.activation(CMB[:, tt, :], CMB[:, tt, :], ACT.Exp), o)
                q.v(lambda e, tt=tt: e.tensor_tensor(CMB[:, tt, :], CMB[:, tt, :], SEL[:, tt, :],
                                                     ALU.mult), o)
                q.v(lambda e, tt=tt, s=s: e.tensor_reduce(s, CMB[:, tt, :], AX.X, ALU.add))
                q.v(lambda e, s=s: e.reciprocal(s, s))
                o = q.v(lambda e, tt=tt, s=s: e.tensor_scalar(CMB[:, tt, :], CMB[:, tt, :], s, None,
                                                              ALU.mult))
            k, bank, fr = B4.take()

            def cum(e, bank=bank):
                e.matmul(bank[:, 0:8], lhsT=C("strict"), rhs=SEL[:, 0, :], start=True, stop=True)
                e.matmul(bank[:, 8:16], lhsT=C("ones"), rhs=SEL[:, 0, :], start=True, stop=False)
                e.matmul(bank[:, 8:16], lhsT=C("strict"), rhs=SEL[:, 1, :], start=False, stop=True)
                e.matmul(bank[:, 16:24], lhsT=C("ones"), rhs=SEL[:, 0, :], start=True, stop=False)
                return e.matmul(bank[:, 16:24], lhsT=C("ones"), rhs=SEL[:, 1, :], start=False,
                                stop=True)
            o = q.pe(cum, o, fr)
            q.v(lambda e, bank=bank: e.tensor_copy(
                POS, bank[:, 0:16].rearrange("p (t n) -> p t n", t=2)), o)
            f_op = q.v(lambda e, bank=bank: e.tensor_scalar(
                flag[0:1, :], bank[0:1, 16:24], P + 0.5, None, ALU.is_gt))
            B4.give(k, f_op)
            q.v(lambda e: e.memset(YA, 0.0))
            return f_op

        def prepare(x):
            xb = x % 2
            for tt in range(2):
                q.v(lambda e, tt=tt: e.tensor_scalar(
                    PL[:, xb, tt, :], C("iota"), POS[:, tt, x:x + 1], SEL[:, tt, x:x + 1],
                    ALU.is_equal, ALU.mult))
                s_op = q.v(lambda e, tt=tt: e.tensor_scalar(
                    PW[:, tt, :], PL[:, xb, tt, :], CMB[:, tt, x:x + 1], None, ALU.mult))
            b, bank, fr = B4.take()

            def tr(e):
                for st in range(2):
                    for tt in range(2):
                        ins = e.transpose(bank[:, (st * 2 + tt) * P:(st * 2 + tt + 1) * P],
                                          PW[:, tt, st * P:(st + 1) * P], ident)
                return ins
            t = q.pe(tr, s_op, fr)
            op = q.v(lambda e: e.tensor_copy(
                PB[:, xb, :, :], bank.rearrange("p (t n) -> p t n", t=2)), t)
            B4.give(b, op)

        def expert(x, nt, ready):
            xb = x % 2
            for k0 in range(0, KB, 4 // nt):
                kn = 4 // nt
                b, bank, fr = B4.take()

                def go(e, k0=k0, bank=bank):
                    for j in range(kn):
                        for tt in range(2):
                            ins = e.matmul(bank[:, j * nt * P:(j + 1) * nt * P],
                                           lhsT=X[:, tt, (k0 + j) * P:(k0 + j + 1) * P],
                                           rhs=PL[:, xb, tt, 0:nt * P], start=tt == 0, stop=tt == 1)
                    return ins
                t = q.pe(go, fr, ready)
                pv = bank.rearrange("p (k s) -> p k s", k=kn)
                xh, xl = XTH[:, k0:k0 + kn, 0:nt * P], XTL[:, k0:k0 + kn, 0:nt * P]
                h = q.a(lambda e, xh=xh, pv=pv: e.activation(xh, pv, ACT.Copy), t)
                op = q.v(lambda e, xh=xh, xl=xl, pv=pv: e.tensor_tensor(
                    xl, pv, xh.bitcast(F32), ALU.subtract), h)
                B4.give(b, op)
            acc = BA if nt == 2 else BA[(x % 2) * 2:(x % 2) * 2 + 2]
            last = network(nt, [(c * 512, 512) for c in range(7)], d["moe_w_gu_2"][0, x], FE,
                           d["moe_w_down_2"][0, x], acc, op,
                           (lambda: prepare(x + 1)) if x + 1 < N_EXP else None)
            for st in range(nt):
                for nh in range(2):
                    ab = acc[st * 2 + nh]
                    ye = q.a(lambda e, st=st, nh=nh, ab=ab: e.activation(
                        YE[:, st, nh * 512:nh * 512 + 512], psum[:, ab, :], ACT.Copy), last)
                    acc_free[ab] = ye
            for nh in range(2):
                for tt in range(2):
                    b, bank, fr = B4.take()
                    o = mms(b, bank, [(PB[:, xb, st, tt * P:(tt + 1) * P],
                                       YE[:, st, nh * 512:nh * 512 + 512]) for st in range(nt)],
                            ye, fr)
                    y = YA[:, tt, nh * 512:nh * 512 + 512]
                    r = q.v(lambda e, y=y, bank=bank: e.tensor_tensor(y, y, bank, ALU.add), o)
                    B4.give(b, r)

        def settle(name):
            ends = [q.end(name, "vector"), q.end(name, "scalar"), q.end(name, "tensor")]
            for b in range(8):
                B4.free[b] = ends
                acc_free[b] = ends
            return ends

        op = hybrid(0, m_x)
        op = hybrid(1, op)
        op = final_rms(op)
        op = pool_layer(op)
        op = nsa(op)
        f_op = route(op)
        f_op.used = True
        prepare(0)
        ends = settle("first")
        for x in range(N_EXP):
            state = unit_n[0], B4.n
            for side in range(2):
                unit_n[0], B4.n = state
                B4.free = {b: ends for b in range(8)}
                for b in range(8):
                    acc_free[b] = ends
                q.enter((f"expert{x}", side))
                expert(x, side + 1, ends)
            B4.n = 0
            ends = settle(f"expert{x}")
        q.enter("last")
        for tt in range(2):
            op = q.v(lambda e, tt=tt: e.scalar_tensor_tensor(
                X[:, tt, :], X[:, tt, :], ALPHA, YA[:, tt, :], ALU.mult, ALU.add), ends)
        op = layer_norm(1, 1, op)
        q.part = "first"
        for u, (src, k, n) in enumerate(units):
            i = u % NSLOT
            q.dma("sync", s_ring[i], ring[:, i * UNIT:i * UNIT + k * n].rearrange(
                "p (k n) -> p k n", k=k), src, Mark(s_lo, u - NSLOT + 1))
        q.dma("sync", s_out, out.rearrange("b (t p) n -> p (b t) n", p=P), X, op)

        q.n_units = len(units)
        q.number()
        block = ctx.enter_context(nc.Block())

        def run(eng, e):
            seen = {}
            branches = eng in ("tensor", "vector", "scalar")
            q.emit(e, eng, "first", seen)
            if branches:
                e.wait_ge(f_op.sem, f_op.value)
                many = [e.value_load(flag[0:1, x:x + 1]) for x in range(N_EXP)]
                for x in range(N_EXP):
                    sides = [dict(seen), dict(seen)]
                    with e.If(many[x] > 0):
                        q.emit(e, eng, (f"expert{x}", 1), sides[1])
                    with e.Else():
                        q.emit(e, eng, (f"expert{x}", 0), sides[0])
                    seen = {k: min(sides[0].get(k, 0), sides[1].get(k, 0)) for k in sides[0]}
            q.emit(e, eng, "last", seen)
            if eng == "sync":
                e.wait_ge(s_out, 16)

        @block.sync
        def _(e):
            run("sync", e)

        @block.tensor
        def _(e):
            run("tensor", e)

        @block.vector
        def _(e):
            run("vector", e)

        @block.scalar
        def _(e):
            run("scalar", e)

        @block.gpsimd
        def _(e):
            run("gpsimd", e)


def arrange(inputs):
    at, cons, pool = constants()
    a = {k: np.ascontiguousarray(np.asarray(v)) for k, v in inputs.items()}

    def cols(x, n):
        return np.ascontiguousarray(x.reshape(2, KB, P).transpose(2, 0, 1).reshape(P, n))

    arrays = {k: a[k] for k in (
        "x", "w_in", "head_norm_g", "w_out", "w_up", "w_down", "final_g", "ln_g_2", "ln_b_2",
        "pool_w_2", "pool_scale_2", "nsa_w_in_2", "nsa_w1_k_2", "nsa_w2_k_2", "nsa_w1_v_2",
        "nsa_w2_v_2", "nsa_w_out_2", "ffn_w_gu_2", "ffn_w_down_2", "moe_router_2", "moe_w_gu_2",
        "moe_w_down_2")}
    arrays["n1g"] = cols(a["norm1_g"], 16)
    arrays["n2g"] = cols(a["norm2_g"], 16)
    arrays["cw"] = np.ascontiguousarray(
        a["conv_w"].reshape(2, 5, KB, P).transpose(3, 0, 2, 1).reshape(P, 80))
    for new, old in (("pek", "nsa_pe_k_2"), ("pev", "nsa_pe_v_2")):
        arrays[new] = np.ascontiguousarray(a[old].reshape(16, P).T)
    arrays["gib"] = a["gate_i_b"].reshape(16)
    arrays["gfb"] = a["gate_f_b"].reshape(16)
    arrays["cons"] = cons
    arrays["poolm"] = pool
    return arrays, (at, cons.shape[1], pool.shape[1])


def kernel(**inputs):
    import concourse.bacc as bacc
    from concourse.bass_utils import run_bass_kernel_spmd

    nc = bacc.Bacc("TRN2", target_bir_lowering=False, num_devices=1)
    arrays, tables = arrange(inputs)
    d = {n: nc.dram_tensor(f"in_{n}", v.shape, mybir.dt.from_np(v.dtype), kind="ExternalInput").ap()
         for n, v in arrays.items()}
    out = nc.dram_tensor("out_0", (1, S, D), F32, kind="ExternalOutput").ap()
    build(nc, d, out, tables)
    r = run_bass_kernel_spmd(nc, [{f"in_{n}": v for n, v in arrays.items()}], core_ids=[0])
    return r.results[0]["out_0"]
```

```python
import math
from contextlib import ExitStack

import numpy as np
import concourse.bass as bass
from concourse import mybir

F32 = mybir.dt.float32
F32R = mybir.dt.float32r
I32 = mybir.dt.int32
ALU = mybir.AluOpType
ACT = mybir.ActivationFunctionType
AX = mybir.AxisListType

P = 128
S = 256
D = 1024
KB = D // P
UNIT = 2048
NSLOT = 4
NHL = 3
NEG = -1.0e30
ALPHA = (2 * 2) ** 0.25
N_EXP = 8
FE = 3584
FF2 = 2816


def constants():
    parts, at = [], {}
    n = 0

    def add(name, a):
        nonlocal n
        a = np.asarray(a, np.float32).reshape(P, -1)
        at[name] = (n, a.shape[1])
        parts.append(a)
        n += a.shape[1]

    i = np.arange(P)
    add("ident", np.eye(P))
    add("ones", np.ones((P, P)))
    add("upper", (i[:, None] <= i[None, :]))
    add("lower", (i[:, None] >= i[None, :]))
    add("strict", (i[:, None] < i[None, :]))
    add("iota", np.tile(np.arange(S), (P, 1)))
    t = np.arange(S)
    d = np.abs(t[:, None] - t[None, :])
    cnt = (d <= 64).astype(np.float32) + (d % 4 == 0) + (d % 16 == 0)
    tok = lambda a: np.asarray(a, np.float32).reshape(2, P, -1).transpose(1, 0, 2)
    add("mask_a", tok(np.where(cnt > 0, np.log(np.maximum(cnt, 1)), NEG)))
    add("mask_f", tok(np.where(t[None, :] <= t[:, None], 0.0, NEG)))
    add("mask_b", tok(np.where(t[None, :] >= t[:, None], 0.0, NEG)))
    nn = np.arange(32)
    cend = 16 * nn + 31
    ok = (cend[None, :] <= t[:, None]) & (nn[None, :] < 15)
    add("mask_c", tok(np.where(ok, 0.0, NEG)))
    add("any_c", tok(ok.any(axis=1)))
    inv = (np.float32(10000.0) ** (-np.arange(32, dtype=np.float32) / np.float32(32))).astype(np.float32)
    ang = (t.astype(np.float32)[:, None] * inv[None, :]).astype(np.float32)
    add("cos", tok(np.cos(ang)))
    add("sin", tok(np.sin(ang)))
    angc = (np.tile(cend, 4).astype(np.float32)[:, None] * inv[None, :]).astype(np.float32)
    add("cos_c", np.cos(angc))
    add("sin_c", np.sin(angc))
    pool = np.zeros((P, 2, 4, S), np.float32)
    for g, w in enumerate((2, 4, 8, 16)):
        m = np.zeros((S, S), np.float32)
        for q in range(S):
            lo = max(q + 1 - w, 0)
            m[lo:q + 1, q] = np.float32(1.0) / np.float32(min(q + 1, w))
            m[q, q] -= 1.0
        pool[:, :, g, :] = m.reshape(2, P, S).transpose(1, 0, 2)
    return at, np.concatenate(parts, axis=1), pool.reshape(P, -1)


class Op:

    def __init__(self, eng, fn, waits, part):
        self.eng, self.fn, self.waits, self.part = eng, fn, waits, part
        self.used = self.own = False
        self.extra = 0
        self.unit = None
        self.sem = self.value = None


class Mark:

    def __init__(self, sem, value):
        self.sem, self.value = sem, value


class End:

    def __init__(self, part, eng):
        self.part, self.eng = part, eng
        self.sem = self.value = None


def flat(w):
    return [v for u in w for v in flat(u)] if isinstance(w, (list, tuple)) else [w]


class Queues:

    def __init__(self, nc, sems):
        self.nc, self.sems = nc, sems
        self.parts = ["first"]
        self.part = "first"
        self.q = {}
        self.last = {}
        self.dcount = {}
        self.ends = []

    def enter(self, part):
        self.part = part
        self.parts.append(part)
        self.last = {}

    def end(self, name, eng):
        m = End(name, eng)
        self.ends.append(m)
        return m

    def add(self, eng, fn, waits, chain, own=None):
        ws = []
        for w in waits:
            ws += flat(w)
        ws = [w for w in ws if w is not None]
        prev = self.last.get(eng)
        if chain and prev is not None:
            ws.append(prev)
        for w in ws:
            if isinstance(w, Op):
                w.used = True
        op = Op(eng, fn, ws, self.part)
        if own is not None:
            op.sem, op.value, op.own = own[0], own[1], True
        self.q.setdefault((self.part, eng), []).append(op)
        if chain:
            self.last[eng] = op
        return op

    def pe(self, fn, *w, own=None):
        return self.add("tensor", fn, w, False, own)

    def v(self, fn, *w):
        return self.add("vector", fn, w, True)

    def a(self, fn, *w):
        return self.add("scalar", fn, w, True)

    def p(self, fn, *w):
        return self.add("gpsimd", fn, w, False)

    def dma(self, eng, sem, out, in_, *w):
        n = self.dcount[sem] = self.dcount.get(sem, 0) + 16
        self.add(eng, lambda e: e.dma_start(out, in_).then_inc(sem, 16), w, False)
        return Mark(sem, n)

    def number(self):
        count = {}
        after = {}
        for part in self.parts:
            side = part[1] if isinstance(part, tuple) else None
            if side is None or side == 0:
                base = dict(count)
            ends = {}
            for eng in ("tensor", "vector", "scalar", "gpsimd"):
                n = base.get(eng, 0)
                ops = [o for o in self.q.get((part, eng), []) if not o.own]
                if ops and eng != "gpsimd":
                    ops[-1].used = True
                for op in ops:
                    if op.used:
                        n += 1
                        op.sem, op.value = self.sems[eng], n
                ends[eng] = n
                if side is not None and ops:
                    after[(part, eng)] = (ops[-1], n)
            if side == 1:
                for eng in ends:
                    hi = max(ends[eng], first_ends[eng])
                    for p in ((part[0], 0), part):
                        if (p, eng) in after:
                            op, n = after[(p, eng)]
                            op.extra = hi - n
                    ends[eng] = hi
            elif side == 0:
                first_ends = dict(ends)
            count = ends
            for m in self.ends:
                if m.part == (part[0] if side is not None else part):
                    m.sem, m.value = self.sems[m.eng], count.get(m.eng, 0)

    def emit(self, e, eng, part, seen):
        for op in self.q.get((part, eng), []):
            if op.unit is not None and op.unit >= self.n_units:
                continue
            need = {}
            for w in op.waits:
                if seen.get(w.sem, 0) < w.value:
                    need[w.sem] = max(need.get(w.sem, 0), w.value)
            for sem, value in need.items():
                e.wait_ge(sem, value)
                seen[sem] = value
            ins = op.fn(e)
            if ins is not None and (op.used or op.own):
                ins.then_inc(op.sem, 1 + op.extra)


class Banks:

    def __init__(self, psum, numbers):
        self.psum, self.numbers, self.n = psum, numbers, 0
        self.free = {}

    def take(self):
        b = self.numbers[self.n % len(self.numbers)]
        self.n += 1
        return b, self.psum[:, b, :], self.free.get(b)

    def give(self, b, *ops):
        self.free[b] = list(ops)


def build(nc, d, out, tables):
    at, cons_cols, pool_cols = tables
    with ExitStack() as ctx:
        def sem(name):
            return ctx.enter_context(nc.semaphore(name))

        def sb(name, cols, dt=F32, rows=P):
            return ctx.enter_context(nc.sbuf_tensor(name, [rows, cols], dt))

        q = Queues(nc, {e: sem(f"s_{e}") for e in ("tensor", "vector", "scalar",
                                                             "gpsimd")})
        psum = ctx.enter_context(nc.psum_tensor("psum", [P, 8, 512], F32))
        ring = sb("ring", NSLOT * UNIT)
        HI = sb("HI", NHL * UNIT, F32R)
        LO = sb("LO", NHL * UNIT, F32R)
        cons = sb("cons", cons_cols)
        par = sb("par", 240)
        bcs = sb("bcs", 2 * D)
        X = sb("X", 2 * D)[:].rearrange("p (t n) -> p t n", t=2)
        XTH = sb("XTH", KB * S, F32R)[:].rearrange("p (k s) -> p k s", k=KB)
        XTL = sb("XTL", KB * S, F32R)[:].rearrange("p (k s) -> p k s", k=KB)
        HTH = sb("HTH", 8 * S, F32R)[:].rearrange("p (b j s) -> p b j s", b=2, j=4)
        HTL = sb("HTL", 8 * S, F32R)[:].rearrange("p (b j s) -> p b j s", b=2, j=4)
        SML = sb("SML", 512)
        EPS = sb("EPS", 2)
        TMP2 = sb("TMP2", 512)
        TG = sb("TG", 256, rows=48)
        AR = sb("AR", 16160)
        flag = sb("flag", N_EXP, I32)

        s_ring = [sem(f"s_ring{i}") for i in range(NSLOT)]
        s_bc = [sem(f"s_bc{i}") for i in range(2)]
        s_x2, s_id, s_g = sem("s_x2"), sem("s_id"), sem("s_g")
        s_x, s_c, s_p, s_out = sem("s_x"), sem("s_c"), sem("s_p"), sem("s_out")
        s_hi, s_lo, s_use = sem("s_hi"), sem("s_lo"), sem("s_use")

        def C(name, rows=P):
            a, n = at[name]
            return cons[0:rows, a:a + n]

        def C2(name):
            return C(name).rearrange("p (t n) -> p t n", t=2)

        ident = C("ident")

        small = [0]

        def sm(n):
            a = small[0]
            if a + n > 512:
                a = 0
            small[0] = a + n
            return SML[:, a:a + n]

        units = []
        unit_n = [0]
        AHEAD = 2
        held = []
        late = []

        def split(u):
            def sizes():
                src, k, n = units[u]
                return k * n

            def hi(e):
                if u >= len(units):
                    return None
                n = sizes()
                r, h = (u % NSLOT) * UNIT, (u % NHL) * UNIT
                return e.activation(HI[:, h:h + n], ring[:, r:r + n], ACT.Copy)

            def lo(e):
                if u >= len(units):
                    return None
                n = sizes()
                r, h = (u % NSLOT) * UNIT, (u % NHL) * UNIT
                return e.tensor_tensor(LO[:, h:h + n], ring[:, r:r + n],
                                       HI[:, h:h + n].bitcast(F32), ALU.subtract)

            loaded = Mark(s_ring[u % NSLOT], 16 * (u // NSLOT + 1))
            used = Mark(s_use, u - NHL + 1)
            q.add("scalar", hi, (loaded, used), False, own=(s_hi, u + 1)).unit = u
            q.add("vector", lo, (Mark(s_hi, u + 1),), False, own=(s_lo, u + 1)).unit = u

        def flush():
            while held:
                split(held.pop(0))

        def unit(src, k, n, defer=False, keep=False):
            if not keep:
                flush()
            u = unit_n[0]
            unit_n[0] += 1
            if u == len(units):
                units.append((src, k, n))
            if u == 0:
                for v in range(AHEAD):
                    split(v)
            held.append(u + AHEAD)
            if not defer:
                flush()
            h = (u % NHL) * UNIT
            view = lambda t: t[:, h:h + k * n].rearrange("p (k n) -> p k n", k=k)
            return view(HI), view(LO), Mark(s_lo, u + 1), (s_use, u + 1)

        def group3(out_ap, trios, start, stop):
            def go(e):
                n, m = 0, 3 * len(trios)
                for lh, ll, rh, rl in trios:
                    for a, b in ((lh, rh), (lh, rl), (ll, rh)):
                        ins = e.matmul(out_ap, lhsT=a, rhs=b, start=start and n == 0,
                                       stop=stop and n == m - 1)
                        n += 1
                return ins
            return go

        def of(ready, t):
            return ready[t] if isinstance(ready, dict) else ready

        def gemm_cols(w, a, b, nt, ready, swap=0, major=False, mid=None, banks=None):
            n = b - a
            kk = 4 if n > 256 else 8
            banks = ([(i, psum[:, i, :], acc_free[i]) for i in banks] if banks else
                     [B4.take() for _ in range(nt)])
            us = []

            def part(k0, t):
                hv, lv, mk, own = us[k0 // kk]
                _, bank, fr = banks[t]
                ts = slice((t ^ swap) * P, (t ^ swap) * P + P)
                return q.pe(group3(bank[:, 0:n], [
                    (XTH[:, k0 + k, ts], XTL[:, k0 + k, ts], hv[:, k, :], lv[:, k, :])
                    for k in range(kk)], k0 == 0, k0 + kk == KB),
                    of(ready, t), mk, fr if k0 == 0 else None, own=own if t == nt - 1 else None)

            def get(k0):
                us.append(unit(w[k0 * P:(k0 + kk) * P, a:b].rearrange("(k p) n -> p k n", p=P),
                               kk, n, major, major and k0 > 0))

            ops = {}
            if major:
                for k0 in range(0, KB, kk):
                    get(k0)
                for t in range(nt):
                    for k0 in range(0, KB, kk):
                        ops[t] = part(k0, t)
                    while late:
                        late.pop(0)()
                    while t == 0 and len(held) > 1:
                        split(held.pop(0))
            else:
                for k0 in range(0, KB, kk):
                    get(k0)
                    for t in range(nt):
                        ops[t] = part(k0, t)
                    for f in (mid or {}).get(k0 // kk, ()):
                        f()
            return [(bk[0], bk[1][:, 0:n], ops[t]) for t, bk in enumerate(banks)]

        tg_free = [None]

        def gemm_few(w, a, b, ready):
            while late:
                late.pop(0)()
            n = b - a
            hv, lv, mk, own = unit(w[:, a:b].rearrange("(k p) n -> p k n", p=P), KB, n)
            k, bank, fr = B4.take()
            made = q.pe(group3(bank[0:n, 0:S], [
                (hv[:, i, :], lv[:, i, :], XTH[:, i, :], XTL[:, i, :]) for i in range(KB)],
                True, True), of(ready, 0), of(ready, 1), mk, fr, own=own)
            c = q.a(lambda e: e.activation(TG[0:n, :], bank[0:n, 0:S], ACT.Copy), made, tg_free[0])
            B4.give(k, c)

            def turned():
                k2, bank2, fr = B4.take()

                def turn(e):
                    for t in range(2):
                        ins = e.transpose(bank2[:, t * n:(t + 1) * n], TG[0:n, t * P:(t + 1) * P],
                                          ident[0:n, 0:n])
                    return ins
                o = tg_free[0] = q.pe(turn, c, fr)
                return [(k2, bank2[:, t * n:(t + 1) * n], o) for t in range(2)]
            return made, turned

        def gemm_rows(w, a, kb, hb, nt, acc, start, stop, ready, major=False):
            us, ops = [], {}

            def part(k0, t):
                hv, lv, mk, own = us[k0 // 2]
                ts = slice(t * P, t * P + P)
                for nh in range(2):
                    bk = acc[t * 2 + nh]
                    ns = slice(nh * 512, nh * 512 + 512)
                    first = start and k0 == 0
                    ops[t * 2 + nh] = q.pe(group3(psum[:, bk, :], [
                        (HTH[:, hb, k0 + k, ts], HTL[:, hb, k0 + k, ts], hv[:, k, ns],
                         lv[:, k, ns]) for k in range(2)], first, stop and k0 + 2 == kb),
                        ready, mk, acc_free[bk] if first else None,
                        own=own if (t, nh) == (nt - 1, 1) else None)

            def get(k0):
                us.append(unit(w[a + k0 * P:a + (k0 + 2) * P, :].rearrange("(k p) n -> p k n", p=P),
                               2, D, major and k0 + 2 == kb))

            if major:
                for k0 in range(0, kb, 2):
                    get(k0)
                for t in range(nt):
                    for k0 in range(0, kb, 2):
                        part(k0, t)
            else:
                for k0 in range(0, kb, 2):
                    get(k0)
                    for t in range(nt):
                        part(k0, t)
            return [ops[i] for i in sorted(ops)]

        bc_n = [0]
        bc_free = [None] * 2

        def bcast(src, n):
            i = bc_n[0] % 2
            bc_n[0] += 1
            dst = bcs[:, i * D:i * D + n]
            mark = q.dma("gpsimd", s_bc[i], dst, src.partition_broadcast(P), bc_free[i])
            return i, dst, mark

        def bdone(i, op):
            bc_free[i] = op

        m_x = [q.dma("sync", s, X[:, t, :], d["x"][0, t * P:(t + 1) * P, :])
               for t, s in enumerate((s_x, s_x2))]
        m_id = q.dma("gpsimd", s_id, cons[:, 0:P], d["cons"][:, 0:P])
        bc_n[0] = 1
        g_first = 0, bcs[:, 0:D], q.dma("sync", s_g, bcs[:, 0:D],
                                        d["norm1_g"][0].partition_broadcast(P))
        m_c = q.dma("gpsimd", s_c, cons[:, P:cons_cols], d["cons"][:, P:cons_cols],
                    Mark(s_ring[1], 16))
        m_p = None
        pat = {}
        n = 0
        for name in ("cw", "pek", "pev"):
            w = d[name].shape[1]
            m_p = q.dma("gpsimd", s_p, par[:, n:n + w], d[name])
            pat[name] = (n, w)
            n += w
        for name in ("gib", "gfb"):
            m_p = q.dma("gpsimd", s_p, par[:, n:n + 16], d[name].partition_broadcast(P))
            pat[name] = (n, 16)
            n += 16

        def PR(name):
            a, w = pat[name]
            return par[:, a:a + w]

        B4 = Banks(psum, [0, 1, 2, 3])
        BA = [4, 5, 6, 7]
        acc_free = [None] * 8

        def mms(b, out_ap, pairs, *waits, start=True, stop=True):
            def go(e):
                for n, (l, r) in enumerate(pairs):
                    ins = e.matmul(out_ap, lhsT=l, rhs=r, start=start and n == 0,
                                   stop=stop and n == len(pairs) - 1)
                return ins
            return q.pe(go, *waits)

        def bc3(ap, n, axis=2):
            a = ap.unsqueeze(axis)
            sh = list(a.shape)
            sh[axis] = n
            return a.to_broadcast(sh)

        def to_cols(src, dst, nblk, ready):
            for tt in range(2):
                for k0 in range(0, nblk, 4):
                    b, bank, fr = B4.take()

                    def go(e, bank=bank, tt=tt, k0=k0):
                        for j in range(4):
                            ins = e.transpose(bank[:, j * P:(j + 1) * P], src(tt, k0 + j), ident)
                        return ins
                    t = q.pe(go, ready, fr, m_id)
                    pv = bank.rearrange("p (k s) -> p k s", k=4)
                    op = q.a(lambda e, pv=pv, k0=k0, tt=tt: e.activation(
                        dst(k0, 4, tt), pv, ACT.Copy), t)
                    B4.give(b, op)
            return op

        def split_tile(src, tt, ready):
            op = None
            for k0 in range(0, KB, 4):
                b, bank, fr = B4.take()

                def go(e, bank=bank, k0=k0):
                    for j in range(4):
                        ins = e.transpose(bank[:, j * P:(j + 1) * P], src(k0 + j), ident)
                    return ins
                t = q.pe(go, ready, fr, m_id)
                pv = bank.rearrange("p (k s) -> p k s", k=4)
                xh = XTH[:, k0:k0 + 4, tt * P:(tt + 1) * P]
                xl = XTL[:, k0:k0 + 4, tt * P:(tt + 1) * P]
                h = q.a(lambda e, xh=xh, pv=pv: e.activation(xh, pv, ACT.Copy), t)
                op = q.v(lambda e, xh=xh, xl=xl, pv=pv: e.tensor_tensor(
                    xl, pv, xh.bitcast(F32), ALU.subtract), h)
                B4.give(b, op)
            return op

        def split_both(rows, ready):
            done = {}

            def tile(t):
                done[t] = split_tile(lambda k: rows[:, t, k * P:(k + 1) * P], t, ready[t])
            tile(0)
            late.append(lambda: tile(1))
            return done

        ROWS = AR[:, 0:2048].rearrange("p (t n) -> p t n", t=2)

        def norm(kind, g, b, source, cols=True, loaded=None):
            gi, gv, mg = loaded or bcast(g, D)
            if kind == "ln":
                bi, bv, mb = bcast(b, D)
            stat, ops = {}, {}
            dst = ROWS if kind == "rms" and cols else X

            def gather(t):
                st = sm(2)
                for nh in range(2):
                    o = source(t, nh, st[:, nh:nh + 1])
                    if kind == "rms":
                        xs = X[:, t, nh * 512:nh * 512 + 512]
                        o = q.a(lambda e, xs=xs, nh=nh: e.activation(
                            TMP2[:, 0:512], xs, ACT.Square, accum_out=st[:, nh:nh + 1]), o)
                stat[t] = st, o

            def apply(t):
                st, o = stat[t]
                x, r, mv = X[:, t, :], sm(1), sm(2)
                if kind == "ln":
                    ss = sm(2)
                    q.v(lambda e: e.tensor_tensor(mv[:, 0:1], st[:, 0:1], st[:, 1:2], ALU.add), o)
                    o = q.v(lambda e: e.tensor_scalar(mv[:, 1:2], mv[:, 0:1], -1.0 / D, None,
                                                      ALU.mult))
                    for nh in range(2):
                        o2 = q.a(lambda e, nh=nh: e.activation(
                            TMP2[:, 0:512], X[:, t, nh * 512:nh * 512 + 512], ACT.Square,
                            bias=mv[:, 1:2], accum_out=ss[:, nh:nh + 1]), o)
                    q.v(lambda e: e.scalar_tensor_tensor(ROWS[:, t, :], x, mv[:, 1:2], gv, ALU.add,
                                                         ALU.mult), mg)
                    o = q.v(lambda e: e.tensor_tensor(mv[:, 0:1], ss[:, 0:1], ss[:, 1:2], ALU.add),
                            o2)
                    o = q.a(lambda e: e.activation(r, mv[:, 0:1], ACT.Sqrt, scale=1.0 / D,
                                                   bias=EPS[:, 0:1]), o)
                    q.v(lambda e: e.reciprocal(r, r), o)
                    ops[t] = q.v(lambda e: e.scalar_tensor_tensor(
                        x, ROWS[:, t, :], r, bv, ALU.mult, ALU.add), mb)
                else:
                    o = q.v(lambda e: e.tensor_tensor(mv[:, 0:1], st[:, 0:1], st[:, 1:2], ALU.add), o)
                    o = q.a(lambda e: e.activation(r, mv[:, 0:1], ACT.Sqrt, scale=1.0 / D,
                                                   bias=EPS[:, 1:2]), o)
                    q.v(lambda e: e.reciprocal(r, r), o)
                    ops[t] = q.v(lambda e: e.scalar_tensor_tensor(
                        dst[:, t, :], x, r, gv, ALU.mult, ALU.mult), mg)

            def turn(t):
                if cols:
                    done[t] = split_tile(lambda k: dst[:, t, k * P:(k + 1) * P], t, ops[t])

            done = {}
            gather(0)
            apply(0)
            turn(0)
            flush()
            gather(1)
            apply(1)
            late.append(lambda: turn(1))
            bdone(gi, ops[1])
            if kind == "ln":
                bdone(bi, ops[1])
            return (done if cols else ops), ops[1]

        def rope(src, dst, nh, cos, sin, tmp, *ready):
            o1, o2 = dst[:, :, 0:32], dst[:, :, 32:64]
            t = tmp[:, 0:nh * 64].rearrange("p (h c) -> p h c", h=nh)

            def all4(ap):
                return ap.rearrange("p h (x c) -> p h x c", x=2)

            def rep4(ap):
                return ap.unsqueeze(1).unsqueeze(1).to_broadcast([P, nh, 2, 32])
            q.v(lambda e: e.tensor_tensor(all4(dst), all4(src), rep4(cos), ALU.mult), *ready)
            last = q.v(lambda e: e.tensor_tensor(all4(t), all4(src), rep4(sin), ALU.mult))
            q.v(lambda e: e.tensor_tensor(o1, o1, t[:, :, 32:64], ALU.subtract))
            op = q.v(lambda e: e.tensor_tensor(o2, o2, t[:, :, 0:32], ALU.add))
            return last, op

        def project_out(w, yt_ready, alpha):
            out = {}
            for nh in range(2):
                for tt, r in enumerate(gemm_cols(w, nh * 512, nh * 512 + 512, 2, yt_ready,
                                                 major=True, banks=[BA[nh], BA[2 + nh]])):
                    out[(tt, nh)] = r

            def source(tt, nh, sums):
                k, bank, o = out[(tt, nh)]
                xs = X[:, tt, nh * 512:nh * 512 + 512]
                op = q.v(lambda e: e.scalar_tensor_tensor(
                    xs, xs, alpha, bank, ALU.mult, ALU.add, accum_out=sums), o)
                acc_free[k] = op
                return op
            return source

        GS = AR[:, 4096:6144].rearrange("p (b t n) -> p b t n", b=2, t=2)

        def network(nt, chunks, wu, second, wd, acc, ready, swap=0, mid=None):
            nc_ = len(chunks)
            hh_free, ht_free = [None, None], [None, None]
            hh, ht = {}, {}

            def up(c):
                a, n = chunks[c]
                hb = c % 2
                parts = []
                for tt, (k, bank, o) in enumerate(
                        gemm_cols(wu, a, a + n, nt, ready, swap, nt == 2 and c == 0)):
                    g = GS[:, hb, tt, 0:n]
                    f = ACT.Silu if second else ACT.Relu
                    op = q.a(lambda e, g=g, bank=bank, f=f: e.activation(g, bank, f), o, hh_free[hb])
                    B4.give(k, op)
                    parts.append(op)
                    if not second:
                        op = q.v(lambda e, g=g: e.tensor_tensor(g, g, g, ALU.mult), op)
                        hh[(c, tt)] = op
                if second:
                    for tt, (k, bank, o) in enumerate(
                            gemm_cols(wu, second + a, second + a + n, nt, ready, swap)):
                        g = GS[:, hb, tt, 0:n]
                        op = q.v(lambda e, g=g, bank=bank: e.tensor_tensor(g, g, bank, ALU.mult),
                                 o, parts[tt])
                        B4.give(k, op)
                        hh[(c, tt)] = op

            def turn(c):
                a, n = chunks[c]
                hb = c % 2
                nb = n // P
                for tt in range(nt):
                    b, bank, fr = B4.take()

                    def go(e, bank=bank, tt=tt):
                        for j in range(nb):
                            ins = e.transpose(bank[:, j * P:(j + 1) * P],
                                              GS[:, hb, tt, j * P:(j + 1) * P], ident)
                        return ins
                    t = q.pe(go, hh[(c, tt)], fr)
                    pv = bank[:, 0:n].rearrange("p (j s) -> p j s", j=nb)
                    xh = HTH[:, hb, 0:nb, tt * P:(tt + 1) * P]
                    xl = HTL[:, hb, 0:nb, tt * P:(tt + 1) * P]
                    h = q.a(lambda e, xh=xh, pv=pv: e.activation(xh, pv, ACT.Copy), t, ht_free[hb])
                    op = q.v(lambda e, xh=xh, xl=xl, pv=pv: e.tensor_tensor(
                        xl, pv, xh.bitcast(F32), ALU.subtract), h)
                    B4.give(b, op)
                hh_free[hb] = t
                ht[c] = op

            def down(c):
                a, n = chunks[c]
                o = gemm_rows(wd, a, n // P, c % 2, nt, acc, c == 0, c == nc_ - 1, ht[c],
                              nt == 2 and c == nc_ - 1)
                ht_free[c % 2] = o
                return o

            for c in range(nc_):
                up(c)
                if mid is not None and c in mid:
                    mid[c]()
                if c >= 1:
                    turn(c - 1)
                if c >= 2:
                    down(c - 2)
            turn(nc_ - 1)
            down(nc_ - 2)
            return down(nc_ - 1)

        def residual(alpha, last):
            def source(tt, nh, sums):
                b = BA[tt * 2 + nh]
                xs = X[:, tt, nh * 512:nh * 512 + 512]
                acc_free[b] = q.v(lambda e: e.scalar_tensor_tensor(
                    xs, xs, alpha, psum[:, b, :], ALU.mult, ALU.add, accum_out=sums),
                    last[tt * 2 + nh])
                return acc_free[b]
            return source

        def softmax_block(bank, nk, nh, mask, cnt, scale, W, fr_b, o):
            pv = bank.rearrange("p (h k) -> p h k", h=nh)
            w3 = W.rearrange("p (h k) -> p h k", h=nh)
            mx, l = sm(nh), sm(nh)
            rd = q.v(lambda e: e.scalar_tensor_tensor(w3, pv, scale, bc3(mask, nh, 1),
                                                      ALU.mult, ALU.add), o, fr_b)
            q.v(lambda e: e.tensor_reduce(mx, w3, AX.X, ALU.max))
            o = q.v(lambda e: e.tensor_tensor(w3, w3, bc3(mx, nk), ALU.subtract))
            o = q.a(lambda e: e.activation(W, W, ACT.Exp), o)
            if cnt is not None:
                o = q.v(lambda e: e.tensor_tensor(w3, w3, bc3(cnt, nh, 1), ALU.mult), o)
            o = q.v(lambda e: e.tensor_reduce(l, w3, AX.X, ALU.add), o)
            return rd, o, l

        def transposed_block(blocks, PT, o, fr_pt):
            b, bank, fr = B4.take()
            nb = len(blocks)

            def go(e):
                for i, src in enumerate(blocks):
                    ins = e.transpose(bank[:, i * P:(i + 1) * P], src, ident)
                return ins
            t = q.pe(go, o, fr)
            c = q.a(lambda e: e.activation(PT[:, 0:nb * P], bank[:, 0:nb * P], ACT.Copy), t, fr_pt)
            B4.give(b, c)
            return t, c

        def attention(nblk, qT, kz, v, mask, causal, W4, PT2, obanks, ready, heads, mid=None):
            res = [[sm(2 * nblk), None] for _ in range(2)]
            todo = [(qt, b) for qt in range(2) for b in range(nblk)]
            wfree, ptfree = [None] * 4, [None] * 2
            probs, turned = {}, {}

            def weigh(n):
                qt, b = todo[n]
                nk = P if (causal and qt == 0) else S
                L = res[qt][0]
                k, bank, fr = B4.take()
                o = mms(k, bank[:, 0:2 * nk], [(qT[:, b, qt * P:(qt + 1) * P],
                                                kz(b)[:, :, 0:nk])], ready, fr)
                W = W4[:, n % 4, 0:2 * nk]
                w3 = W.rearrange("p (h k) -> p h k", h=2)
                nm = sm(2)
                rd = q.v(lambda e: e.scalar_tensor_tensor(
                    w3, bank[:, 0:2 * nk].rearrange("p (h k) -> p h k", h=2), 0.125,
                    bc3(mask[:, qt, 0:nk], 2, 1), ALU.mult, ALU.add), o, wfree[n % 4])
                B4.give(k, rd)
                o = q.v(lambda e: e.tensor_reduce(nm, w3, AX.X, ALU.max, negate=True))
                for h in range(2):
                    o2 = q.a(lambda e, h=h: e.activation(
                        w3[:, h, :], w3[:, h, :], ACT.Exp, bias=nm[:, h:h + 1],
                        accum_out=L[:, 2 * b + h:2 * b + h + 1]), o)
                probs[n] = W, nk // P, o2

            def turn(n):
                W, kt, o = probs[n]
                t, c = transposed_block([W[:, i * P:(i + 1) * P] for i in range(2 * kt)],
                                        PT2[:, n % 2, :], o, ptfree[n % 2])
                wfree[n % 4] = t
                turned[n] = c

            def gather(n):
                qt, b = todo[n]
                kt = probs[n][1]
                for h in range(2):
                    head = 2 * b + h
                    ob = obanks[qt][head // 8]
                    col = (head % 8) * 64
                    PT = PT2[:, n % 2, :]
                    last = mms(ob, psum[:, ob, col:col + 64],
                               [(PT[:, (h * kt + i) * P:(h * kt + i + 1) * P], v(i, head))
                                for i in range(kt)], turned[n], acc_free[ob])
                ptfree[n % 2] = last
                res[qt][1] = last

            for n in range(len(todo) + 3):
                if 2 <= n < len(todo) + 2:
                    turn(n - 2)
                if n < len(todo):
                    weigh(n)
                if mid is not None and n in mid:
                    mid[n]()
                if n >= 3:
                    gather(n - 3)
                    if todo[n - 3][1] == nblk - 1:
                        heads(todo[n - 3][0], *res[todo[n - 3][0]])

        def hybrid(l, source):
            w_in = d["w_in"][l]
            xr, xop = norm("rms", d["norm1_g"][l], None, source,
                           loaded=None if l else g_first)
            A = lambda a, n: AR[:, a:a + n]
            two = lambda r: r.rearrange("p (t n) -> p t n", t=2)
            PADW = S + 4
            pad = A(0, 8 * PADW).rearrange("p (b s) -> p b s", b=8)
            kz = A(2080, 2048).rearrange("p (b h s) -> p b h s", b=4, h=2)
            qk = A(2080, 2048).rearrange("p (b s) -> p b s", b=8)
            mv, mo = two(A(4128, 1024)), two(A(5152, 1024))
            aq, ak = two(A(6176, 1024)), two(A(7200, 1024))
            qks = two(A(0, 2048))
            av = two(A(8224, 1024))
            qT = A(9248, 1024).rearrange("p (b s) -> p b s", b=4)
            Y = two(A(10272, 2048))
            W2 = two(A(12320, 2048))
            W4 = A(12320, 2048).rearrange("p (t n) -> p t n", t=4)
            PT2 = two(A(14368, 1024))
            HM = Y[:, :, 0:512]
            TM = A(15392, 768)

            cw = PR("cw").rearrange("p (l b k) -> p l b k", l=2, b=8)
            raw = [two(A(12320, 1024)), two(A(13344, 1024))]
            rop = {}

            def project(part):
                for tt, (k, bank, o) in enumerate(
                        gemm_cols(w_in, part * 512, part * 512 + 512, 2, xr, major=part == 0)):
                    c = q.a(lambda e, tt=tt, bank=bank: e.activation(
                        raw[part][:, tt, :], bank, ACT.Copy), o)
                    B4.give(k, c)
                    rop[(part, tt)] = c

            padded, sums = {}, {}

            def pad_cols(part):
                for tt in range(2):
                    b, bank, fr = B4.take()

                    def go(e, tt=tt, bank=bank):
                        for j in range(4):
                            ins = e.transpose(bank[:, j * P:(j + 1) * P],
                                              raw[part][:, tt, j * P:(j + 1) * P], ident)
                        return ins
                    t = q.pe(go, rop[(part, tt)], fr)
                    c = q.a(lambda e, tt=tt, bank=bank: e.activation(
                        pad[:, part * 4:part * 4 + 4, 2 + tt * P:2 + tt * P + P],
                        bank.rearrange("p (b s) -> p b s", b=4), ACT.Copy), t)
                    B4.give(b, c)
                padded[part] = c

            def conv(part, half):
                for j in range(part * 4 + half * 2, part * 4 + half * 2 + 2):
                    q.v(lambda e, j=j: e.tensor_scalar(
                        qk[:, j, :], pad[:, j, 0:S], cw[:, l, j, 0:1], None, ALU.mult),
                        padded[part], m_p)
                    for k in range(1, 5):
                        sums[part] = q.v(lambda e, j=j, k=k: e.scalar_tensor_tensor(
                            qk[:, j, :], pad[:, j, k:k + S], cw[:, l, j, k:k + 1], qk[:, j, :],
                            ALU.mult, ALU.add))

            def silu(part):
                return q.a(lambda e: e.activation(
                    qk[:, part * 4:part * 4 + 4, :], qk[:, part * 4:part * 4 + 4, :], ACT.Silu),
                    sums[part])

            project(0)
            q.v(lambda e: e.memset(pad[:, :, 0:2], 0.0), xr[0], xr[1])
            q.v(lambda e: e.memset(pad[:, :, PADW - 2:PADW], 0.0))
            project(1)
            _, gates = gemm_few(w_in, 2048, 2064, xr)
            pad_cols(0)
            G, LF, CC, BB = (sm(n).rearrange("p (t g) -> p t g", t=2) for n in (32, 16, 16, 16))
            CT = TM[0:8, 512:768]
            gate = {}

            def input_gates():
                for tt, (k, bank, o) in enumerate(gates()):
                    q.v(lambda e, tt=tt, bank=bank: e.tensor_tensor(
                        G[:, tt, 0:8], bank[:, 0:8], PR("gib")[:, l * 8:l * 8 + 8], ALU.add), o, m_p)
                    o = q.v(lambda e, tt=tt, bank=bank: e.tensor_tensor(
                        G[:, tt, 8:16], bank[:, 8:16], PR("gfb")[:, l * 8:l * 8 + 8], ALU.add))
                    B4.give(k, o)
                f = G[:, :, 8:16]
                ab, ex, ln = (sm(16).rearrange("p (t g) -> p t g", t=2) for _ in range(3))
                o = q.v(lambda e: e.scalar_tensor_tensor(ab, f, -1.0, f, ALU.mult, ALU.max))
                o = q.a(lambda e: e.activation(ex, ab, ACT.Exp, scale=-1.0), o)
                o = q.v(lambda e: e.tensor_scalar(ex, ex, 1.0, None, ALU.add), o)
                o = q.a(lambda e: e.activation(ln, ex, ACT.Ln), o)
                gate["lf"] = q.v(lambda e: e.scalar_tensor_tensor(
                    LF, f, 0.0, ln, ALU.min, ALU.subtract), o)

            def cumulate():
                b, bank, fr = B4.take()
                ct = bank[:, 0:16].rearrange("p (t g) -> p t g", t=2)
                up, lo, on = C("upper"), C("lower"), C("ones")

                def cums(e):
                    for tt, dr, pairs in ((0, 0, [(up, 0)]), (1, 0, [(on, 0), (up, 1)]),
                                          (1, 1, [(lo, 1)]), (0, 1, [(lo, 0), (on, 1)])):
                        for n, (m, s) in enumerate(pairs):
                            ins = e.matmul(ct[:, tt, dr * 4:dr * 4 + 4], lhsT=m,
                                           rhs=LF[:, s, dr * 4:dr * 4 + 4], start=n == 0,
                                           stop=n == len(pairs) - 1)
                    return ins
                o = q.pe(cums, gate["lf"], fr)
                o = q.v(lambda e: e.tensor_copy(BB, ct), o)
                B4.give(b, o)
                gate["cc"] = q.v(lambda e: e.tensor_tensor(CC, G[:, :, 0:8], BB, ALU.subtract))

            def turn_gates():
                b, bank, fr = B4.take()

                def tr(e):
                    for tt in range(2):
                        ins = e.transpose(bank[0:8, tt * P:(tt + 1) * P], CC[:, tt, :], ident)
                    return ins
                o = q.pe(tr, gate["cc"], fr)
                gate["ct"] = q.v(lambda e: e.tensor_copy(CT, bank[0:8, 0:256]), o)
                B4.give(b, gate["ct"])

            for tt, (k, bank, o) in enumerate(gemm_cols(
                    w_in, 1024, 1536, 2, xr,
                    mid={0: [input_gates, lambda: conv(0, 0)], 1: [lambda: conv(0, 1)]})):
                mv_op = q.a(lambda e, tt=tt, bank=bank: e.activation(mv[:, tt, :], bank, ACT.Copy), o)
                B4.give(k, mv_op)
            pad_cols(1)
            for tt, (k, bank, o) in enumerate(gemm_cols(
                    w_in, 1536, 2048, 2, xr,
                    mid={0: [cumulate, lambda: silu(0), lambda: conv(1, 0)],
                         1: [turn_gates, lambda: conv(1, 1)]})):
                mo_op = q.a(lambda e, tt=tt, bank=bank: e.activation(
                    mo[:, tt, :], bank, ACT.Sigmoid), o)
                B4.give(k, mo_op)
            conv_done, qk_op = sums[1], silu(1)
            ct_op = gate["ct"]

            def scores():
                for qt in range(2):
                    for hp in range(2):
                        b, bank, fr = B4.take()

                        def sc(e, qt=qt, hp=hp, bank=bank):
                            for h in range(2):
                                hd = hp * 2 + h
                                ins = e.matmul(bank[:, h * S:(h + 1) * S],
                                               lhsT=qk[:, hd, qt * P:(qt + 1) * P],
                                               rhs=qk[:, 4 + hd, :], start=True, stop=True)
                            return ins
                        o = gate["sc"] = q.pe(sc, qk_op, fr)
                        gate["qs"] = q.a(lambda e, qt=qt, hp=hp, bank=bank: e.activation(
                            qks[:, qt, hp * 512:(hp + 1) * 512], bank, ACT.Copy,
                            scale=1.0 / math.sqrt(128.0)), o, conv_done)
                        B4.give(b, gate["qs"])

            todo = [(dr, qt) for dr in range(2) for qt in range(2)]
            ranges = ((0, P), (0, S), (0, S), (P, S))
            wf, ptf = [None, None], [None, None]
            logw, multiplied, turned = {}, {}, {}

            def weigh(n):
                dr, qt = todo[n]
                k0, k1 = ranges[n]
                nk = k1 - k0
                cbb = BA[dr * 2:dr * 2 + 2]
                if qt == 0:
                    def cb(e):
                        for h in range(4):
                            ins = e.matmul(
                                psum[:, cbb[h // 2], (h % 2) * S:(h % 2) * S + S],
                                lhsT=ident[0:8, dr * 4 + h:dr * 4 + h + 1].to_broadcast([8, P]),
                                rhs=CT, start=True, stop=True)
                        return ins
                    cbo[dr] = q.pe(cb, ct_op, acc_free[cbb[0]], acc_free[cbb[1]])
                mask = C2("mask_b" if dr else "mask_f")
                W = W2[:, n % 2, 0:4 * nk]
                w3 = W.rearrange("p (h k) -> p h k", h=4)
                nm, en = sm(4), sm(4)
                for hp in range(2):
                    pv = psum[:, cbb[hp], :].rearrange("p (h k) -> p h k", h=2)
                    acc_free[cbb[hp]] = q.v(lambda e, hp=hp, pv=pv: e.tensor_tensor(
                        w3[:, hp * 2:hp * 2 + 2, :], pv[:, :, k0:k1],
                        bc3(mask[:, qt, k0:k1], 2, 1), ALU.add), cbo[dr], wf[n % 2])
                o = q.v(lambda e: e.tensor_reduce(nm, w3, AX.X, ALU.max, negate=True))
                o3 = q.v(lambda e: e.tensor_tensor(
                    en, nm, BB[:, qt, dr * 4:dr * 4 + 4], ALU.subtract))
                for h in range(4):
                    o2 = q.a(lambda e, h=h: e.activation(
                        w3[:, h, :], w3[:, h, :], ACT.Exp, bias=nm[:, h:h + 1]), o)
                o3 = q.a(lambda e: e.activation(en, en, ACT.Exp), o3)
                logw[n] = W, w3, en, o3

            def products(n):
                dr, qt = todo[n]
                k0, k1 = ranges[n]
                W, w3, en, o3 = logw[n]
                den, ad = sm(4), sm(4)
                qv = qks[:, qt, :].rearrange("p (h k) -> p h k", h=4)
                for h in range(4):
                    w_op = q.v(lambda e, h=h: e.scalar_tensor_tensor(
                        w3[:, h, :], w3[:, h, :], 1.0, qv[:, h, k0:k1], ALU.mult, ALU.mult,
                        accum_out=den[:, h:h + 1]), o3, gate["qs"])
                q.v(lambda e: e.scalar_tensor_tensor(ad, den, -1.0, den, ALU.mult, ALU.max))
                q.v(lambda e: e.tensor_tensor(en, en, ad, ALU.max))
                q.v(lambda e: e.reciprocal(en, en))
                multiplied[n] = w_op

            def turn(n):
                k0, k1 = ranges[n]
                kt = (k1 - k0) // P
                W, w_op = logw[n][0], multiplied[n]
                cs = []
                for hp in range(0, 4, 2):
                    t, c = transposed_block(
                        [W[:, (h * kt + i) * P:(h * kt + i + 1) * P]
                         for h in (hp, hp + 1) for i in range(kt)], PT2[:, hp // 2, :], w_op,
                        ptf[hp // 2])
                    cs.append(c)
                wf[n % 2] = t
                turned[n] = cs

            def gather(n):
                dr, qt = todo[n]
                k0, k1 = ranges[n]
                kt = (k1 - k0) // P
                en = logw[n][2]
                ob = BA[(2, 0, 1, 0)[n]]
                bank, fr = psum[:, ob, :], acc_free[ob]
                for hp in range(0, 4, 2):
                    PT = PT2[:, hp // 2, :]
                    for h in (hp, hp + 1):
                        o = mms(ob, bank[:, h * P:(h + 1) * P],
                                [(PT[:, ((h - hp) * kt + i) * P:((h - hp) * kt + i + 1) * P],
                                  mv[:, k0 // P + i, h * P:(h + 1) * P]) for i in range(kt)],
                                turned[n][hp // 2], mv_op, fr)
                    ptf[hp // 2] = o
                ov = bank.rearrange("p (h k) -> p h k", h=4)
                hm = HM[:, qt, :].rearrange("p (h k) -> p h k", h=4)
                if dr == 0:
                    r = q.v(lambda e: e.tensor_tensor(hm, ov, bc3(en, P), ALU.mult), o)
                else:
                    tm = TM[:, 0:512].rearrange("p (h k) -> p h k", h=4)
                    r = q.v(lambda e: e.tensor_tensor(tm, ov, bc3(en, P), ALU.mult), o)
                    q.v(lambda e: e.tensor_tensor(hm, hm, tm, ALU.add))
                acc_free[ob] = r

            cbo = {}

            def stage(*fs):
                return [lambda f=f, n=n: f(n) for f, n in fs]

            weigh(0)
            mids = {2064: {},
                    2576: {0: stage((turn, 0), (products, 1)), 1: stage((gather, 0))}}
            for dst, c0 in ((aq, 2064), (ak, 2576)):
                for tt, (k, bank, o) in enumerate(gemm_cols(w_in, c0, c0 + 512, 2, xr, mid=mids[c0])):
                    rd, aop = rope(bank.rearrange("p (h c) -> p h c", h=8),
                                   dst[:, tt, :].rearrange("p (h c) -> p h c", h=8), 8,
                                   C2("cos")[:, tt, :], C2("sin")[:, tt, :], TM[:, 0:512], o, m_c)
                    B4.give(k, rd)
                if c0 == 2064:
                    scores()
                    weigh(1)
                    products(0)
                else:
                    weigh(2)
            for tt, (k, bank, o) in enumerate(gemm_cols(
                    w_in, 3088, 3600, 2, xr,
                    mid={0: stage((turn, 1), (products, 2)), 1: stage((gather, 1))})):
                av_op = q.a(lambda e, tt=tt, bank=bank: e.activation(av[:, tt, :], bank, ACT.Copy), o)
                B4.give(k, av_op)
            qt_op = to_cols(lambda tt, k: aq[:, tt, k * P:(k + 1) * P],
                            lambda k0, nb, tt: qT[:, k0:k0 + nb, tt * P:(tt + 1) * P], 4, aop)
            turn(2)
            weigh(3)
            gather(2)
            z_op = q.p(lambda e: e.memset(kz, 0.0), gate["sc"], gate["qs"])
            kz_ops = []
            for tt in range(2):
                b, bank, fr = B4.take()

                def go(e, tt=tt, bank=bank):
                    for j in range(4):
                        ins = e.transpose(bank[:, j * P:(j + 1) * P], ak[:, tt, j * P:(j + 1) * P],
                                          ident)
                    return ins
                t = q.pe(go, aop, fr)
                pv = bank.rearrange("p (k s) -> p k s", k=4)
                kz_ops.append(q.a(lambda e, tt=tt, pv=pv: e.activation(
                    kz[0:64, :, 0, tt * P:(tt + 1) * P], pv[0:64], ACT.Copy), t, z_op))
                kz_ops.append(q.v(lambda e, tt=tt, pv=pv: e.tensor_copy(
                    kz[64:128, :, 1, tt * P:(tt + 1) * P], pv[64:128]), t, z_op))
                B4.give(b, *kz_ops[-2:])

            products(3)
            turn(3)
            gather(3)
            gi, hg, mg = bcast(d["head_norm_g"][l], 512)

            hn = sm(8)
            scaled = {}

            def head_norm(qt):
                hm = HM[:, qt, :].rearrange("p (h k) -> p h k", h=4)
                tm = TM[:, 0:512].rearrange("p (h k) -> p h k", h=4)
                q.v(lambda e: e.tensor_tensor(tm, hm, hm, ALU.mult))
                q.v(lambda e: e.tensor_reduce(hn[:, qt * 4:qt * 4 + 4], tm, AX.X, ALU.add))
                o = q.v(lambda e: e.tensor_tensor(HM[:, qt, :], HM[:, qt, :], hg, ALU.mult),
                        mg, mo_op)
                bdone(gi, o)
                return q.v(lambda e: e.tensor_tensor(
                    HM[:, qt, :], HM[:, qt, :], mo[:, qt, :], ALU.mult))

            def head_scale():
                o = head_norm(1)
                o = q.a(lambda e: e.activation(hn, hn, ACT.Sqrt, scale=1.0 / P, bias=EPS[:, 1:2]), o)
                q.v(lambda e: e.reciprocal(hn, hn), o)
                for qt in range(2):
                    hm = HM[:, qt, :].rearrange("p (h k) -> p h k", h=4)
                    scaled[0] = q.v(lambda e, hm=hm, qt=qt: e.tensor_tensor(
                        hm, hm, bc3(hn[:, qt * 4:qt * 4 + 4], P), ALU.mult))

            y_ops = {}

            def heads(qt, L, last):
                q.v(lambda e: e.reciprocal(L, L), last)
                ob = (BA[0], BA[2])[qt]
                y_ops[qt] = acc_free[ob] = q.v(lambda e: e.tensor_tensor(
                    Y[:, qt, 512:1024].rearrange("p (h c) -> p h c", h=8),
                    psum[:, ob, :].rearrange("p (h c) -> p h c", h=8), bc3(L, 64), ALU.mult), last)

            attention(4, qT, lambda b: kz[:, b, :, :], lambda i, h: av[:, i, h * 64:h * 64 + 64],
                            C2("mask_a"), False, W4, PT2, [[BA[0]], [BA[2]]], [kz_ops, av_op, qt_op], heads,
                      {4: lambda: head_norm(0), 7: head_scale})
            yt = split_both(Y, {t: [y_ops[t], scaled[0]] for t in range(2)})
            xo = project_out(d["w_out"][l], yt, 1.0)

            xr, xop = norm("rms", d["norm2_g"][l], None, xo)
            if l == 1:
                load_pool(xop)
            last = network(2, [(c * 512, 512) for c in range(8)], d["w_up"][l], 0, d["w_down"][l],
                           BA, xr)
            return residual(1.0, last)

        pool_in = {}

        def load_pool(ready):
            for name, a, n, src in (("sc", 8704, D, d["pool_scale_2"][0].partition_broadcast(P)),
                                    ("pm", 10752, 2048, d["poolm"])):
                pool_in[name] = AR[:, a:a + n], q.dma("gpsimd", s_p, AR[:, a:a + n], src, ready)
            pw = AR[:, 6656:8704].rearrange("p (g n) -> p g n", g=8)
            pool_in["pw"] = pw, q.dma("gpsimd", s_c, pw, d["pool_w_2"][0].rearrange(
                "g (c p) n -> p (g c) n", p=P), ready)

        def pool_layer(source):
            ready = list(norm("rms", d["final_g"], None, source, False)[0].values())
            sc, ms = pool_in["sc"]
            pm, mk = pool_in["pm"]
            pm = pm.rearrange("p (t g s) -> p t g s", t=2, g=4)
            PX = AR[:, 2048:4096].rearrange("p (k s) -> p k s", k=8)
            pw, mk2 = pool_in["pw"]
            for kp in range(4):
                b, bank, fr = B4.take()

                def go(e, kp=kp, bank=bank):
                    for h in range(2):
                        k = kp * 2 + h
                        for jt in range(2):
                            ins = e.matmul(bank[:, h * S:(h + 1) * S],
                                           lhsT=X[:, jt, k * P:(k + 1) * P], rhs=pm[:, jt, k // 2, :],
                                           start=jt == 0, stop=jt == 1)
                    return ins
                o = q.pe(go, ready, mk, fr)
                c = q.v(lambda e, kp=kp, bank=bank: e.tensor_copy(
                    PX[:, kp * 2:kp * 2 + 2, :], bank.rearrange("p (k s) -> p k s", k=2)), o)
                B4.give(b, c)
            outs = {}
            for tt in range(2):
                for nh in range(2):
                    b, bank, fr = B4.take()

                    def go(e, tt=tt, nh=nh, bank=bank):
                        for gg in range(2):
                            g = nh * 2 + gg
                            for c in range(2):
                                ins = e.matmul(bank[:, gg * 256:gg * 256 + 256],
                                               lhsT=PX[:, g * 2 + c, tt * P:(tt + 1) * P],
                                               rhs=pw[:, g * 2 + c, :], start=c == 0, stop=c == 1)
                        return ins
                    outs[(tt, nh)] = b, bank, q.pe(go, c, mk2, fr)

            def mixed(tt, nh, sums):
                b, bank, o = outs[(tt, nh)]
                t = AR[:, 4096:4608]
                xs = X[:, tt, nh * 512:nh * 512 + 512]
                r = q.v(lambda e: e.tensor_tensor(t, bank, sc[:, nh * 512:nh * 512 + 512],
                                                  ALU.mult), o, ms)
                B4.give(b, r)
                return q.v(lambda e: e.scalar_tensor_tensor(xs, xs, ALPHA, t, ALU.mult, ALU.add,
                                                            accum_out=sums))

            xc, _ = norm("ln", d["ln_g_2"][0, 0], d["ln_b_2"][0, 0], mixed)
            chunks = [(c * 512, min(512, FF2 - c * 512)) for c in (0, 1, 5, 2, 3, 4)]
            last = network(2, chunks, d["ffn_w_gu_2"][0], FF2, d["ffn_w_down_2"][0], BA, xc)
            return norm("ln", d["ln_g_2"][0, 1], d["ln_b_2"][0, 1], residual(ALPHA, last))[0]

        cleared = []

        def nsa(xc):
            w_in = d["nsa_w_in_2"][0]
            A = lambda a, n: AR[:, a:a + n]
            two = lambda r: r.rearrange("p (t n) -> p t n", t=2)
            Q = two(A(0, 2048))
            KZ = [A(0, 2048).rearrange("p (g h s) -> p g h s", g=4, h=2),
                  A(2048, 2048).rearrange("p (g h s) -> p g h s", g=4, h=2)]
            KR = [two(A(8192, 1024)), two(A(9216, 1024))]
            KCD = [two(A(4096, 1024)), two(A(10240, 1024))]
            qT = A(5120, 2048).rearrange("p (b s) -> p b s", b=8)
            V = [two(A(7168, 512)), two(A(7680, 512))]
            Y = two(A(8192, 2048))
            WC = two(A(4096, 1024))
            PTC = two(A(13312, 1024))
            W4 = A(10240, 2048).rearrange("p (t n) -> p t n", t=4)
            PT2 = two(A(12288, 1024))
            TM = A(14336, 1024)
            CBH = XTH.rearrange("p k s -> p (k s)").rearrange("p (k r c) -> p k r c", k=2, r=16)
            CBL = XTL.rearrange("p k s -> p (k s)").rearrange("p (k r c) -> p k r c", k=2, r=16)
            HID = A(15360, 128)
            KZC = A(15488, 256).rearrange("p (g h s) -> p g h s", g=4, h=2)
            VBD = A(15744, 256).rearrange("p (g c) -> p g c", g=4)
            GT = two(A(16000, 96))
            KC = A(4864, 64)
            KC2 = A(4608, 256)
            dup = lambda r: r.rearrange("p (g h c) -> p g h c", g=4, h=2)

            for nh in range(2):
                for tt, (k, bank, o) in enumerate(gemm_cols(
                        w_in, nh * 512, nh * 512 + 512, 2, xc, major=nh == 0)):
                    rd, q_op = rope(bank.rearrange("p (h c) -> p h c", h=8),
                                    Q[:, tt, nh * 512:nh * 512 + 512].rearrange("p (h c) -> p h c", h=8),
                                    8, C2("cos")[:, tt, :], C2("sin")[:, tt, :], TM[:, 0:512], o)
                    B4.give(k, rd)
            for tt, (k, bank, o) in enumerate(gemm_cols(w_in, 1024, 1536, 2, xc)):
                for kind in range(2):
                    for h in range(2):
                        c_op = q.a(lambda e, kind=kind, h=h, tt=tt, bank=bank: e.activation(
                            dup(KCD[kind][:, tt, :])[:, :, h, :],
                            bank[:, kind * 256:kind * 256 + 256].rearrange("p (g c) -> p g c", g=4),
                            ACT.Copy), o)
                B4.give(k, c_op)
            qt_op = to_cols(lambda tt, k: Q[:, tt, k * P:(k + 1) * P],
                            lambda k0, nb, tt: qT[:, k0:k0 + nb, tt * P:(tt + 1) * P], 8,
                            [q_op, c_op])
            for kind, a in enumerate((1536, 2048)):
                for tt, (k, bank, o) in enumerate(gemm_cols(w_in, a, a + 512, 2, xc)):
                    kd = dup(KR[kind][:, tt, :])
                    rd, o2 = rope(bank[:, 0:256].rearrange("p (h c) -> p h c", h=4),
                                  kd[:, :, 0, :], 4,
                                  C2("cos")[:, tt, :], C2("sin")[:, tt, :], TM[:, 0:512], o)
                    v_op = q.v(lambda e, kind=kind, tt=tt, bank=bank: e.tensor_copy(
                        V[kind][:, tt, :], bank[:, 256:512]))
                    B4.give(k, v_op)
                    k_op = q.v(lambda e, kd=kd: e.tensor_copy(kd[:, :, 1, :], kd[:, :, 0, :]))
            gates_op, gates = gemm_few(w_in, 2560, 2608, xc)
            def both(hv, lv, src, *w):
                h = q.a(lambda e: e.activation(hv, src, ACT.Copy), *w)
                return q.v(lambda e: e.tensor_tensor(lv, src, hv.bitcast(F32), ALU.subtract), h)

            for kind in range(2):
                pe3 = bc3(PR(("pek", "pev")[kind]), 2)
                both(CBH[:, kind, :, 60:62], CBL[:, kind, :, 60:62], pe3, m_p, gates_op)
                for gp in range(2):
                    b, bank, fr = B4.take()

                    def go(e, kind=kind, gp=gp, bank=bank):
                        for g in range(2):
                            for tt in range(2):
                                n = g * 2 + tt
                                ins = e.transpose(
                                    bank[:, n * P:(n + 1) * P],
                                    KCD[kind][:, tt, (gp * 2 + g) * P:(gp * 2 + g + 1) * P], ident)
                        return ins
                    t = q.pe(go, c_op, fr)
                    pv = bank.rearrange("p (g n r c) -> p g n r c", g=2, n=16, r=8)
                    todo = []
                    for c in range(2):
                        ps = slice(64 * c, 64 * c + 64)
                        for a in range(2):
                            cv = [z[ps, kind, 8 * a:8 * a + 8, gp * 30:gp * 30 + 30].rearrange(
                                "p r (g n) -> p r g n", g=2) for z in (CBH, CBL)]
                            src = pv[ps, :, a:a + 15, :, c].rearrange("p g n r -> p r g n")
                            todo.append((cv, src))
                    for cv, src in todo:
                        h = q.a(lambda e, cv=cv, src=src: e.activation(cv[0], src, ACT.Copy), t)
                    for cv, src in todo:
                        cb_op = q.v(lambda e, cv=cv, src=src: e.tensor_tensor(
                            cv[1], src, cv[0].bitcast(F32), ALU.subtract), h)
                    B4.give(b, cb_op)
            kz_ops = []
            for kind in range(2):
                z_op = q.p(lambda e, kind=kind: e.memset(KZ[kind], 0.0), qt_op)
                for tt in range(2):
                    b, bank, fr = B4.take()

                    def go(e, kind=kind, tt=tt, bank=bank):
                        for g in range(4):
                            ins = e.transpose(bank[:, g * P:(g + 1) * P],
                                              KR[kind][:, tt, g * P:(g + 1) * P], ident)
                        return ins
                    t = q.pe(go, k_op, fr)
                    pv = bank.rearrange("p (k s) -> p k s", k=4)
                    kz_ops.append(q.a(lambda e, kind=kind, tt=tt, pv=pv: e.activation(
                        KZ[kind][0:64, :, 0, tt * P:(tt + 1) * P], pv[0:64], ACT.Copy), t, z_op))
                    kz_ops.append(q.v(lambda e, kind=kind, tt=tt, pv=pv: e.tensor_copy(
                        KZ[kind][64:128, :, 1, tt * P:(tt + 1) * P], pv[64:128]), t, z_op))
                    B4.give(b, *kz_ops[-2:])
            for tt, (k, bank, o) in enumerate(gates()):
                gt_op = q.a(lambda e, tt=tt, bank=bank: e.activation(
                    GT[:, tt, :], bank, ACT.Sigmoid), o)
                B4.give(k, gt_op)
            q.v(lambda e: e.memset(HID, 0.0))
            q.v(lambda e: e.memset(KC2, 0.0))
            q.v(lambda e: e.memset(KZC, 0.0))
            q.v(lambda e: e.memset(VBD, 0.0))
            st = {}

            def compress(kind, half):
                bk = BA[2 + kind]
                bank = psum[:, bk, :]
                if half == 0:
                    w1n = ("nsa_w1_k_2", "nsa_w1_v_2")[kind]
                    st["w1"] = unit(d[w1n][0].rearrange("(r p) n -> p r n", p=P), 16, P)
                w1h, w1l, mk, own1 = st["w1"]

                def go(e):
                    for r in range(half * 8, half * 8 + 8):
                        for n, (a, b_) in enumerate(((w1h, CBH), (w1h, CBL), (w1l, CBH))):
                            ins = e.matmul(bank[:, 0:62], lhsT=a[:, r, :],
                                           rhs=b_[:, kind, r, 0:62], start=r + n == 0,
                                           stop=r + n == 17)
                    return ins
                o = q.pe(go, cb_op, mk, acc_free[bk], own=own1 if half else None)
                if half:
                    pc = sm(1)
                    q.v(lambda e: e.tensor_copy(pc, bank[:, 60:61]), o)
                    hv = HID.rearrange("p (g n) -> p g n", g=4)[:, :, 0:15]
                    o = q.v(lambda e: e.tensor_scalar(
                        hv, bank[:, 0:60].rearrange("p (g n) -> p g n", g=4), pc, None, ALU.add))
                    acc_free[bk] = o
                    st["hid"] = q.a(lambda e: e.activation(hv, hv, ACT.Silu), o)

            def second(kind):
                w2n = ("nsa_w2_k_2", "nsa_w2_v_2")[kind]
                w2h, w2l, mk2, own2 = unit(d[w2n][0].unsqueeze(1), 1, 64)
                w2 = [w2h.bitcast(F32)[:, 0, :], w2l.bitcast(F32)[:, 0, :]]
                b, bank, fr = B4.take()
                o = q.pe(lambda e: [e.matmul(
                    bank[:, 0:64], lhsT=HID, rhs=w2[n], start=n == 0, stop=n == 1)
                    for n in range(2)][-1], st["hid"], fr, mk2, own=own2)
                if kind == 0:
                    rd, o = rope(bank[:, 0:64].rearrange("p (h c) -> p h c", h=1),
                                 KC.rearrange("p (h c) -> p h c", h=1), 1,
                                 C("cos_c"), C("sin_c"), TM[:, 0:512], o)
                    B4.give(b, rd)
                    q.v(lambda e: e.tensor_copy(KC2[:, 0:64], KC))
                    st["kc2"] = q.v(lambda e: e.tensor_copy(KC2[:, 128 + 64:256], KC))
                else:
                    for g in range(4):
                        st["vc"] = q.v(lambda e, g=g: e.tensor_copy(
                            VBD[32 * g:32 * g + 32, g, :], bank[32 * g:32 * g + 32, 0:64]), o)
                    B4.give(b, st["vc"])

            def turn_keys():
                b, bank, fr = B4.take()

                def tr(e):
                    for h in range(2):
                        ins = e.transpose(bank[:, h * P:(h + 1) * P], KC2[:, h * P:(h + 1) * P],
                                          ident)
                    return ins
                t = q.pe(tr, st["kc2"], fr)
                st["kc"] = q.v(lambda e: e.tensor_copy(
                    KZC, bank[:, 0:256].rearrange("p (h g n) -> p g h n", h=2, g=4)), t)
                B4.give(b, st["kc"])

            def weigh_c(qt):
                b, bank, fr = B4.take()

                def sc(e):
                    for blk in range(8):
                        ins = e.matmul(bank[:, blk * 64:blk * 64 + 64],
                                       lhsT=qT[:, blk, qt * P:(qt + 1) * P],
                                       rhs=KZC[:, blk // 2, :, :], start=True, stop=True)
                    return ins
                o = q.pe(sc, st["kc"], qt_op, fr)
                W = WC[:, qt, :]
                rd, o, l = softmax_block(bank, 32, 16, C2("mask_c")[:, qt, :], None, 0.125, W, None, o)
                B4.give(b, rd)
                st["l"] = l

            def turn_c(qt):
                l, gl, W = st["l"], sm(16), WC[:, qt, :]
                q.v(lambda e: e.reciprocal(l, l))
                q.v(lambda e: e.scalar_tensor_tensor(
                    gl, l, C2("any_c")[:, qt, :],
                    GT[:, qt, :].rearrange("p (h b) -> p h b", b=3)[:, :, 0],
                    ALU.mult, ALU.mult), gt_op)
                st["gl"] = gl
                wp = TM[:, 512:1024]
                o = q.v(lambda e: e.tensor_copy(
                    wp.rearrange("p (x g n) -> p g x n", x=4, g=4),
                    W.rearrange("p (g x n) -> p g x n", g=4, x=4)), st.get("wp"))
                st["wp"], st["ptc"] = transposed_block(
                    [wp[:, x * P:(x + 1) * P] for x in range(4)], PTC[:, qt, :], o, None)

            def gather_c(qt):
                for xp in range(2):
                    b, bank, fr = B4.take()

                    def pv_(e, xp=xp, bank=bank):
                        for x in range(2):
                            ins = e.matmul(bank[:, x * 256:x * 256 + 256],
                                           lhsT=PTC[:, qt, (xp * 2 + x) * P:(xp * 2 + x + 1) * P],
                                           rhs=VBD, start=True, stop=True)
                        return ins
                    o = q.pe(pv_, st["ptc"], st["vc"], fr)
                    for x in range(2):
                        yv = Y[:, qt, :].rearrange("p (g x c) -> p g x c", g=4, x=4)[:, :, xp * 2 + x, :]
                        glv = st["gl"].rearrange("p (g x) -> p g x", g=4)[:, :, xp * 2 + x]
                        r = q.v(lambda e, yv=yv, glv=glv, bank=bank, x=x: e.tensor_tensor(
                            yv, bank[:, x * 256:x * 256 + 256].rearrange("p (g c) -> p g c", g=4),
                            bc3(glv, 64), ALU.mult), o)
                    B4.give(b, r)

            def both_of(*fs):
                def go():
                    for f, *a in fs:
                        f(*a)
                return go
            steps = {0: both_of((compress, 0, 0)), 1: both_of((compress, 0, 1)),
                     2: both_of((second, 0)), 3: both_of((turn_keys,), (compress, 1, 0)),
                     4: both_of((compress, 1, 1)), 5: both_of((second, 1)),
                     6: both_of((weigh_c, 0)), 7: both_of((turn_c, 0)),
                     8: both_of((gather_c, 0)), 9: both_of((weigh_c, 1)),
                     10: both_of((turn_c, 1)), 11: both_of((gather_c, 1))}
            y_ops = {}
            for kind in range(2):
                def heads(qt, L, last, kind=kind):
                    q.v(lambda e: e.reciprocal(L, L), last)
                    q.v(lambda e: e.tensor_tensor(
                        L, L, GT[:, qt, :].rearrange("p (h b) -> p h b", b=3)[:, :, 1 + kind],
                        ALU.mult))
                    for hb in range(2):
                        ob = BA[qt * 2 + hb]
                        tm = TM[:, 0:512].rearrange("p (h c) -> p h c", h=8)
                        acc_free[ob] = q.v(lambda e, ob=ob, hb=hb, tm=tm: e.tensor_tensor(
                            tm, psum[:, ob, :].rearrange("p (h c) -> p h c", h=8),
                            bc3(L[:, hb * 8:hb * 8 + 8], 64), ALU.mult), last)
                        y_ops[qt] = q.v(lambda e, hb=hb: e.tensor_tensor(
                            Y[:, qt, hb * 512:hb * 512 + 512], Y[:, qt, hb * 512:hb * 512 + 512],
                            TM[:, 0:512], ALU.add))

                attention(8, qT, lambda b, kind=kind: KZ[kind][:, b // 2, :, :],
                          lambda i, h, kind=kind: V[kind][:, i, (h // 4) * 64:(h // 4) * 64 + 64],
                          C2("mask_f"), True, W4, PT2, [BA[0:2], BA[2:4]],
                          [kz_ops, v_op, qt_op] if kind == 0 else list(y_ops.values()), heads,
                          steps if kind == 0 else None)
            yt = split_both(Y, y_ops)
            xo = project_out(d["nsa_w_out_2"][0], yt, ALPHA)
            out, xop = norm("ln", d["ln_g_2"][1, 0], d["ln_b_2"][1, 0], xo)
            cleared.append(q.p(lambda e: e.memset(YA, 0.0), xop))
            return out

        A_ = lambda a, n: AR[:, a:a + n]
        YA = A_(0, 2048).rearrange("p (t n) -> p t n", t=2)
        SEL = A_(2816, 16).rearrange("p (t n) -> p t n", t=2)
        CMB = A_(2832, 16).rearrange("p (t n) -> p t n", t=2)
        POS = A_(2848, 16).rearrange("p (t n) -> p t n", t=2)
        LG = A_(2864, 16).rearrange("p (t n) -> p t n", t=2)
        EQ = A_(2880, 128)
        EQ2 = A_(3008, 128)
        RK = A_(3136, 16).rearrange("p (t n) -> p t n", t=2)
        PL = A_(6144, 2 * 2 * S).rearrange("p (b t n) -> p b t n", b=2, t=2)
        PW = A_(7168, 2 * S).rearrange("p (t n) -> p t n", t=2)
        PB = A_(7680, 2 * 2 * S).rearrange("p (b t n) -> p b t n", b=2, t=2)
        YE = A_(8704, 2048).rearrange("p (t n) -> p t n", t=2)

        LOW = A_(3152, 64).rearrange("p (a b) -> p a b", a=8)

        def route(xc):
            idx = C("iota")[:, 0:8]
            q.v(lambda e: e.tensor_tensor(LOW, bc3(idx, 8, 1), bc3(idx, 8, 2), ALU.is_lt))
            for tt, (k, bank, o) in enumerate(gemm_few(d["moe_router_2"][0], 0, 8, xc)[1]()):
                r = q.v(lambda e, tt=tt, bank=bank: e.tensor_copy(LG[:, tt, :], bank), o)
                B4.give(k, r)
            sh = [P, 2, 8, 8]
            a = LG.unsqueeze(2).to_broadcast(sh)
            b = LG.unsqueeze(3).to_broadcast(sh)
            m = EQ.rearrange("p (t a b) -> p t a b", t=2, a=8)
            m2 = EQ2.rearrange("p (t a b) -> p t a b", t=2, a=8)
            q.v(lambda e: e.tensor_tensor(m, a, b, ALU.is_gt))
            q.v(lambda e: e.tensor_tensor(m2, a, b, ALU.is_equal))
            q.v(lambda e: e.tensor_tensor(m2, m2, LOW.unsqueeze(1).to_broadcast(sh), ALU.mult))
            q.v(lambda e: e.tensor_tensor(m, m, m2, ALU.add))
            q.v(lambda e: e.tensor_reduce(RK, m, AX.X, ALU.add))
            sel = q.v(lambda e: e.tensor_scalar(SEL, RK, 1.5, None, ALU.is_lt))
            mx, s = sm(2), sm(2)
            q.v(lambda e: e.tensor_reduce(mx, LG, AX.X, ALU.max))
            o = q.v(lambda e: e.tensor_tensor(CMB, LG, bc3(mx, 8), ALU.subtract))
            o = q.a(lambda e: e.activation(CMB, CMB, ACT.Exp), o)
            q.v(lambda e: e.tensor_tensor(CMB, CMB, SEL, ALU.mult), o)
            q.v(lambda e: e.tensor_reduce(s, CMB, AX.X, ALU.add))
            q.v(lambda e: e.reciprocal(s, s))
            q.v(lambda e: e.tensor_tensor(CMB, CMB, bc3(s, 8), ALU.mult))
            k, bank, fr = B4.take()

            def cum(e, bank=bank):
                e.matmul(bank[:, 0:8], lhsT=C("strict"), rhs=SEL[:, 0, :], start=True, stop=True)
                e.matmul(bank[:, 8:16], lhsT=C("ones"), rhs=SEL[:, 0, :], start=True, stop=False)
                e.matmul(bank[:, 8:16], lhsT=C("strict"), rhs=SEL[:, 1, :], start=False, stop=True)
                e.matmul(bank[:, 16:24], lhsT=C("ones"), rhs=SEL[:, 0, :], start=True, stop=False)
                return e.matmul(bank[:, 16:24], lhsT=C("ones"), rhs=SEL[:, 1, :], start=False,
                                stop=True)
            o = q.pe(cum, sel, fr)
            q.v(lambda e, bank=bank: e.tensor_copy(
                POS, bank[:, 0:16].rearrange("p (t n) -> p t n", t=2)), o)
            f_op = q.v(lambda e, bank=bank: e.tensor_scalar(
                flag[0:1, :], bank[0:1, 16:24], P + 0.5, None, ALU.is_gt))
            B4.give(k, f_op)
            return f_op

        pl_done, pw_done = {}, {}

        def lists(x):
            xb = x % 2
            for tt in range(2):
                pl_done[x] = q.v(lambda e, tt=tt: e.tensor_scalar(
                    PL[:, xb, tt, :], C("iota"), POS[:, tt, x:x + 1], SEL[:, tt, x:x + 1],
                    ALU.is_equal, ALU.mult))
            for tt in range(2):
                pw_done[x] = q.v(lambda e, tt=tt: e.tensor_scalar(
                    PW[:, tt, :], PL[:, xb, tt, :], CMB[:, tt, x:x + 1], None, ALU.mult))

        def turn_lists(x, *ready):
            b, bank, fr = B4.take()

            def tr(e):
                for st in range(2):
                    for tt in range(2):
                        ins = e.transpose(bank[:, (st * 2 + tt) * P:(st * 2 + tt + 1) * P],
                                          PW[:, tt, st * P:(st + 1) * P], ident)
                return ins
            t = q.pe(tr, pw_done[x], fr)
            op = q.a(lambda e: e.activation(
                PB[:, x % 2, :, :], bank.rearrange("p (t n) -> p t n", t=2), ACT.Copy), t, *ready)
            B4.give(b, op)

        def fetch(x, st, half, *ready):
            hs = slice(half * P, half * P + P)
            for k0 in range(0, KB, 4):
                b, bank, fr = B4.take()

                def go(e, k0=k0, bank=bank):
                    for j in range(4):
                        for tt in range(2):
                            ins = e.matmul(bank[:, j * P:(j + 1) * P],
                                           lhsT=X[:, tt, (k0 + j) * P:(k0 + j + 1) * P],
                                           rhs=PL[:, x % 2, tt, st * P:(st + 1) * P],
                                           start=tt == 0, stop=tt == 1)
                    return ins
                t = q.pe(go, fr, *ready)
                pv = bank.rearrange("p (k s) -> p k s", k=4)
                xh, xl = XTH[:, k0:k0 + 4, hs], XTL[:, k0:k0 + 4, hs]
                h = q.a(lambda e, xh=xh, pv=pv: e.activation(xh, pv, ACT.Copy), t)
                op = q.v(lambda e, xh=xh, xl=xl, pv=pv: e.tensor_tensor(
                    xl, pv, xh.bitcast(F32), ALU.subtract), h)
                B4.give(b, op)
            return op

        def scatter(x, st, acc, ready):
            for nh in range(2):
                ns = slice(nh * 512, nh * 512 + 512)
                ye = q.a(lambda e, nh=nh, ns=ns: e.activation(
                    YE[:, st, ns], psum[:, acc[nh], :], ACT.Copy), ready)
                acc_free[acc[nh]] = ye
                for tt in range(2):
                    b, bank, fr = B4.take()
                    o = mms(b, bank, [(PB[:, x % 2, st, tt * P:(tt + 1) * P], YE[:, st, ns])],
                            ye, fr)
                    y = YA[:, tt, ns]
                    r = q.v(lambda e, y=y, bank=bank: e.tensor_tensor(y, y, bank, ALU.add), o)
                    B4.give(b, r)
            return o

        def pair(x):
            return BA[(x % 2) * 2:(x % 2) * 2 + 2]

        def expert(x, nt, ready):
            half = x % 2
            done = ready
            if nt == 2:
                done = [ready, fetch(x, 1, 1 - half, ready)]
            acc = pair(x) + (pair(x + 1) if nt == 2 else [])
            free = [ready]
            before_last = Mark(s_use, unit_n[0])

            def before():
                if x > 0:
                    free.append(scatter(x - 1, 0, pair(x - 1), [ready, before_last]))
                if x + 1 < N_EXP:
                    lists(x + 1)

            def residue():
                for tt in range(2):
                    q.v(lambda e, tt=tt: e.scalar_tensor_tensor(
                        YA[:, tt, :], X[:, tt, :], ALPHA, YA[:, tt, :], ALU.mult, ALU.add))

            mid = {0: before}
            if x + 1 < N_EXP:
                mid[1] = lambda: turn_lists(x + 1, *free)
                mid[6 if nt == 2 else 2] = lambda: fetch(x + 1, 0, 1 - half, pl_done[x + 1])
            else:
                mid[2] = residue
            last = network(nt, [(c * 512, 512) for c in range(7)], d["moe_w_gu_2"][0, x], FE,
                           d["moe_w_down_2"][0, x], acc, done, half, mid)
            flush()
            if nt == 2:
                scatter(x, 1, pair(x + 1), last)

        def settle(name):
            ends = [q.end(name, "vector"), q.end(name, "scalar"), q.end(name, "tensor")]
            for b in range(8):
                B4.free[b] = ends
                acc_free[b] = ends
            return ends

        q.v(lambda e: e.memset(EPS[:, 0:1], 1e-5))
        q.v(lambda e: e.memset(EPS[:, 1:2], 1e-6))
        op = hybrid(0, lambda t, nh, sums: m_x[t])
        op = hybrid(1, op)
        op = pool_layer(op)
        op = nsa(op)
        f_op = route(op)
        f_op.used = True
        lists(0)
        fetch(0, 0, 0, pl_done[0])
        turn_lists(0)
        ends = settle("first") + cleared
        for x in range(N_EXP):
            state = unit_n[0], B4.n
            for side in range(2):
                unit_n[0], B4.n = state
                B4.free = {b: ends for b in range(8)}
                for b in range(8):
                    acc_free[b] = ends
                q.enter((f"expert{x}", side))
                expert(x, side + 1, ends)
            B4.n = 0
            ends = settle(f"expert{x}")
        q.enter("last")
        x7 = {}

        def scattered(t, nh, sums):
            x, acc, done = N_EXP - 1, pair(N_EXP - 1), [ends, Mark(s_use, unit_n[0])]
            if not x7:
                for h in range(2):
                    x7[h] = q.a(lambda e, h=h: e.activation(
                        YE[:, 0, h * 512:h * 512 + 512], psum[:, acc[h], :], ACT.Copy), done)
            ns = slice(nh * 512, nh * 512 + 512)
            b, bank, fr = B4.take()
            o = mms(b, bank, [(PB[:, x % 2, 0, t * P:(t + 1) * P], YE[:, 0, ns])], x7[nh], fr)
            return q.v(lambda e: e.scalar_tensor_tensor(
                X[:, t, ns], YA[:, t, ns], 1.0, bank, ALU.mult, ALU.add, accum_out=sums), o)

        outs, op = norm("ln", d["ln_g_2"][1, 1], d["ln_b_2"][1, 1], scattered, False)
        q.part = "first"
        for u, (src, k, n) in enumerate(units):
            i = u % NSLOT
            q.dma("sync", s_ring[i], ring[:, i * UNIT:i * UNIT + k * n].rearrange(
                "p (k n) -> p k n", k=k), src, Mark(s_lo, u - NSLOT + 1))
        for t in range(2):
            q.dma("sync", s_out, out[0, t * P:(t + 1) * P, :], X[:, t, :], outs[t])

        q.n_units = len(units)
        q.number()
        block = ctx.enter_context(nc.Block())

        def run(eng, e):
            seen = {}
            branches = eng in ("tensor", "vector", "scalar")
            q.emit(e, eng, "first", seen)
            if branches:
                e.wait_ge(f_op.sem, f_op.value)
                many = [e.value_load(flag[0:1, x:x + 1]) for x in range(N_EXP)]
                for x in range(N_EXP):
                    sides = [dict(seen), dict(seen)]
                    with e.If(many[x] > 0):
                        q.emit(e, eng, (f"expert{x}", 1), sides[1])
                    with e.Else():
                        q.emit(e, eng, (f"expert{x}", 0), sides[0])
                    seen = {k: min(sides[0].get(k, 0), sides[1].get(k, 0)) for k in sides[0]}
            q.emit(e, eng, "last", seen)
            if eng == "sync":
                e.wait_ge(s_out, 32)

        @block.sync
        def _(e):
            run("sync", e)

        @block.tensor
        def _(e):
            run("tensor", e)

        @block.vector
        def _(e):
            run("vector", e)

        @block.scalar
        def _(e):
            run("scalar", e)

        @block.gpsimd
        def _(e):
            run("gpsimd", e)


def arrange(inputs):
    at, cons, pool = constants()
    a = {k: np.ascontiguousarray(np.asarray(v)) for k, v in inputs.items()}

    arrays = {k: a[k] for k in (
        "x", "norm1_g", "norm2_g", "w_in", "head_norm_g", "w_out", "w_up", "w_down", "final_g", "ln_g_2", "ln_b_2",
        "pool_w_2", "pool_scale_2", "nsa_w_in_2", "nsa_w1_k_2", "nsa_w2_k_2", "nsa_w1_v_2",
        "nsa_w2_v_2", "nsa_w_out_2", "ffn_w_gu_2", "ffn_w_down_2", "moe_router_2", "moe_w_gu_2",
        "moe_w_down_2")}
    arrays["cw"] = np.ascontiguousarray(
        a["conv_w"].reshape(2, 5, KB, P).transpose(3, 0, 2, 1).reshape(P, 80))
    for new, old in (("pek", "nsa_pe_k_2"), ("pev", "nsa_pe_v_2")):
        arrays[new] = np.ascontiguousarray(a[old].reshape(16, P).T)
    arrays["gib"] = a["gate_i_b"].reshape(16)
    arrays["gfb"] = a["gate_f_b"].reshape(16)
    arrays["cons"] = cons
    arrays["poolm"] = pool
    return arrays, (at, cons.shape[1], pool.shape[1])


def kernel(**inputs):
    import concourse.bacc as bacc
    from concourse.bass_utils import run_bass_kernel_spmd

    nc = bacc.Bacc("TRN2", target_bir_lowering=False, num_devices=1)
    arrays, tables = arrange(inputs)
    d = {n: nc.dram_tensor(f"in_{n}", v.shape, mybir.dt.from_np(v.dtype), kind="ExternalInput").ap()
         for n, v in arrays.items()}
    out = nc.dram_tensor("out_0", (1, S, D), F32, kind="ExternalOutput").ap()
    build(nc, d, out, tables)
    r = run_bass_kernel_spmd(nc, [{f"in_{n}": v for n, v in arrays.items()}], core_ids=[0])
    return r.results[0]["out_0"]
```
